# Optimizing a Trainium2 kernel written in Bass

```python
import jax, jax.numpy as jnp
from jax import lax
import numpy as np

D_MODEL = 1024
BATCH = 1
SEQ = 256
DEPTH = 2

GRID_W = 64
CTX_LEN = 256
EPS = 1e-6
F_FLOOR = 1e-20
N_MOD = 6
HG_WIDTH = 512
HG_HEADS = 4
HG_DIM = HG_WIDTH // HG_HEADS
CHUNK = 16
SC_WIDTH = 512
SC_HALF = SC_WIDTH // 2
CONV_W = 3
IN_COLS = 5 * HG_WIDTH + 3 * SC_WIDTH
SPLITS = tuple(HG_WIDTH * i for i in range(1, 6)) + (5 * HG_WIDTH + SC_WIDTH, 5 * HG_WIDTH + 2 * SC_WIDTH)
PEER_HEADS = 8
PEER_QDIM = 256
PEER_HALF = PEER_QDIM // 2
N_KEYS = 128
N_EXPERTS = N_KEYS * N_KEYS
PEER_TOPK = 16
PEER_BLOCK = 128


def rms_norm(x, g):
    xf = x.astype(jnp.float32)
    y = xf * lax.rsqrt(jnp.mean(xf * xf, axis=-1, keepdims=True) + EPS)
    return (y * g.astype(jnp.float32)).astype(x.dtype)

def modulate(h, shift, scale):
    return h * (1 + scale) + shift

def to_heads(a):
    return a.reshape(a.shape[0], a.shape[1], HG_HEADS, HG_DIM).astype(jnp.float32)

def flip(a):
    return a[:, ::-1]

def forget_terms(z, lb):
    f = lb + (1.0 - lb) * jax.nn.sigmoid(z)
    logf = jnp.log(jnp.maximum(f, F_FLOOR))
    key = (1.0 - lb) * jax.nn.sigmoid(-z)
    return logf, key

def gla_chunk(q, k, v, logf, s0):
    bsz, t, h, _ = q.shape
    dv = v.shape[-1]
    n = t // CHUNK
    q, k, v, logf = (a.reshape(bsz, n, CHUNK, h, a.shape[-1]) for a in (q, k, v, logf))
    b = jnp.cumsum(logf, axis=2)
    mask = jnp.tril(jnp.ones((CHUNK, CHUNK), bool))[None, None, :, :, None, None]
    diff = b[:, :, :, None] - b[:, :, None, :]
    decay = jnp.where(mask, jnp.exp(jnp.where(mask, diff, 0.0)), 0.0)
    att = jnp.einsum('bnthk,bntshk,bnshk->bnhts', q, decay, k)
    o_intra = jnp.einsum('bnhts,bnshv->bnthv', att, v)
    b_last = b[:, :, -1]
    q_in = q * jnp.exp(b)
    k_out = k * jnp.exp(b_last[:, :, None] - b)

    def step(s, xs):
        qc, kc, vc, dc = xs
        o = jnp.einsum('bchk,bhkv->bchv', qc, s)
        s = dc[..., None] * s + jnp.einsum('bchk,bchv->bhkv', kc, vc)
        return s, o

    xs = tuple(jnp.moveaxis(a, 1, 0) for a in (q_in, k_out, v, jnp.exp(b_last)))
    s_final, o_inter = lax.scan(step, s0, xs)
    o = o_intra + jnp.moveaxis(o_inter, 0, 1)
    return o.reshape(bsz, t, h, dv), s_final

def gla_final_state(k, v, logf):
    b = jnp.cumsum(logf, axis=1)
    kd = k * jnp.exp(b[:, -1:] - b)
    return jnp.einsum('bthk,bthv->bhkv', kd, v)

def hgrn2_mix(q, iv, zf, zb, g, lbf, lbb, s0f, s0b):
    q, iv, zf, zb = (to_heads(a) for a in (q, iv, zf, zb))
    logf_f, k_f = forget_terms(zf, lbf)
    o_f, s_f = gla_chunk(q, k_f, iv, logf_f, s0f)
    logf_b, k_b = forget_terms(zb, lbb)
    o_b, s_b = gla_chunk(flip(q), flip(k_b), flip(iv), flip(logf_b), s0b)
    o = o_f + flip(o_b)
    o = o * lax.rsqrt(jnp.mean(o * o, axis=-1, keepdims=True) + EPS)
    o = o.reshape(g.shape).astype(g.dtype) * jax.nn.silu(g)
    return o, s_f, s_b

def hgrn2_final_states(iv, zf, zb, lbf, lbb):
    iv, zf, zb = (to_heads(a) for a in (iv, zf, zb))
    logf_f, k_f = forget_terms(zf, lbf)
    s_f = gla_final_state(k_f, iv, logf_f)
    logf_b, k_b = forget_terms(zb, lbb)
    s_b = gla_final_state(flip(k_b), flip(iv), flip(logf_b))
    return s_f, s_b

def conv3(u, w, axis):
    n = u.shape[axis]
    pad = [(0, 0)] * u.ndim
    pad[axis] = (1, 1)
    up = jnp.pad(u, pad)
    return (w[0] * lax.slice_in_dim(up, 0, n, axis=axis)
            + w[1] * lax.slice_in_dim(up, 1, n + 1, axis=axis)
            + w[2] * lax.slice_in_dim(up, 2, n + 2, axis=axis))

def grid_conv(u, w, rows):
    bsz, t, ch = u.shape
    grid = u.reshape(bsz, rows, GRID_W, ch)
    horiz = conv3(grid[..., :SC_HALF], w[:, :SC_HALF], axis=2)
    vert = conv3(grid[..., SC_HALF:], w[:, SC_HALF:], axis=1)
    return jnp.concatenate([horiz, vert], axis=-1).reshape(bsz, t, ch)

def seq_conv(u, w):
    return conv3(u, w, axis=1)

def token_mixer(h, w_in_l, w_out_l, conv_w_l, lbf, lbb, s0f, s0b, conv_fn):
    iv, zf, zb, q, g, cg, bg, hv = jnp.split(h @ w_in_l, SPLITS, axis=-1)
    o_rec, s_f, s_b = hgrn2_mix(q, iv, zf, zb, g, lbf, lbb, s0f, s0b)
    o_conv = bg * conv_fn(cg * hv, conv_w_l)
    y = jnp.concatenate([o_rec, o_conv], axis=-1) @ w_out_l
    return y, s_f, s_b

def peer_ffn(h, wq, subkeys, u, v):
    bsz, t, d = h.shape
    qr = (h @ wq).astype(jnp.float32).reshape(bsz, t, PEER_HEADS, 2, PEER_HALF)
    scores = jnp.einsum('bthpd,hpkd->bthpk', qr, subkeys.astype(jnp.float32))
    s1, i1 = lax.top_k(scores[..., 0, :], PEER_TOPK)
    s2, i2 = lax.top_k(scores[..., 1, :], PEER_TOPK)
    n_cand = PEER_TOPK * PEER_TOPK
    cand = (s1[..., :, None] + s2[..., None, :]).reshape(bsz, t, PEER_HEADS, n_cand)
    cidx = (i1[..., :, None] * N_KEYS + i2[..., None, :]).reshape(bsz, t, PEER_HEADS, n_cand)
    top, pos = lax.top_k(cand, PEER_TOPK)
    eidx = jnp.take_along_axis(cidx, pos, axis=-1)
    gate = jax.nn.softmax(top, axis=-1).astype(h.dtype)
    n_blk = bsz * t // PEER_BLOCK
    n_sel = PEER_HEADS * PEER_TOPK
    hb = h.reshape(n_blk, PEER_BLOCK, d)
    eb = eidx.reshape(n_blk, PEER_BLOCK, n_sel)
    gb = gate.reshape(n_blk, PEER_BLOCK, n_sel)

    def block(args):
        hk, ek, gk = args
        act = jax.nn.gelu(jnp.einsum('ted,td->te', u[ek], hk), approximate=False)
        return jnp.einsum('te,ted->td', gk * act, v[ek])

    return lax.map(block, (hb, eb, gb)).reshape(bsz, t, d)

def first_inputs(seed: int = 0) -> dict:
    key = jax.random.key(seed)
    ks = jax.random.split(key, 17)
    nrm = lambda k, shape, scale: jax.random.normal(k, shape, jnp.float32) * scale
    mix_w = HG_WIDTH + SC_WIDTH
    return {
        'x': nrm(ks[0], (BATCH, SEQ, D_MODEL), 1.0),
        'c': nrm(ks[1], (BATCH, D_MODEL), 1.0),
        'ctx': nrm(ks[2], (BATCH, CTX_LEN, D_MODEL), 1.0),
        'c_ctx': nrm(ks[3], (D_MODEL,), 1.0),
        'w_mod': nrm(ks[4], (DEPTH, D_MODEL, N_MOD * D_MODEL), 0.5 * D_MODEL ** -0.5),
        'b_mod': nrm(ks[5], (DEPTH, N_MOD * D_MODEL), 0.01),
        'norm1_g': 1.0 + nrm(ks[6], (DEPTH, D_MODEL), 0.1),
        'norm2_g': 1.0 + nrm(ks[7], (DEPTH, D_MODEL), 0.1),
        'w_in': nrm(ks[8], (DEPTH, D_MODEL, IN_COLS), D_MODEL ** -0.5),
        'conv_w': nrm(ks[9], (DEPTH, CONV_W, SC_WIDTH), CONV_W ** -0.5),
        'w_out': nrm(ks[10], (DEPTH, mix_w, D_MODEL), mix_w ** -0.5),
        'lb_logits': nrm(ks[11], (DEPTH, 2, HG_WIDTH), 0.5),
        'peer_wq': nrm(ks[12], (DEPTH, D_MODEL, PEER_HEADS * PEER_QDIM), D_MODEL ** -0.5),
        'peer_subkeys': nrm(ks[13], (DEPTH, PEER_HEADS, 2, N_KEYS, PEER_HALF), PEER_HALF ** -0.5),
        'peer_u': nrm(ks[14], (DEPTH, N_EXPERTS, D_MODEL), D_MODEL ** -0.5),
        'peer_v': nrm(ks[15], (DEPTH, N_EXPERTS, D_MODEL), PEER_HEADS ** -0.5),
        'final_g': 1.0 + nrm(ks[16], (D_MODEL,), 0.1),
    }

def first_block(x, c, ctx, c_ctx, w_mod, b_mod, norm1_g, norm2_g, w_in, conv_w, w_out,
              lb_logits, peer_wq, peer_subkeys, peer_u, peer_v, final_g):
    rows = x.shape[1] // GRID_W
    p_lb = jax.nn.softmax(lb_logits.astype(jnp.float32), axis=0)
    lower = jnp.cumsum(p_lb, axis=0) - p_lb[0]
    cond_x = jax.nn.silu(c)
    cond_c = jax.nn.silu(c_ctx)
    latent_conv = lambda u, w: grid_conv(u, w, rows)
    zero_state = jnp.zeros((ctx.shape[0], HG_HEADS, HG_DIM, HG_DIM), jnp.float32)
    xc = ctx
    for l in range(DEPTH):
        lbf = lower[l, 0].reshape(HG_HEADS, HG_DIM)
        lbb = lower[l, 1].reshape(HG_HEADS, HG_DIM)
        mod_x = (cond_x @ w_mod[l] + b_mod[l])[:, None, :]
        mod_c = (cond_c @ w_mod[l] + b_mod[l])[None, None, :]
        sh1x, sc1x, g1x, sh2x, sc2x, g2x = jnp.split(mod_x, N_MOD, axis=-1)
        sh1c, sc1c, g1c, sh2c, sc2c, g2c = jnp.split(mod_c, N_MOD, axis=-1)
        hc = modulate(rms_norm(xc, norm1_g[l]), sh1c, sc1c)
        if l < DEPTH - 1:
            yc, s_f, s_b = token_mixer(hc, w_in[l], w_out[l], conv_w[l], lbf, lbb,
                                       zero_state, zero_state, seq_conv)
            xc = xc + g1c * yc
            hc2 = modulate(rms_norm(xc, norm2_g[l]), sh2c, sc2c)
            xc = xc + g2c * peer_ffn(hc2, peer_wq[l], peer_subkeys[l], peer_u[l], peer_v[l])
        else:
            iv_c, zf_c, zb_c = jnp.split(hc @ w_in[l][:, :3 * HG_WIDTH], 3, axis=-1)
            s_f, s_b = hgrn2_final_states(iv_c, zf_c, zb_c, lbf, lbb)
        hx = modulate(rms_norm(x, norm1_g[l]), sh1x, sc1x)
        yx, _, _ = token_mixer(hx, w_in[l], w_out[l], conv_w[l], lbf, lbb, s_f, s_b, latent_conv)
        x = x + g1x * yx
        hx2 = modulate(rms_norm(x, norm2_g[l]), sh2x, sc2x)
        x = x + g2x * peer_ffn(hx2, peer_wq[l], peer_subkeys[l], peer_u[l], peer_v[l])
    return rms_norm(x, final_g)


D_FF = 2816
RET_HEADS = 4
RET_QK_DIM = 128
RET_V_DIM = 128
RET_CHUNK = 128
MLA_HEADS = 8
MLA_NOPE = 64
MLA_ROPE = 32
MLA_V = 64
Q_LORA = 256
KV_LORA = 128
Q_BLOCK = 128
ROPE_THETA = 10000.0
RET_Q_W = RET_HEADS * RET_QK_DIM
RET_V_W = RET_HEADS * RET_V_DIM
IN_SPLITS = [RET_Q_W, RET_Q_W, RET_V_W, RET_V_W, Q_LORA, KV_LORA, MLA_ROPE]
IN_WIDTH = sum(IN_SPLITS)
IN_OFFSETS = list(np.cumsum(IN_SPLITS)[:-1])
MIX_WIDTH = RET_HEADS * RET_V_DIM + MLA_HEADS * MLA_V


def rms_norm_2(x, g):
    xf = x.astype(jnp.float32)
    y = xf * lax.rsqrt(jnp.mean(xf * xf, axis=-1, keepdims=True) + EPS)
    return (y * g.astype(jnp.float32)).astype(x.dtype)

def rope_tables(positions, dim):
    inv = 1.0 / (ROPE_THETA ** (jnp.arange(0, dim, 2, dtype=jnp.float32) / dim))
    ang = positions.astype(jnp.float32)[..., None] * inv
    return jnp.cos(ang)[:, :, None, :], jnp.sin(ang)[:, :, None, :]

def apply_rope(x, cos, sin):
    xf = x.astype(jnp.float32)
    x1, x2 = jnp.split(xf, 2, axis=-1)
    return jnp.concatenate([x1 * cos - x2 * sin, x2 * cos + x1 * sin], axis=-1).astype(x.dtype)

def swiglu_ffn(h, w_gate, w_up, w_down):
    return (jax.nn.silu(h @ w_gate) * (h @ w_up)) @ w_down

def retention(q, k, v, g, gn, cos, sin):
    out_dtype = v.dtype
    B, S, H, dk = q.shape
    n = S // RET_CHUNK
    C = RET_CHUNK
    q = apply_rope(q, cos, sin).astype(jnp.float32)
    k = apply_rope(k, cos, sin).astype(jnp.float32) * (dk ** -0.5)
    v = v.astype(jnp.float32)

    def chunk(t):
        return t.reshape(B, n, C, H, -1).transpose(0, 3, 1, 2, 4)

    qc, kc, vc = chunk(q), chunk(k), chunk(v)
    lg = jnp.log(1.0 - 2.0 ** (-5.0 - jnp.arange(H, dtype=jnp.float32)))
    idx = jnp.arange(C, dtype=jnp.float32)
    rel = idx[:, None] - idx[None, :]
    decay = jnp.where(rel >= 0, jnp.exp(jnp.maximum(rel, 0.0)[None] * lg[:, None, None]), 0.0)
    scores = jnp.einsum('bhncd,bhnmd->bhncm', qc, kc) * decay[None, :, None]
    y_intra = jnp.einsum('bhncm,bhnme->bhnce', scores, vc)
    zeta = jnp.exp((C - 1 - idx)[None, :] * lg[:, None])
    chunk_kv = jnp.einsum('bhncd,bhnce->bhnde', kc * zeta[None, :, None, :, None], vc)
    chunk_decay = jnp.exp(C * lg)[None, :, None, None]

    def step(state, kv_n):
        return state * chunk_decay + kv_n, state

    init = jnp.zeros((B, H, dk, vc.shape[-1]), jnp.float32)
    _, prev = lax.scan(step, init, jnp.moveaxis(chunk_kv, 2, 0))
    prev = jnp.moveaxis(prev, 0, 2)
    xi = jnp.exp((idx + 1.0)[None, :] * lg[:, None])
    y_cross = jnp.einsum('bhncd,bhnde->bhnce', qc, prev) * xi[None, :, None, :, None]
    y = (y_intra + y_cross).transpose(0, 2, 3, 1, 4).reshape(B, S, H, -1)
    y = rms_norm_2(y, gn) * jax.nn.silu(g.astype(jnp.float32))
    return y.reshape(B, S, -1).astype(out_dtype)

def mla_attention(c_q, c_kv, k_rope, q_lat_norm, w_uq, kv_lat_norm, w_ukv,
                  qn_nope, qn_rope, kn_nope, kn_rope, cos, sin):
    B, S, _ = c_q.shape
    q = (rms_norm_2(c_q, q_lat_norm) @ w_uq).reshape(B, S, MLA_HEADS, MLA_NOPE + MLA_ROPE)
    kv = (rms_norm_2(c_kv, kv_lat_norm) @ w_ukv).reshape(B, S, MLA_HEADS, MLA_NOPE + MLA_V)
    q_nope, q_rope = q[..., :MLA_NOPE], q[..., MLA_NOPE:]
    k_nope, v = kv[..., :MLA_NOPE], kv[..., MLA_NOPE:]
    q_nope = rms_norm_2(q_nope, qn_nope)
    q_rope = apply_rope(rms_norm_2(q_rope, qn_rope), cos, sin)
    k_nope = rms_norm_2(k_nope, kn_nope)
    k_rope = apply_rope(rms_norm_2(k_rope[:, :, None, :], kn_rope), cos, sin)
    k_rope = jnp.broadcast_to(k_rope, (B, S, MLA_HEADS, MLA_ROPE))
    qf = jnp.concatenate([q_nope, q_rope], -1).transpose(0, 2, 1, 3).astype(jnp.float32)
    kf = jnp.concatenate([k_nope, k_rope], -1).transpose(0, 2, 1, 3).astype(jnp.float32)
    vf = v.transpose(0, 2, 1, 3).astype(jnp.float32)
    scale = (MLA_NOPE + MLA_ROPE) ** -0.5
    n_blk = S // Q_BLOCK
    q_blocks = qf.reshape(B, MLA_HEADS, n_blk, Q_BLOCK, -1).transpose(2, 0, 1, 3, 4)
    key_pos = jnp.arange(S)

    def block(args):
        qb, bi = args
        s = jnp.einsum('bhqd,bhkd->bhqk', qb, kf) * scale
        qpos = bi * Q_BLOCK + jnp.arange(Q_BLOCK)
        s = jnp.where(qpos[:, None] >= key_pos[None, :], s, -1e30)
        p = jax.nn.softmax(s, axis=-1)
        return jnp.einsum('bhqk,bhkd->bhqd', p, vf)

    o = lax.map(block, (q_blocks, jnp.arange(n_blk)))
    o = o.transpose(1, 0, 3, 2, 4).reshape(B, S, MLA_HEADS * MLA_V)
    return o.astype(c_q.dtype)

def second_inputs(seed: int = 0) -> dict:
    key = jax.random.key(seed)
    ks = iter(jax.random.split(key, 32))
    L, D, F = DEPTH, D_MODEL, D_FF

    def w(shape, fan_in):
        return jax.random.normal(next(ks), shape, jnp.float32) * (fan_in ** -0.5)

    def gain(shape):
        return 1.0 + 0.02 * jax.random.normal(next(ks), shape, jnp.float32)

    x = jax.random.normal(next(ks), (BATCH, SEQ, D), jnp.float32)
    positions = jnp.broadcast_to(jnp.arange(SEQ, dtype=jnp.int32)[None], (BATCH, SEQ))
    return {
        "x": x,
        "positions": positions,
        "ffn1_norm": gain((L, D)),
        "ffn1_w_gate": w((L, D, F), D),
        "ffn1_w_up": w((L, D, F), D),
        "ffn1_w_down": w((L, F, D), F),
        "mix_norm": gain((L, D)),
        "w_in": w((L, D, IN_WIDTH), D),
        "ret_head_norm": gain((L, RET_HEADS, RET_V_DIM)),
        "q_lat_norm": gain((L, Q_LORA)),
        "w_uq": w((L, Q_LORA, MLA_HEADS * (MLA_NOPE + MLA_ROPE)), Q_LORA),
        "kv_lat_norm": gain((L, KV_LORA)),
        "w_ukv": w((L, KV_LORA, MLA_HEADS * (MLA_NOPE + MLA_V)), KV_LORA),
        "qn_nope": gain((L, MLA_NOPE)),
        "qn_rope": gain((L, MLA_ROPE)),
        "kn_nope": gain((L, MLA_NOPE)),
        "kn_rope": gain((L, MLA_ROPE)),
        "w_o": w((L, MIX_WIDTH, D), MIX_WIDTH),
        "ffn2_norm": gain((L, D)),
        "ffn2_w_gate": w((L, D, F), D),
        "ffn2_w_up": w((L, D, F), D),
        "ffn2_w_down": w((L, F, D), F),
    }

def second_block(x, positions, ffn1_norm, ffn1_w_gate, ffn1_w_up, ffn1_w_down, mix_norm,
              w_in, ret_head_norm, q_lat_norm, w_uq, kv_lat_norm, w_ukv,
              qn_nope, qn_rope, kn_nope, kn_rope, w_o,
              ffn2_norm, ffn2_w_gate, ffn2_w_up, ffn2_w_down):
    B, S, _ = x.shape
    cos_r, sin_r = rope_tables(positions, RET_QK_DIM)
    cos_m, sin_m = rope_tables(positions, MLA_ROPE)
    for l in range(DEPTH):
        x = x + 0.5 * swiglu_ffn(rms_norm_2(x, ffn1_norm[l]), ffn1_w_gate[l], ffn1_w_up[l], ffn1_w_down[l])
        h = rms_norm_2(x, mix_norm[l])
        proj = h @ w_in[l]
        rq, rk, rv, rg, c_q, c_kv, k_rope = jnp.split(proj, IN_OFFSETS, axis=-1)
        y_ret = retention(rq.reshape(B, S, RET_HEADS, RET_QK_DIM), rk.reshape(B, S, RET_HEADS, RET_QK_DIM),
                          rv.reshape(B, S, RET_HEADS, RET_V_DIM), rg.reshape(B, S, RET_HEADS, RET_V_DIM),
                          ret_head_norm[l], cos_r, sin_r)
        y_mla = mla_attention(c_q, c_kv, k_rope, q_lat_norm[l], w_uq[l], kv_lat_norm[l], w_ukv[l],
                              qn_nope[l], qn_rope[l], kn_nope[l], kn_rope[l], cos_m, sin_m)
        x = x + jnp.concatenate([y_ret, y_mla], axis=-1) @ w_o[l]
        x = x + 0.5 * swiglu_ffn(rms_norm_2(x, ffn2_norm[l]), ffn2_w_gate[l], ffn2_w_up[l], ffn2_w_down[l])
    return x


def setup_inputs(seed=0):
    out = dict(first_inputs(seed))
    for name, value in second_inputs(seed + 1).items():
        if name != "x":
            out[name + "_2"] = value
    return out


def reference(
    x, c, ctx, c_ctx, w_mod, b_mod, norm1_g, norm2_g, w_in, conv_w, w_out, lb_logits, peer_wq,
    peer_subkeys, peer_u, peer_v, final_g, positions_2, ffn1_norm_2, ffn1_w_gate_2, ffn1_w_up_2,
    ffn1_w_down_2, mix_norm_2, w_in_2, ret_head_norm_2, q_lat_norm_2, w_uq_2, kv_lat_norm_2,
    w_ukv_2, qn_nope_2, qn_rope_2, kn_nope_2, kn_rope_2, w_o_2, ffn2_norm_2, ffn2_w_gate_2,
    ffn2_w_up_2, ffn2_w_down_2,
):
    x = first_block(
        x, c, ctx, c_ctx, w_mod, b_mod, norm1_g, norm2_g, w_in, conv_w, w_out, lb_logits,
        peer_wq, peer_subkeys, peer_u, peer_v, final_g,
    )
    return second_block(
        x, positions_2, ffn1_norm_2, ffn1_w_gate_2, ffn1_w_up_2, ffn1_w_down_2, mix_norm_2,
        w_in_2, ret_head_norm_2, q_lat_norm_2, w_uq_2, kv_lat_norm_2, w_ukv_2, qn_nope_2,
        qn_rope_2, kn_nope_2, kn_rope_2, w_o_2, ffn2_norm_2, ffn2_w_gate_2, ffn2_w_up_2,
        ffn2_w_down_2,
    )


_drawn_inputs = setup_inputs


def setup_inputs(seed=0):
    import zlib

    import numpy as np

    out = dict(_drawn_inputs(seed))
    spreads = {}
    factors = {'c_ctx': 3.66,
     'ffn1_norm_2': 3.795,
     'ret_head_norm_2': 4.992,
     'q_lat_norm_2': 8.0,
     'kv_lat_norm_2': 8.0,
     'qn_nope_2': 8.0,
     'qn_rope_2': 8.0,
     'kn_nope_2': 8.0,
     'kn_rope_2': 8.0,
     'ffn2_norm_2': 5.124}
    for name, (base, spread) in spreads.items():
        noise = np.random.default_rng([zlib.crc32(name.encode()), seed]).standard_normal(out[name].shape)
        drawn = base * np.exp(spread * noise) if base else spread * noise
        out[name] = __import__('jax').numpy.asarray(drawn.astype(out[name].dtype))
    for name, factor in factors.items():
        out[name] = (out[name] * factor).astype(out[name].dtype)
    return out
```

```python
import numpy as np
import concourse.bass as bass
from concourse import mybir
from concourse.alu_op_type import AluOpType as ALU

F32 = mybir.dt.float32
F32R = mybir.dt.float32r
F16 = mybir.dt.float16
U8 = mybir.dt.uint8
U32 = mybir.dt.uint32
I32 = mybir.dt.int32
ACT = mybir.ActivationFunctionType
AX = mybir.AxisListType

EPS = 1e-6
F_FLOOR = 1e-20
LOWEST = -3.0e38

PARAMS = [('norm1_g', 16), ('norm2_g', 16), ('b_mod', 96), ('final_g', 8), ('conv_w', 24), ('lb_logits', 16),
          ('c', 8), ('c_ctx', 8), ('ffn1_norm', 16), ('mix_norm', 16), ('ffn2_norm', 16), ('ret_norm', 8),
          ('q_lat', 4), ('kv_lat', 2), ('qn', 2), ('kn', 2)]
PCOL, PN = {}, 0
for _n, _w in PARAMS:
    PCOL[_n] = PN
    PN += _w


class Lane:

    def __init__(self, nc, eng, name):
        self.nc, self.eng, self.name = nc, eng, name
        self.turn, self.n, self.seen = 0, 0, {}
        self.sem = nc.alloc_semaphore(name + '0')
        self.last = None

    def after(self, *marks):
        for m in marks:
            if m is None:
                continue
            if isinstance(m, list):
                self.after(*m)
                continue
            key, sem, value = m
            if self.seen.get(key, 0) < value:
                self.eng.wait_ge(sem, value)
                self.seen[key] = value
        return self.eng

    def mark(self, ins):
        if self.n == 16000:
            self.turn, self.n = self.turn + 1, 0
            self.sem = self.nc.alloc_semaphore('%s%d' % (self.name, self.turn))
        self.n += 1
        ins.then_inc(self.sem, 1)
        self.last = ('%s%d' % (self.name, self.turn), self.sem, self.n)
        return self.last


class Arena:

    def __init__(self, nc, tag, start, end):
        self.nc, self.tag, self.at, self.end = nc, tag, start, end

    def take(self, name, shape, dtype=F32):
        size = int(np.prod(shape[1:])) * mybir.dt.size(dtype)
        at = self.at
        self.at += (size + 31) // 32 * 32
        assert self.at <= self.end, (self.tag, name, self.at, self.end)
        return self.nc.alloc_sbuf_tensor_at('%s_%s' % (self.tag, name), list(shape), dtype, offset=at)


class Tile:
    def __init__(self, tag, granule, sub, raw):
        self.tag, self.granule, self.sub, self.raw = tag, granule, sub, raw
        self.hi = self.lo = None
        self.ready = []


def schedule():
    def run(name, a, b):
        return [(name, g, 2, False) for g in range(a, b)]

    def mods(layer, a, b):
        return [('w_mod%d' % layer, g, 2, True) for g in range(a, b)]

    def mixed(main, side):
        out = []
        for n, g in enumerate(main):
            out.append(g)
            if n < len(side):
                out.append(side[n])
        return out

    def peer(layer, side):
        u, v = 'peer_u%d' % layer, 'peer_v%d' % layer
        return (run('peer_wq%d' % layer, 0, 8) + mixed(run(u, 0, 32), side) + run(u, 32, 64)
                + run(v, 0, 32) + run(v, 32, 64))

    order = mods(0, 0, 8)
    order += mixed(run('w_in0', 0, 16), mods(0, 8, 24))
    order += run('w_in0', 0, 16) + run('w_out0', 0, 4) + run('w_out0', 0, 4)
    order += peer(0, mods(1, 0, 24)) + peer(0, [])
    order += run('w_in1', 0, 16) + run('w_in1', 0, 6) + run('w_out1', 0, 4) + peer(1, [])
    for l in range(2):
        order += run('ffn1%d' % l, 0, 33) + run('w_in2%d' % l, 0, 10) + run('w_o2%d' % l, 0, 4)
        order += run('ffn2%d' % l, 0, 33)
    return order


def build(nc, t):
    pe = Lane(nc, nc.tensor, 'pe')
    act = Lane(nc, nc.scalar, 'act')
    dve = Lane(nc, nc.vector, 'dve')
    pool = Lane(nc, nc.gpsimd, 'pool')
    sp = Lane(nc, nc.sync, 'sp')
    engines = [pe, act, dve, pool]

    KB = 1024
    CONST0 = 16512
    RAW0 = CONST0 + 4960
    HL0 = RAW0 + 24 * KB
    H0 = HL0 + 24 * KB
    G0 = H0 + 16 * KB
    BIG0 = G0 + 11 * KB
    BIG1 = BIG0 + 128 * KB
    R1 = BIG0 + 64 * KB
    NG, NH = 3, 3

    ca = Arena(nc, 'const', CONST0, RAW0)
    ident = ca.take('ident', [128, 128])
    ones = ca.take('ones', [128, 128])
    onehot = ca.take('onehot', [128, 128])
    iota16 = ca.take('iota16', [128, 128], F16)
    par = ca.take('par', [128, PN])
    mod = ca.take('mod', [128, 2, 48, 2])
    gain1 = ca.take('gain1', [128, 2, 2, 8])
    gain2 = ca.take('gain2', [128, 2, 2, 8])
    lbv = ca.take('lbv', [128, 2, 8])
    lbc = ca.take('lbc', [128, 2, 8])
    epsc = ca.take('epsc', [128, 2])
    cols = ca.take('cols', [128, 64])
    gate_s = ca.take('gate_s', [128, 8])

    raw = nc.alloc_sbuf_tensor_at('raw', [128, NG, 2, 1024], F32, offset=RAW0)
    whi = nc.alloc_sbuf_tensor_at('whi', [128, NH, 1024], F32R, offset=HL0)
    wlo = nc.alloc_sbuf_tensor_at('wlo', [128, NH, 1024], F32R, offset=HL0 + 4 * KB * NH)
    ha = Arena(nc, 'h', H0, G0)
    h_hi = ha.take('hi', [128, 8, 256], F32R)
    h_lo = ha.take('lo', [128, 8, 256], F32R)
    X = nc.alloc_sbuf_tensor_at('X', [128, 8, 256], F32, offset=BIG0)
    na = Arena(nc, 'norm', BIG0 + 8 * KB, BIG0 + 16 * KB)
    nsq = na.take('sq', [128, 4, 256])
    nrt = na.take('rt', [128, 256])
    nrs = na.take('rs', [128, 256])
    ny = na.take('y', [128, 2, 256])

    bank = [nc.alloc_psum_tensor('bank%d' % b, [128, 512], F32) for b in range(8)]
    free = [[] for _ in range(8)]

    count = [0]

    def dma(dst, src, *deps):
        s = nc.alloc_semaphore('dma%d' % count[0])
        count[0] += 1
        sp.after(*deps).dma_start(dst, src).then_inc(s, 16)
        return ('dma%d' % (count[0] - 1), s, 16)

    def marks():
        return [e.last for e in engines]

    def fence():
        now = marks()
        for e in engines:
            e.after(now)

    order = schedule()
    tiles = []
    for g, (name, index, k, as_is) in enumerate(order):
        for sub in range(k):
            tiles.append(Tile(name, g, sub, as_is))
    split_tiles = [x for x in tiles if not x.raw]
    slot_sem = [nc.alloc_semaphore('raw%d' % s) for s in range(NG)]
    state = dict(pos=0, fetched=0, split=0, sidx=0, share=0, lot=0)
    landed = {}
    freed = {g: [] for g in range(len(order))}
    used_up = {}
    spent = {}

    def fetch():
        while state['fetched'] < len(order):
            g = state['fetched']
            if g >= NG and used_up.get(g - NG, 0) < order[g - NG][2]:
                return
            name, index, k, as_is = order[g]
            deps = freed[g - NG] if g >= NG else []
            sp.after(*deps).dma_start(raw[:, g % NG, 0:k, :], t[name][index]).then_inc(slot_sem[g % NG], 16)
            landed[g] = ('raw%d' % (g % NG), slot_sem[g % NG], 16 * (g // NG + 1))
            state['fetched'] += 1

    def give_back(g, *marks):
        freed[g].extend(marks)
        used_up[g] = used_up.get(g, 0) + 1
        fetch()

    def split():
        j = state['split']
        x = split_tiles[j]
        fetch()
        src = raw[:, x.granule % NG, x.sub, :]
        s = j % NH
        gone = spent[j - NH] if j >= NH else None
        x.hi, x.lo = whi[:, s, :], wlo[:, s, :]
        m = act.mark(act.after(landed[x.granule], gone).activation(x.hi, src, ACT.Copy))
        state['lot'] += state['share']
        lane = dve
        if state['lot'] >= 16:
            state['lot'] -= 16
            lane = pool
        k = lane.mark(lane.after(landed[x.granule], m, gone).tensor_tensor(x.lo, src, x.hi.bitcast(F32), ALU.subtract))
        x.ready = [m, k]
        state['split'] += 1
        give_back(x.granule, m, k)

    def take(tag):
        x = tiles[state['pos']]
        assert x.tag == tag, (x.tag, tag, state['pos'])
        state['pos'] += 1
        if x.raw:
            fetch()
            x.hi = raw[:, x.granule % NG, x.sub, :]
            x.ready = [landed[x.granule]]
            return x
        x.at = state['sidx']
        state['sidx'] += 1
        while state['split'] < min(x.at + NH, len(split_tiles)):
            split()
        return x

    def done(x, m):
        if x.raw:
            give_back(x.granule, m)
        else:
            spent[x.at] = m

    def mm(out, lhsT, rhs, start=True, stop=True, **kw):
        return nc.tensor.matmul(out, lhsT, rhs, start=start, stop=stop, skip_group_check=True, **kw)

    class Split:

        def __init__(self, hi, lo):
            self.hi, self.lo, self.m = hi, lo, [None] * 8

    def dense(tag, out, src, first, blocks=range(8)):
        x = take(tag)
        pe.after(first, x.ready)
        blocks = list(blocks)
        for n, b in enumerate(blocks):
            w, v = x.hi[:, b * 128:(b + 1) * 128], x.lo[:, b * 128:(b + 1) * 128]
            pe.after(src.m[b])
            mm(out, w, src.hi[:, b, :], start=n == 0, stop=False)
            mm(out, w, src.lo[:, b, :], start=False, stop=False)
            ins = mm(out, v, src.hi[:, b, :], start=False, stop=n == 7)
        m = pe.mark(ins)
        done(x, m)
        return m

    def dense_rows(tag, outs, src, first):
        res = []
        for j in range(4):
            x = take(tag)
            pe.after(first, x.ready)
            for k in range(2):
                b = 2 * j + k
                pe.after(src.m[b])
                w, v = x.hi[:, k * 512:(k + 1) * 512], x.lo[:, k * 512:(k + 1) * 512]
                for tt in range(2):
                    c = slice(tt * 128, (tt + 1) * 128)
                    mm(outs[tt], src.hi[:, b, c], w, start=b == 0, stop=False)
                    mm(outs[tt], src.lo[:, b, c], w, start=False, stop=False)
                    ins = mm(outs[tt], src.hi[:, b, c], v, start=False, stop=b == 7)
            m = pe.mark(ins)
            done(x, m)
            res.append(m)
            yield res

    cm = [dma(ident[:, :], t['consts'][:, 0:128]), dma(ones[:, :], t['consts'][:, 128:256]),
          dma(onehot[:, :], t['consts'][:, 384:512]), dma(cols[:, :], t['consts'][:, 512:576]),
          dma(par[:, :], t['params'])]
    iof = nsq[:, 0, 0:128]
    im = dma(iof, t['consts'][:, 256:384])
    m_eps = [dve.mark(nc.vector.memset(epsc[:, 0:1], EPS)), dve.mark(nc.vector.memset(epsc[:, 1:2], float(np.pi / 2)))]
    m_iota = dve.mark(dve.after(im).tensor_copy(iota16[:, :], iof))
    for e in engines:
        e.after(cm, m_eps, m_iota)

    def P(name, a, b=None):
        i = PCOL[name] + a
        return par[:, i:i + 1] if b is None else par[:, i:PCOL[name] + b]

    lm = nsq[:, 1, 0:8]
    le = nsq[:, 1, 16:32].rearrange('p (l e) -> p l e', l=2)
    ls = nsq[:, 1, 32:40]
    lg = P('lb_logits', 0, 16).rearrange('p (l e) -> p l e', l=2)
    m = dve.mark(nc.vector.tensor_tensor(lm, lg[:, 0, :], lg[:, 1, :], ALU.max))
    m = dve.mark(dve.after(m).tensor_tensor(le, lg, lm.unsqueeze(1).to_broadcast([128, 2, 8]), ALU.subtract))
    m = act.mark(act.after(m).activation(le, le, ACT.Exp))
    m = dve.mark(dve.after(m).tensor_tensor(ls, le[:, 0, :], le[:, 1, :], ALU.add))
    m = dve.mark(dve.after(m).reciprocal(ls, ls))
    m = dve.mark(dve.after(m).tensor_tensor(le, le, ls.unsqueeze(1).to_broadcast([128, 2, 8]), ALU.mult))
    m1 = dve.mark(dve.after(m).tensor_tensor(lbv[:, 0, :], le[:, 0, :], le[:, 0, :], ALU.subtract))
    m = dve.mark(dve.after(m).tensor_tensor(ls, le[:, 0, :], le[:, 1, :], ALU.add))
    m = dve.mark(dve.after(m).tensor_tensor(lbv[:, 1, :], ls, le[:, 0, :], ALU.subtract))
    m_lb = dve.mark(dve.after(m, m1).tensor_scalar(lbc[:, :, :], lbv[:, :, :], -1.0, 1.0, ALU.mult, ALU.add))
    for e in (act, dve, pool):
        e.after(m_lb)

    sca = Arena(nc, 'cond', G0 + 2 * KB, G0 + 5 * KB)
    cond = sca.take('cond', [128, 8, 32])
    mev = sca.take('mev', [128, 512])
    m0 = dve.mark(nc.vector.memset(cond[:, :, :], 0.0))
    m1 = act.mark(act.after(m0).activation(cond[:, :, 0], P('c', 0, 8), ACT.Silu))
    m2 = act.mark(act.after(m0).activation(cond[:, :, 1], P('c_ctx', 0, 8), ACT.Silu))
    pe.after(m0, m1, m2)
    mod_m = {}

    def modulation(layer, groups):
        ev_free = None
        for g in groups:
            first = free[4]
            for j in range(4):
                x = take('w_mod%d' % layer)
                pe.after(first, x.ready)
                for k in range(2):
                    b = 2 * j + k
                    q = b % 4
                    ins = mm(bank[4][32 * q:32 * q + 32, :], cond[:, b, :], x.hi[:, k * 512:(k + 1) * 512],
                             start=b < 4, stop=b >= 4, tile_position=(0, 32 * q))
                m = pe.mark(ins)
                done(x, m)
                if j % 2:
                    yield
            m = act.mark(act.after(m, ev_free).activation(mev[:, :], bank[4][:, :], ACT.Copy))
            free[4] = [m]
            pe.after(m, free[5])
            for b in range(4):
                ins = mm(bank[5][:, b * 128:(b + 1) * 128], mev[:, b * 128:(b + 1) * 128], onehot[:, :])
            ev_free = pe.mark(ins)
            turned = bank[5][:, :].rearrange('p (b j) -> p b j', b=4)[:, :, 0:2]
            bias = P('b_mod', layer * 48 + g * 4, layer * 48 + g * 4 + 4).unsqueeze(2).to_broadcast([128, 4, 2])
            m = dve.mark(dve.after(ev_free).tensor_tensor(mod[:, layer, g * 4:g * 4 + 4, :], turned, bias, ALU.add))
            free[5] = [m]
            mod_m[layer, g] = m
            for dst, norm, base in ((gain1, 'norm1_g', 2), (gain2, 'norm2_g', 8)):
                if base <= g < base + 2:
                    h = g - base
                    for who in range(2):
                        mod_m[layer, g, who] = dve.mark(dve.after(m).scalar_tensor_tensor(
                            dst[:, layer, who, 4 * h:4 * h + 4], mod[:, layer, g * 4:g * 4 + 4, who], 1.0,
                            P(norm, layer * 8 + 4 * h, layer * 8 + 4 * h + 4), ALU.add, ALU.mult))

    def M(layer, part, who):
        return mod[:, layer, part * 8:part * 8 + 8, who]

    class Squares:
        pass

    def squares_into(b):
        s = Squares()
        s.bank, s.squared, s.added = b, [], []
        return s

    def square(s, x, m):
        k = len(s.squared)
        if k >= 4:
            act.after(s.added[k - 4])
        s.squared.append(act.mark(act.after(m).activation(nsq[:, k % 4, :], x, ACT.Square)))

    def add_square(s):
        k = len(s.added)
        if k == 0:
            pe.after(free[s.bank])
        pe.after(s.squared[k])
        s.added.append(pe.mark(mm(bank[s.bank][:, 0:256], ones[:, :], nsq[:, k % 4, :], start=k == 0, stop=k == 7)))

    def one_over_rms(s):
        while len(s.added) < 8:
            add_square(s)
        m = act.mark(act.after(s.added[7]).activation(
            nrt[:, :], bank[s.bank][:, 0:256], ACT.Sqrt, bias=epsc[:, 0:1], scale=1.0 / 1024))
        free[s.bank] = [m]
        return dve.mark(dve.after(m).reciprocal(nrs[:, :], nrt[:, :]))

    yfree = [None, None]

    def norm(x, s, gain, shift, dst, dst_free, x_m=None):
        mr = one_over_rms(s)
        for b in range(8):
            y = ny[:, b % 2, :]
            m = dve.mark(dve.after(mr, yfree[b % 2], x_m).scalar_tensor_tensor(
                y, x[:, b, :], gain[:, b:b + 1], nrs[:, :], ALU.mult, ALU.mult))
            if shift is None:
                m1 = act.mark(act.after(m, dst_free).activation(dst.hi[:, b, :], y, ACT.Copy))
                m2 = dve.mark(dve.after(m1, dst_free).tensor_tensor(dst.lo[:, b, :], y, dst.hi[:, b, :].bitcast(F32),
                                                                    ALU.subtract))
            else:
                m1 = act.mark(act.after(m, dst_free).activation(dst.hi[:, b, :], y, ACT.Identity, bias=shift[:, b:b + 1]))
                m2 = dve.mark(dve.after(m1, dst_free).scalar_tensor_tensor(
                    dst.lo[:, b, :], y, shift[:, b:b + 1], dst.hi[:, b, :].bitcast(F32), ALU.add, ALU.subtract))
            yfree[b % 2] = [m1, m2]
            dst.m[b] = [m1, m2]
        return m2

    def run(main, *side):
        for _ in main:
            for s in side:
                next(s, None)

    def every(k, gen):
        while True:
            for _ in range(k - 1):
                yield
            next(gen, None)
            yield

    def finish(gen):
        for _ in gen:
            pass

    class Mixer:
        pass

    def mixers(layer):
        a = Arena(nc, 'mix%d' % layer, BIG0 + 16 * KB, BIG1)
        s = Mixer()
        s.conv_free = None
        s.KC = a.take('KC', [128, 1024])
        s.QC = a.take('QC', [128, 1024])
        s.att = a.take('att', [128, 2, 4, 256])
        s.o = a.take('o', [128, 4, 256])
        s.X2 = nc.alloc_sbuf_tensor_at('mix_X2_%d' % layer, [128, 8, 256], F32, offset=BIG0 + 24 * KB)
        s.cg = a.take('cg', [128, 4, 256])
        s.u = a.take('u', [128, 4, 256])
        s.cv = a.take('cv', [128, 4, 256])
        pair = []
        for n in range(2):
            m = Mixer()
            m.shared = s
            m.tag = n
            m.V = a.take('V%d' % n, [128, 2, 512])
            m.qP, m.qS, m.kX, m.kY, m.ff, m.fb, m.g = (a.take('%s%d' % (k, n), [128, 4, 256])
                                                      for k in ('qP', 'qS', 'kX', 'kY', 'ff', 'fb', 'g'))
            if n == 0:
                hi, lo = h_hi, h_lo
            else:
                hi, lo = a.take('hi', [128, 8, 256], F32R), a.take('lo', [128, 8, 256], F32R)
            m.h, m.mix = Split(hi, lo), Split(hi, lo)
            pair.append(m)
        b = Arena(nc, 'mixc%d' % layer, G0, G0 + 2 * KB)
        s.spread = b.take('spread', [8, 512])
        b = Arena(nc, 'mixs%d' % layer, G0 + 5 * KB, G0 + 11 * KB)
        s.S = b.take('S', [128, 2, 4, 128])
        s.masks = b.take('masks', [128, 8, 128], U8)
        wide = s.KC[:, :].rearrange('p (l t) -> p l t', l=8)
        deps = marks()
        m = dma(wide, t['masks'], deps)
        s.cm = [dma(s.spread[:, :], t['spread'][:, 0:512], deps),
                dve.mark(dve.after(m, deps).tensor_copy(s.masks[:, :, :], wide))]
        return pair

    def pairs(bk):
        return bk[:, :].rearrange('p (a b) -> p a b', a=2)

    def win(M_, layer, latent, only_state=False):
        s, h, tag = M_.shared, M_.h, 'w_in%d' % layer
        res = None
        for res in dense_rows(tag, [bank[2][:, :], bank[3][:, :]], h, free[2] + free[3]):
            yield
        M_.mV = []
        for tt in range(2):
            m = act.mark(act.after(res).activation(M_.V[:, tt, :], bank[2 + tt][:, :], ACT.Copy))
            free[2 + tt] = [m]
            M_.mV.append(m)

        turn = [0]

        def two():
            b = turn[0] % 2
            turn[0] += 1
            first = free[b]
            m = None
            for n in range(2):
                m = dense(tag, pairs(bank[b])[:, n, :], h, first)
                yield b, m if n else None

        M_.mk = [[], []]
        M_.mf = [[], []]
        for d, (f, k) in enumerate(((M_.ff, M_.kX), (M_.fb, M_.kY))):
            for j in range(2):
                for b, m in two():
                    yield
                c = slice(2 * j, 2 * j + 2)
                m1 = act.mark(act.after(m).activation(f[:, c, :], pairs(bank[b]), ACT.Sigmoid))
                m2 = act.mark(act.after(m).activation(k[:, c, :], pairs(bank[b]), ACT.Sigmoid, scale=-1.0))
                free[b] = [m1, m2]
                for n in range(2):
                    e = 2 * j + n
                    lb, lc = lbv[:, layer, 4 * d + e:4 * d + e + 1], lbc[:, layer, 4 * d + e:4 * d + e + 1]
                    m = dve.mark(dve.after(m1).tensor_scalar(f[:, e, :], f[:, e, :], lc, lb, ALU.mult, ALU.add))
                    M_.mf[d].append(dve.mark(dve.after(m).tensor_scalar(f[:, e, :], f[:, e, :], F_FLOOR, None, ALU.max)))
                    M_.mk[d].append(dve.mark(dve.after(m2).tensor_scalar(k[:, e, :], k[:, e, :], lc, None, ALU.mult)))
        M_.mk, M_.mf = M_.mk[0] + M_.mk[1], M_.mf[0] + M_.mf[1]
        if only_state:
            return
        M_.mq, M_.mg = [], []
        for j in range(2):
            for b, m in two():
                yield
            m = act.mark(act.after(m).activation(M_.qP[:, 2 * j:2 * j + 2, :], pairs(bank[b]), ACT.Copy))
            free[b] = [m]
            M_.mq.append(m)
        for j in range(2):
            for b, m in two():
                yield
            m = act.mark(act.after(m).activation(M_.g[:, 2 * j:2 * j + 2, :], pairs(bank[b]), ACT.Silu))
            free[b] = [m]
            M_.mg.append(m)
        mc, mu, mv = [], [], [None] * 4
        for j in range(2):
            for b, m in two():
                yield
            m = act.mark(act.after(m, s.conv_free).activation(s.cg[:, 2 * j:2 * j + 2, :], pairs(bank[b]), ACT.Copy))
            free[b] = [m]
            mc.append(m)
        for j in range(2):
            for b, m in two():
                yield
            c = slice(2 * j, 2 * j + 2)
            m = dve.mark(dve.after(m, mc[j]).tensor_tensor(s.u[:, c, :], pairs(bank[b]), s.cg[:, c, :], ALU.mult))
            free[b] = [m]
            mu.append(m)
        for e in range(4):
            w = [P('conv_w', layer * 12 + 4 * i + e) for i in range(3)]
            u, v = s.u[:, e, :], s.cv[:, e, :]
            m = act.mark(act.after(mu[e // 2]).activation(v, u, ACT.Copy, scale=w[1]))
            if latent and e < 2:
                u2, v2 = u.rearrange('p (r c) -> p r c', c=64), v.rearrange('p (r c) -> p r c', c=64)
                steps = [(v2[:, :, 1:64], u2[:, :, 0:63]), (v2[:, :, 0:63], u2[:, :, 1:64])]
            else:
                k = 64 if latent else 1
                steps = [(v[:, k:256], u[:, 0:256 - k]), (v[:, 0:256 - k], u[:, k:256])]
            for (vo, ui), wi in zip(steps, (w[0], w[2])):
                m = dve.mark(dve.after(m, mu[e // 2]).scalar_tensor_tensor(vo, ui, wi, vo, ALU.mult, ALU.add))
            mv[e] = m
        mb = []
        for j in range(2):
            for b, m in two():
                yield
            c = slice(2 * j, 2 * j + 2)
            m = dve.mark(dve.after(m, mv[2 * j:2 * j + 2]).tensor_tensor(s.cv[:, c, :], pairs(bank[b]), s.cv[:, c, :],
                                                                     ALU.mult))
            free[b] = [m]
            mb.append(m)
        M_.m_in = pe.last
        for j in range(2):
            put(M_.mix, 4 + 2 * j, s.cv[:, 2 * j:2 * j + 2, :], mb[j], M_.m_in)
        s.conv_free = M_.mix.m[4] + M_.mix.m[6]

    def put(dst, b, src, m, wait):
        c = slice(b, b + 2)
        m1 = act.mark(act.after(m, wait).activation(dst.hi[:, c, :], src, ACT.Copy))
        m2 = dve.mark(dve.after(m, m1, wait).tensor_tensor(dst.lo[:, c, :], src, dst.hi[:, c, :].bitcast(F32), ALU.subtract))
        dst.m[b] = dst.m[b + 1] = [m1, m2]

    def level_view(a, B):
        v = a.rearrange('p (n w) -> p n w', w=2 * B)
        return v[:, :, 0:B], v[:, :, B:2 * B]

    def flat(a):
        return a[:, :, :].rearrange('p h t -> p (h t)')

    def scan(M_, need_q, before=None):
        s = M_.shared
        for e in engines:
            e.after(before)
        qP, qS, kX, kY, ff, fb = (flat(x) for x in (M_.qP, M_.qS, M_.kX, M_.kY, M_.ff, M_.fb))
        mk, mf = M_.mk, M_.mf
        mu = [mk, mf]
        if need_q:
            kd = dve.mark(dve.after(mk).tensor_tensor(s.KC[:, :], kX, kY, ALU.add))
            m1 = dve.mark(dve.after(mf, M_.mq).tensor_tensor(qS, qP, fb, ALU.mult))
            yield
            pe.after(kd, M_.mq, free[6], free[7])
            for tt in range(2):
                for e in range(4):
                    c = slice(e * 256 + tt * 128, e * 256 + tt * 128 + 128)
                    ins = mm(bank[6 + tt][:, e * 128:(e + 1) * 128], s.KC[:, c], qP[:, c])
            mp = pe.mark(ins)
            m_att = []
            for tt in range(2):
                m = dve.mark(dve.after(mp).tensor_tensor(
                    s.att[:, tt, :, tt * 128:tt * 128 + 128], bank[6 + tt][:, :].rearrange('p (h t) -> p h t', h=4),
                    ident[:, :].unsqueeze(1).to_broadcast([128, 4, 128]), ALU.mult))
                free[6 + tt] = [m]
                m_att.append(m)
            m2 = dve.mark(dve.after(mp, mf).tensor_tensor(qP, qP, ff, ALU.mult))
            mu = [mk, mf, m1, m2]
        B, lev = 1, 0
        kc_free = mp if need_q else None
        while B <= 64:
            n = 1024 // (2 * B)
            p0, p1 = level_view(qP, B)
            s0, s1 = level_view(qS, B)
            x0, x1 = level_view(kX, B)
            y0, y1 = level_view(kY, B)
            f0, f1 = (v[:, :, 0:1].to_broadcast([128, n, B]) for v in level_view(ff, B))
            b0, b1 = (v[:, :, 0:1].to_broadcast([128, n, B]) for v in level_view(fb, B))
            copied = None
            if need_q:
                c0, c1 = level_view(s.KC[:, :], B)
                d0, d1 = level_view(s.QC[:, :], B)
                copied = [act.mark(act.after(mu, kc_free).activation(o, i, ACT.Copy))
                          for o, i in ((c0, x0), (c1, y1), (d0, s0), (d1, p1))]
            mu = [dve.mark(dve.after(mu, copied).tensor_tensor(a, a, f, ALU.mult)) for a, f in ((x0, f1), (y1, b0))]
            if need_q:
                mu += [dve.mark(dve.after(copied).tensor_tensor(a, a, f, ALU.mult)) for a, f in ((s0, b1), (p1, f0))]
            tm = []
            for a in (ff, fb):
                lo, hi = (v[:, :, 0:1] for v in level_view(a, B))
                tm.append(pool.mark(pool.after(mu).tensor_tensor(lo, lo, hi, ALU.mult)))
            mu += tm
            yield
            if need_q:
                pe.after(copied, free[6], free[7])
                for tt in range(2):
                    for e in range(4):
                        c = slice(e * 256 + tt * 128, e * 256 + tt * 128 + 128)
                        ins = mm(bank[6 + tt][:, e * 128:(e + 1) * 128], s.KC[:, c], s.QC[:, c])
                kc_free = pe.mark(ins)
                for tt in range(2):
                    m_att[tt] = dve.mark(dve.after(kc_free, m_att[tt]).copy_predicated(
                        s.att[:, tt, :, tt * 128:tt * 128 + 128],
                        s.masks[:, lev, :].unsqueeze(1).to_broadcast([128, 4, 128]),
                        bank[6 + tt][:, :].rearrange('p (h t) -> p h t', h=4)))
                    free[6 + tt] = [m_att[tt]]
                yield
            B, lev = 2 * B, lev + 1
        if need_q:
            pe.after(mu, free[6], free[7])
            for e in range(4):
                a, b = slice(e * 256, e * 256 + 128), slice(e * 256 + 128, e * 256 + 256)
                mm(bank[6][:, e * 128:(e + 1) * 128], kX[:, a], qP[:, b])
                ins = mm(bank[7][:, e * 128:(e + 1) * 128], kY[:, b], qS[:, a])
            mp = pe.mark(ins)
            mo = []
            for tt in range(2):
                c = slice(128 - tt * 128, 256 - tt * 128)
                m = act.mark(act.after(mp).activation(s.att[:, tt, :, c],
                                                            bank[6 + tt][:, :].rearrange('p (h t) -> p h t', h=4), ACT.Copy))
                free[6 + tt] = [m]
                mo.append(m)
            M_.m_att = m_att + mo
        v = lambda a: a.rearrange('p (h t) -> p h t', h=4)
        wide = lambda a, i: v(a)[:, :, i:i + 1].to_broadcast([128, 4, 128])
        M_.m_full = [
            dve.mark(dve.after(mu, mp if need_q else None).tensor_tensor(v(kX)[:, :, 0:128], v(kX)[:, :, 0:128], wide(ff, 128), ALU.mult)),
            dve.mark(dve.after(mu).tensor_tensor(v(kY)[:, :, 128:256], v(kY)[:, :, 128:256], wide(fb, 0), ALU.mult))]
        if need_q:
            M_.m_full += [
                dve.mark(dve.after(mu).tensor_tensor(v(qS)[:, :, 0:128], v(qS)[:, :, 0:128], wide(fb, 128), ALU.mult)),
                dve.mark(dve.after(mu).tensor_tensor(v(qP)[:, :, 128:256], v(qP)[:, :, 128:256], wide(ff, 0), ALU.mult))]
        M_.m_full += mu
        yield

    def states(M_, before=None):
        s = M_.shared
        for e in engines:
            e.after(before)
        ms = []
        kT = [s.KC, s.QC]
        for d, k in enumerate((M_.kX, M_.kY)):
            mt = []
            for tt in range(2):
                pe.after(M_.m_full, free[6 + tt])
                for e in range(4):
                    ins = nc.tensor.transpose(bank[6 + tt][:, e * 128:(e + 1) * 128], k[:, e, tt * 128:(tt + 1) * 128],
                                              ident[:, :])
                mp = pe.mark(ins)
                m = act.mark(act.after(mp).activation(kT[d][:, tt * 512:(tt + 1) * 512], bank[6 + tt][:, :], ACT.Copy))
                free[6 + tt] = [m]
                mt.append(m)
            yield
            pe.after(mt, M_.mV, free[4 + d])
            for e in range(4):
                for tt in range(2):
                    ins = mm(bank[4 + d][:, e * 128:(e + 1) * 128], kT[d][:, tt * 512 + e * 128:tt * 512 + (e + 1) * 128],
                             M_.V[:, tt, e * 128:(e + 1) * 128], start=tt == 0, stop=tt == 1)
            mp = pe.mark(ins)
            m = dve.mark(dve.after(mp).tensor_copy(s.S[:, d, :, :], bank[4 + d][:, :].rearrange('p (h v) -> p h v', h=4)))
            free[4 + d] = [m]
            ms.append(m)
            yield
        s.mS = ms

    def head_norm(o, mo, row_bank, wide_banks, gains, gate, mg, sq, rows, mix, spread, mix_free):
        rt, rr = rows
        pe.after(free[row_bank])
        for e in range(4):
            m = act.mark(act.after(mo[e // 2]).activation(sq[:, e, :], o[:, e, :], ACT.Square))
            pe.after(m)
            ins = mm(bank[row_bank][0:8, 0:256], cols[:, 7 - e:15 - e], sq[:, e, :], start=e == 0, stop=e == 3)
        mp = pe.mark(ins)
        m = act.mark(act.after(mp).activation(rt, bank[row_bank][0:8, 0:256], ACT.Sqrt, bias=epsc[0:8, 0:1], scale=1.0 / 128))
        free[row_bank] = [m]
        m = dve.mark(dve.after(m).reciprocal(rr, rt))
        yield
        for j in range(2):
            b = wide_banks[j]
            pe.after(m, free[b])
            for n in range(2):
                e = 2 * j + n
                ins = mm(pairs(bank[b])[:, n, :], spread[:, e * 128:(e + 1) * 128], rr)
            mp = pe.mark(ins)
            c = slice(2 * j, 2 * j + 2)
            if gains is None:
                ma = dve.mark(dve.after(mp, mo[j]).tensor_tensor(o[:, c, :], o[:, c, :], pairs(bank[b]), ALU.mult))
            else:
                for n in range(2):
                    e = 2 * j + n
                    ma = dve.mark(dve.after(mp, mo[j]).scalar_tensor_tensor(
                        o[:, e, :], o[:, e, :], gains[e], pairs(bank[b])[:, n, :], ALU.mult, ALU.mult))
            free[b] = [ma]
            ma = dve.mark(dve.after(ma, mg).tensor_tensor(o[:, c, :], o[:, c, :], gate[:, c, :], ALU.mult))
            put(mix, 2 * j, o[:, c, :], ma, mix_free)
            yield

    def mix_out(M_, state, before=None):
        s = M_.shared
        for e in engines:
            e.after(before)
        mo = []
        for j in range(2):
            b = 4 + j
            pe.after(M_.m_att, M_.mV, M_.m_full if state else None, s.mS if state else None, free[b])
            for n in range(2):
                e = 2 * j + n
                c = slice(e * 128, (e + 1) * 128)
                out = pairs(bank[b])[:, n, :]
                mm(out, M_.V[:, 0, c], s.att[:, 0, e, :], start=True, stop=False)
                ins = mm(out, M_.V[:, 1, c], s.att[:, 1, e, :], start=False, stop=not state)
                if state:
                    mm(out, s.S[:, 0, e, :], M_.qP[:, e, :], start=False, stop=False)
                    ins = mm(out, s.S[:, 1, e, :], M_.qS[:, e, :], start=False, stop=True)
            mp = pe.mark(ins)
            m = act.mark(act.after(mp).activation(s.o[:, 2 * j:2 * j + 2, :], pairs(bank[b]), ACT.Copy))
            free[b] = [m]
            mo.append(m)
            yield
        sq = s.KC[:, :].rearrange('p (h t) -> p h t', h=4)
        rows = s.QC[0:8, 0:256], s.QC[0:8, 256:512]
        yield from head_norm(s.o, mo, 6, (7, 6), None, M_.g, M_.mg, sq, rows, M_.mix, s.spread[:, :], M_.m_in)

    def residual(tag, src, gate, sums, blocks, xm, banks):
        out = []
        for j in range(4):
            b = banks[j % 2]
            first = free[b]
            for n in range(2):
                m = dense(tag, pairs(bank[b])[:, n, :], src, first, blocks)
            for n in range(2):
                e = 2 * j + n
                if gate is None:
                    mx = dve.mark(dve.after(m, xm).tensor_tensor(X[:, e, :], pairs(bank[b])[:, n, :], X[:, e, :], ALU.add))
                else:
                    mx = dve.mark(dve.after(m, xm).scalar_tensor_tensor(
                        X[:, e, :], pairs(bank[b])[:, n, :], gate[:, e:e + 1], X[:, e, :], ALU.mult, ALU.add))
                free[b] = [mx]
                out.append(mx)
                if sums is not None:
                    square(sums, X[:, e, :], mx)
            if sums is not None and j:
                add_square(sums)
                add_square(sums)
            yield out

    ua = Arena(nc, 'sel', G0, BIG0)
    i1T, i2T, g1T, g2T = (ua.take(k, [128, 256], F16) for k in ('i1T', 'i2T', 'g1T', 'g2T'))
    oneA = ua.take('oneA', [128, 2, 8, 128], F16)
    oneB1 = ua.take('oneB1', [128, 2, 8, 64], F16)
    oneB2 = ua.take('oneB2', [128, 2, 8, 64], F16)
    oneO = ua.take('oneO', [128, 8, 64], F16)
    acts = [nc.alloc_sbuf_tensor_at('act%d' % n, [128, 64, 256], F32, offset=BIG0 + n * 64 * KB) for n in range(2)]
    za = Arena(nc, 'z', H0, G0)
    z_hi = za.take('hi', [128, 4, 2, 256], F32R)
    z_lo = za.take('lo', [128, 4, 2, 256], F32R)
    ra = Arena(nc, 'rank', R1, BIG1)
    skT = ra.take('skT', [128, 16, 128])
    qrT = ra.take('qrT', [128, 16, 256])
    SC = ra.take('SC', [128, 2, 16, 128])
    tv = ra.take('tv', [128, 2, 16, 16])
    ti = ra.take('ti', [128, 2, 16, 16], U32)
    tif = ra.take('tif', [128, 2, 16, 16])
    cand = ra.take('cand', [128, 2, 2, 256])
    top = ra.take('top', [128, 2, 8, 16])
    pos = ra.take('pos', [128, 2, 8, 16], U32)
    pab = ra.take('pab', [128, 2, 2, 8, 16], U32)
    paf = ra.take('paf', [128, 2, 2, 8, 16])
    hot = ra.take('hot', [128, 2, 2, 16, 16])
    sel = ra.take('sel', [128, 3, 2, 128])
    tsum = ra.take('tsum', [128, 2, 2, 8])
    iota_f = cols[:, 16:32]

    def ranks(j, msc):
        def best(vals, ids, src, deps, n):
            ms = [dve.mark(dve.after(deps).max(vals(q)[:, 0:8], src(q))) for q in range(n)]
            yield
            m1 = [dve.mark(dve.after(ms[q]).max_index(ids(q)[:, 0:8], vals(q)[:, 0:8], src(q))) for q in range(n)]
            yield
            m2 = [dve.mark(dve.after(m1[q]).match_replace(src(q), vals(q)[:, 0:8], src(q), LOWEST)) for q in range(n)]
            yield
            m3 = [dve.mark(dve.after(m2[q]).max(vals(q)[:, 8:16], src(q))) for q in range(n)]
            yield
            m4 = [dve.mark(dve.after(m3[q]).max_index(ids(q)[:, 8:16], vals(q)[:, 8:16], src(q))) for q in range(n)]
            yield m4

        at = lambda q: (q // 2, 2 * j + q % 2)
        for m in best(lambda q: tv[:, at(q)[0], at(q)[1], :], lambda q: ti[:, at(q)[0], at(q)[1], :],
                      lambda q: SC[:, at(q)[0], at(q)[1], :], msc, 4):
            yield
        mi = dve.mark(dve.after(m).tensor_copy(tif[:, :, 2 * j:2 * j + 2, :], ti[:, :, 2 * j:2 * j + 2, :]))
        cd = cand[:, j % 2, :, :]
        mc = [dve.mark(dve.after(m).tensor_tensor(
            cd[:, tt, :].rearrange('p (a b) -> p a b', a=16),
            tv[:, tt, 2 * j, :].unsqueeze(2).to_broadcast([128, 16, 16]),
            tv[:, tt, 2 * j + 1, :].unsqueeze(1).to_broadcast([128, 16, 16]), ALU.add)) for tt in range(2)]
        yield
        for m in best(lambda q: top[:, q, j, :], lambda q: pos[:, q, j, :], lambda q: cd[:, q, :], mc, 2):
            yield
        m1 = dve.mark(dve.after(m).tensor_scalar(pab[:, 0, :, j, :], pos[:, :, j, :], 4, None, ALU.logical_shift_right))
        m2 = dve.mark(dve.after(m).tensor_scalar(pab[:, 1, :, j, :], pos[:, :, j, :], 15, None, ALU.bitwise_and))
        mf = dve.mark(dve.after(m1, m2).tensor_copy(paf[:, :, :, j, :], pab[:, :, :, j, :]))
        for p in range(2):
            hp = hot[:, p, :, :, :]
            m = dve.mark(dve.after(mf).tensor_tensor(
                hp, paf[:, p, :, j, :].unsqueeze(3).to_broadcast([128, 2, 16, 16]),
                iota_f.unsqueeze(1).unsqueeze(1).to_broadcast([128, 2, 16, 16]), ALU.is_equal))
            yield
            m = dve.mark(dve.after(m, mi).tensor_tensor(
                hp, hp, tif[:, :, 2 * j + p, :].unsqueeze(2).to_broadcast([128, 2, 16, 16]), ALU.mult))
            yield
            m = dve.mark(dve.after(m).tensor_reduce(
                sel[:, p, :, 16 * j:16 * j + 16], hp, AX.X, ALU.add))
            yield
        U.ranked = m

    class Unit:
        pass

    U = Unit()

    def gates():
        ta = top[:, :, :, :]
        m = dve.mark(dve.after(U.ranked).tensor_tensor(
            paf[:, 0, :, :, :], ta, top[:, :, :, 0:1].to_broadcast([128, 2, 8, 16]), ALU.subtract))
        m = act.mark(act.after(m).activation(paf[:, 1, :, :, :], paf[:, 0, :, :, :], ACT.Exp))
        m1 = dve.mark(dve.after(m).tensor_reduce(tsum[:, 0, :, :], paf[:, 1, :, :, :], AX.X, ALU.add))
        m1 = dve.mark(dve.after(m1).reciprocal(tsum[:, 1, :, :], tsum[:, 0, :, :]))
        m1 = dve.mark(dve.after(m1).tensor_scalar(tsum[:, 1, :, :], tsum[:, 1, :, :], 4096.0, None, ALU.mult))
        m = dve.mark(dve.after(m1).tensor_tensor(
            sel[:, 2, :, :].rearrange('p t (h k) -> p t h k', h=8), paf[:, 1, :, :, :],
            tsum[:, 1, :, :].unsqueeze(3).to_broadcast([128, 2, 8, 16]), ALU.mult))
        yield
        pe.after(m, U.ranked, free[2], free[3])
        for n in range(3):
            for tt in range(2):
                c = (n % 2) * 256 + tt * 128
                ins = nc.tensor.transpose(bank[2 + n // 2][:, c:c + 128], sel[:, n, tt, :], ident[:, :])
        m = pe.mark(ins)
        U.off_scratch = [m, dve.last]
        a = act.mark(act.after(m, U.sel_free).activation(i1T[:, :], bank[2][:, 0:256], ACT.Copy))
        b = act.mark(act.after(m, U.sel_free).activation(i2T[:, :], bank[2][:, 256:512], ACT.Copy))
        c = act.mark(act.after(m, U.sel_free).activation(g1T[:, :], bank[3][:, 0:256], ACT.Copy))
        d = dve.mark(dve.after(m, c, U.sel_free).tensor_tensor(g2T[:, :], bank[3][:, 0:256], g1T[:, :], ALU.subtract))
        free[2] = [a, b]
        free[3] = [c, d]
        U.m_sel = [a, b, c, d]

    def queries(layer, h, before):
        ms = dma(skT[:, :, :], t['subkeys'][layer], before)
        for e in (act, dve):
            e.after(before)
        mq, U.todo = [None] * 8, []

        def score(j):
            b = 2 + j % 2
            pe.after(mq[j], ms, free[b])
            out = bank[b][:, :].rearrange('p (s t k) -> p s t k', s=2, t=2)
            for p in range(2):
                for tt in range(2):
                    ins = mm(out[:, p, tt, :], qrT[:, 2 * j + p, tt * 128:(tt + 1) * 128], skT[:, 2 * j + p, :])
            m = pe.mark(ins)
            m = act.mark(act.after(m).activation(
                SC[:, :, 2 * j:2 * j + 2, :].rearrange('p t s k -> p s t k'), out, ACT.Copy))
            free[b] = [m]
            U.todo.append(ranks(j, m))

        for j in range(8):
            first = free[j % 2]
            for n in range(2):
                m = dense('peer_wq%d' % layer, pairs(bank[j % 2])[:, n, :], h, first)
                yield
            mq[j] = act.mark(act.after(m).activation(qrT[:, 2 * j:2 * j + 2, :], pairs(bank[j % 2]), ACT.Copy))
            free[j % 2] = [mq[j]]
            if j:
                score(j - 1)
        score(7)
        U.queried = True

    def ranking():
        n = 0
        while n < 8:
            while len(U.todo) <= n:
                yield
            yield from U.todo[n]
            n += 1
        yield from gates()

    def first_half(layer, h, half, before):
        for i in range(32):
            b = i % 2
            first = free[b]
            for n in range(2):
                m = dense('peer_u%d' % layer, pairs(bank[b])[:, n, :], h, first)
                yield
            m = act.mark(act.after(m, before() if i == 0 else None).activation(
                acts[half][:, 2 * i:2 * i + 2, :], pairs(bank[b]), ACT.Gelu))
            free[b] = [m]
            U.m_act[half] = m

    def gating(half):
        used = U.hot_free
        zm = [None, None]
        dep = U.m_sel

        made = [None, None]

        def build(n):
            k, c = n % 2, slice(8 * n, 8 * n + 8)
            w = lambda a, x: a.unsqueeze(2).to_broadcast([128, 8, x])
            mA = dve.mark(dve.after(dep, used[k]).tensor_tensor(
                oneA[:, k, :, :], iota16[:, :].unsqueeze(1).to_broadcast([128, 8, 128]), w(i1T[:, c], 128), ALU.is_equal))
            mO = dve.mark(dve.after(dep, made).tensor_tensor(
                oneO[:, :, :], iota16[:, 64 * half:64 * half + 64].unsqueeze(1).to_broadcast([128, 8, 64]),
                w(i2T[:, c], 64), ALU.is_equal))
            m1 = dve.mark(dve.after(mO, used[k]).tensor_tensor(oneB1[:, k, :, :], oneO[:, :, :], w(g1T[:, c], 64), ALU.mult))
            m2 = dve.mark(dve.after(mO, used[k]).tensor_tensor(oneB2[:, k, :, :], oneO[:, :, :], w(g2T[:, c], 64), ALU.mult))
            made[:] = [m1, m2]
            return [mA, m1, m2]

        ready = build(0)
        yield
        for n in range(32):
            k, b = n % 2, 2 + n % 2
            pe.after(ready, free[b])
            for q in range(8):
                out = bank[b][:, 64 * q:64 * q + 64]
                mm(out, oneA[:, k, q, :], oneB1[:, k, q, :], start=True, stop=False)
                ins = mm(out, oneA[:, k, q, :], oneB2[:, k, q, :], start=False, stop=True)
            mp = pe.mark(ins)
            used[k] = mp
            if n < 31:
                ready = build(n + 1)
            yield
            z = acts[half][:, :, 8 * n:8 * n + 8]
            m = dve.mark(dve.after(mp, U.m_act[half]).tensor_tensor(
                z, z, bank[b][:, :].rearrange('p (t k) -> p k t', t=8), ALU.mult))
            free[b] = [m]
            U.m_z[half] = m
            yield

    def second_half(layer, half, accs, last):
        parts = {}

        def split_z(i):
            k = (32 * half + i) % 4
            src = acts[half][:, 2 * i:2 * i + 2, :]
            f = U.z_free[k]
            a = act.mark(act.after(U.m_z[half], f).activation(z_hi[:, k, :, :], src, ACT.Copy))
            b = dve.mark(dve.after(U.m_z[half], a, f).tensor_tensor(z_lo[:, k, :, :], src, z_hi[:, k, :, :].bitcast(F32),
                                                                  ALU.subtract))
            parts[i] = (k, [a, b])

        split_z(0)
        split_z(1)
        for i in range(32):
            if i + 2 < 32:
                split_z(i + 2)
            k, mz = parts[i]
            for n in range(2):
                x = take('peer_v%d' % layer)
                pe.after(x.ready, mz, accs)
                for b in range(8):
                    w, v = x.hi[:, b * 128:(b + 1) * 128], x.lo[:, b * 128:(b + 1) * 128]
                    out = pairs(bank[4 + b // 2])[:, b % 2, :]
                    first, end = half == 0 and i == 0 and n == 0, half == 1 and i == 31 and n == 1
                    mm(out, w, z_hi[:, k, n, :], start=first and b % 2 == 0, stop=False)
                    mm(out, w, z_lo[:, k, n, :], start=False, stop=False)
                    ins = mm(out, v, z_hi[:, k, n, :], start=False, stop=end)
                m = pe.mark(ins)
                done(x, m)
                yield
            U.z_free[k] = m
        U.m_out = m
        U.m_split[half] = dve.last

    def chain(*gens):
        for g in gens:
            yield from g

    def peer(layer, who, h, before, side, load, sums_bank):
        U.m_act, U.m_z, U.m_split = [None, None], [None, None], [None, None]
        U.z_free = [None] * 4
        U.sel_free = before
        state['share'] = 16
        rank = None
        q = queries(layer, h, before)
        next(q)
        rank = ranking()
        run(q, rank, rank)
        run(first_half(layer, h, 0, lambda: before), rank, rank, rank, every(2, side))
        finish(rank)
        finish(side)
        state['share'] = 13
        U.hot_free = [[pe.last, act.last]] * 2
        g0, g1 = gating(0), gating(1)
        run(first_half(layer, h, 1, lambda: U.off_scratch), g0)
        finish(g0)
        U.z_free = [pe.last] * 4
        run(second_half(layer, 0, free[4] + free[5] + free[6] + free[7], False), g1)
        finish(g1)
        xm = load([U.m_split[0], act.last])
        state['share'] = 8
        finish(second_half(layer, 1, [], True))
        gs = gate_s[:, :]
        mg = dve.mark(dve.after(xm).tensor_scalar(gs, M(layer, 5, who), 2.0 ** -12, None, ALU.mult))
        s = squares_into(sums_bank) if sums_bank is not None else None
        for e in range(8):
            b = 4 + e // 2
            m = dve.mark(dve.after(U.m_out, xm, mg).scalar_tensor_tensor(
                X[:, e, :], pairs(bank[b])[:, e % 2, :], gs[:, e:e + 1], X[:, e, :], ALU.mult, ALU.add))
            free[b] = [m]
            if s is not None:
                square(s, X[:, e, :], m)
                if e >= 2:
                    add_square(s)
        return s, m

    def scratch(name):
        return nc.dram_tensor(name, [128, 8, 256], F32).ap()

    def modulated():
        for e in engines:
            e.after(list(mod_m.values()))

    def squares(x, mx, b):
        s = squares_into(b)
        for e in range(8):
            square(s, x[:, e, :], mx)
            if e >= 2:
                add_square(s)
        return s

    def first_norm(x, s, layer, who, dst, before, mx):
        return norm(x, s, gain1[:, layer, who, :], M(layer, 0, who), dst, before, mx)

    def second_norm(s, layer, who, dst, before, mx):
        return norm(X, s, gain2[:, layer, who, :], M(layer, 3, who), dst, before, mx)

    def other_norm(x, src, layer, who, dst, deps):
        mx = dma(x[:, :, :], src, deps)
        yield
        yield
        yield
        s = squares(x, mx, 6)
        yield
        first_norm(x, s, layer, who, dst, None, mx)

    mx = dma(X[:, :, :], t['ctx'], marks())
    pair = mixers(0)
    mc_, mr_ = pair
    sh = mc_.shared
    for e in engines:
        e.after(sh.cm)
    finish(modulation(0, range(4)))
    modulated()
    first_norm(X, squares(X, mx, 6), 0, 1, mc_.h, None, mx)
    late = modulation(0, range(4, 12))
    run(win(mc_, 0, False), other_norm(sh.X2, t['x'], 0, 0, mr_.h, marks()), every(2, late))
    finish(late)
    modulated()

    def context_chain():
        yield from scan(mc_, True)
        yield from states(mc_)
        yield from mix_out(mc_, False, marks())

    def latent_chain(m, before):
        yield from scan(m, True, before)
        yield from mix_out(m, True, marks())

    side = context_chain()
    run(win(mr_, 0, True), side)
    finish(side)
    side = latent_chain(mr_, marks())
    next(side)
    by = [4, 5, 6, 7, 0, 1, 2, 3]
    s = squares_into(2)
    for res in residual('w_out0', mc_.mix, M(0, 2, 1), s, by, mx, (0, 1)):
        next(side)
    xc1, x1, xc2 = scratch('xc1'), scratch('x1'), scratch('xc2')
    m_xc1 = dma(xc1, X[:, :, :], res)
    h = Split(h_hi, h_lo)
    m = second_norm(s, 0, 1, h, pe.last, res)
    finish(side)
    mx = dma(X[:, :, :], t['x'], m, m_xc1)
    for res in residual('w_out0', mr_.mix, M(0, 2, 0), None, by, mx, (0, 1)):
        pass
    m_x1 = dma(x1, X[:, :, :], res)

    def loader(src, written):
        return lambda deps: dma(X[:, :, :], src, deps, written)

    _, m = peer(0, 1, h, marks() + [m_x1], modulation(1, range(12)), loader(xc1, m_xc1), None)
    modulated()
    m_xc2 = dma(xc2, X[:, :, :], m)
    mx = dma(X[:, :, :], x1, m_x1, m_xc2)
    second_norm(squares(X, mx, 0), 0, 0, h, pe.last, mx)
    s, m = peer(0, 0, h, marks(), iter(()), loader(x1, m_x1), 0)

    pair = mixers(1)
    mr_, mc_ = pair
    fence()
    sh = mr_.shared
    for e in engines:
        e.after(sh.cm)
    first_norm(X, s, 1, 0, mr_.h, None, m)
    run(win(mr_, 1, True), other_norm(sh.X2, xc2, 1, 1, mc_.h, marks() + [m_xc2]))
    side = scan(mr_, True)
    next(side)
    run(win(mc_, 1, False, True), side)
    other = scan(mc_, False)
    run(side, other)
    finish(other)
    finish(states(mc_, marks()))
    finish(mix_out(mr_, True, marks()))
    s = squares_into(2)
    for res in residual('w_out1', mr_.mix, M(1, 2, 0), s, by, m, (0, 1)):
        pass
    x2 = scratch('x2')
    m_x2 = dma(x2, X[:, :, :], res)
    second_norm(s, 1, 0, h, pe.last, res)
    s, m = peer(1, 0, h, marks() + [m_x2], iter(()), loader(x2, m_x2), 0)
    fence()

    ga = Arena(nc, 'tab', G0, BIG0)
    cosr, sinr, cosm, sinm = (ga.take(k, [128, 256]) for k in ('cosr', 'sinr', 'cosm', 'sinm'))
    permr, permm = ga.take('permr', [128, 128]), ga.take('permm', [128, 128])
    mask = ga.take('mask', [128, 384])
    spread = ga.take('spread', [8, 1024])
    a = Arena(nc, 'two', BIG0 + 16 * KB, BIG1)
    dec = a.take('dec', [128, 4, 384])
    spread16 = a.take('spread16', [16, 1024])
    cols2 = a.take('cols2', [128, 64])
    post = a.take('pos', [128, 256], I32)
    w_uq = a.take('uq', [128, 2, 1024])
    w_ukv = a.take('ukv', [128, 1024])
    rv = a.take('rv', [128, 2, 512])
    rraw = a.take('rraw', [128, 2, 2, 256])
    rk, rq, ry, rg = (a.take(k, [128, 4, 256]) for k in ('rk', 'rq', 'ry', 'rg'))
    rP = a.take('rP', [128, 4, 384])
    rsq = rP[:, :, 0:256]
    rows = a.take('rows', [16, 2, 256])
    rrows = a.take('rrows', [8, 2, 256])
    lat = a.take('lat', [128, 4, 256])
    tmp = a.take('tmp', [128, 2, 2, 256])
    qf, kf = a.take('qf', [128, 8, 256]), a.take('kf', [128, 8, 256])
    mv = a.take('mv', [128, 2, 512])
    mstat = a.take('mstat', [128, 4, 16])
    at = a.at
    mS = a.take('S', [128, 8, 384])
    PT = a.take('PT', [128, 8, 384])
    fa = Arena(nc, 'ffn', at, BIG1)
    fsg, fa32 = fa.take('sg', [128, 2, 256]), fa.take('a', [128, 2, 256])
    f_hi, f_lo = fa.take('hi', [128, 2, 256], F32R), fa.take('lo', [128, 2, 256], F32R)
    start = marks()
    m_tab = [dma(permr[:, :], t['perms'][:, 0:128], start), dma(permm[:, :], t['perms'][:, 128:256]),
             dma(mask[:, :], t['mask']), dma(spread[:, :], t['spread']), dma(dec[:, :, :], t['decay']),
             dma(spread16[:, :], t['spread16']), dma(cols2[:, :], t['cols2']),
             dma(post[:, :], t['positions'].partition_broadcast(128))]

    def tables(inv, sin, cos):
        r, k = tmp[:, 0, 0, :], tmp[:, 0, 1, :]
        big = 1.5 * 2.0 ** 23
        m = dve.mark(dve.after(m_tab).tensor_copy(k, post[:, :]))
        m = dve.mark(dve.after(m).tensor_scalar(r, k, inv, None, ALU.mult))
        yield
        m = dve.mark(dve.after(m).tensor_scalar(k, r, float(np.float32(0.5 / np.pi)), big, ALU.mult, ALU.add))
        m = dve.mark(dve.after(m).tensor_scalar(k, k, big, None, ALU.subtract))
        yield
        rest = 2 * np.pi
        for bits in (5, 14, 24, 34, 60):
            part = float(np.floor(rest * 2.0 ** bits) / 2.0 ** bits) if bits < 60 else float(rest)
            rest -= part
            m = dve.mark(dve.after(m).scalar_tensor_tensor(r, k, -part, r, ALU.mult, ALU.add))
            yield
        top = float(np.nextafter(np.float32(np.pi), np.float32(0)))
        m = dve.mark(dve.after(m).tensor_scalar(r, r, top, -top, ALU.min, ALU.max))
        m1 = act.mark(act.after(m).activation(sin, r, ACT.Sin))
        m = dve.mark(dve.after(m).scalar_tensor_tensor(k, r, -1.0, r, ALU.mult, ALU.max))
        m2 = act.mark(act.after(m).activation(cos, k, ACT.Sin, bias=epsc[:, 1:2], scale=-1.0))
        for e in (dve, pool):
            e.after(m1, m2)
        yield

    def ffn(tag, src, s, *side):
        f_free, ma = [None, None], {}
        accs = free[4] + free[5] + free[6] + free[7]
        for f in range(23):
            if f < 22:
                b = k = f % 2
                first = free[b]
                m1 = dense(tag, pairs(bank[b])[:, 0, :], src, first)
                m2 = dense(tag, pairs(bank[b])[:, 1, :], src, first)
                m = act.mark(act.after(m1, m2).activation(fsg[:, k, :], pairs(bank[b])[:, 0, :], ACT.Silu))
                free[b] = [m]
                m = dve.mark(dve.after(m, m2).tensor_tensor(fa32[:, k, :], pairs(bank[b])[:, 1, :], fsg[:, k, :], ALU.mult))
                free[b] = [m]
                m1 = act.mark(act.after(m, f_free[k]).activation(f_hi[:, k, :], fa32[:, k, :], ACT.Copy))
                m2 = dve.mark(dve.after(m1, f_free[k]).tensor_tensor(f_lo[:, k, :], fa32[:, k, :],
                                                                     f_hi[:, k, :].bitcast(F32), ALU.subtract))
                ma[f] = [m1, m2]
            if f:
                k = (f - 1) % 2
                x = take(tag)
                pe.after(x.ready, ma[f - 1], accs)
                for b in range(8):
                    w, v = x.hi[:, b * 128:(b + 1) * 128], x.lo[:, b * 128:(b + 1) * 128]
                    out = pairs(bank[4 + b // 2])[:, b % 2, :]
                    mm(out, w, f_hi[:, k, :], start=f == 1 and b % 2 == 0, stop=False)
                    mm(out, w, f_lo[:, k, :], start=False, stop=False)
                    ins = mm(out, v, f_hi[:, k, :], start=False, stop=f == 22)
                f_free[k] = pe.mark(ins)
                done(x, f_free[k])
            for g in side:
                next(g, None)
        for e in range(8):
            b = 4 + e // 2
            m = dve.mark(dve.after(f_free[1]).scalar_tensor_tensor(
                X[:, e, :], pairs(bank[b])[:, e % 2, :], 0.5, X[:, e, :], ALU.mult, ALU.add))
            free[b] = [m]
            if s is not None:
                square(s, X[:, e, :], m)
                if e >= 2:
                    add_square(s)
        return m

    def win2(l, src, R):
        tag = 'w_in2%d' % l
        R.lat = []
        for j in range(2):
            first = free[j]
            for n in range(2):
                m = dense(tag, pairs(bank[j])[:, n, :], src, first)
                yield
            m1 = act.mark(act.after(m).activation(lat[:, 2 * j:2 * j + 2, :], pairs(bank[j]), ACT.Copy))
            free[j] = [m1]
            m2 = act.mark(act.after(m).activation(tmp[:, j, :, :], pairs(bank[j]), ACT.Square))
            free[j] = [m2]
            R.lat += [m1, m2]
        R.started = True
        for res in dense_rows(tag, [bank[2][:, :], bank[3][:, :]], src, free[2] + free[3]):
            yield
        R.mv = []
        for tt in range(2):
            m = act.mark(act.after(res).activation(rv[:, tt, :], bank[2 + tt][:, :], ACT.Copy))
            free[2 + tt] = [m]
            R.mv.append(m)
        raw_free = [None, None]
        R.mk, R.mq, R.mg = [], [], []
        late = []

        def rotate(dst, j, n, m, marks_):
            pe.after(m, free[2 + n])
            mp = pe.mark(mm(bank[2 + n][:, :], permr[:, :], rraw[:, n, :, :].rearrange('p a b -> p (a b)')))
            c = slice(2 * j, 2 * j + 2)
            w = lambda x: x[:, :].unsqueeze(1).to_broadcast([128, 2, 256])
            ma = dve.mark(dve.after(m).tensor_tensor(dst[:, c, :], rraw[:, n, :, :], w(cosr), ALU.mult))
            mb = dve.mark(dve.after(mp, ma).tensor_tensor(rraw[:, n, :, :], pairs(bank[2 + n]), w(sinr), ALU.mult))
            free[2 + n] = [mb]
            m = dve.mark(dve.after(ma, mb).tensor_tensor(dst[:, c, :], dst[:, c, :], rraw[:, n, :, :], ALU.add))
            raw_free[n] = m
            marks_.append(m)

        for dst, marks_ in ((rk, R.mk), (rq, R.mq)):
            for j in range(2):
                first = free[j]
                for n in range(2):
                    m = dense(tag, pairs(bank[j])[:, n, :], src, first)
                    if n == 0 and late:
                        rotate(*late.pop(0))
                    yield
                m = act.mark(act.after(m, raw_free[j]).activation(rraw[:, j, :, :], pairs(bank[j]), ACT.Copy))
                free[j] = [m]
                late.append((dst, j, j, m, marks_))
        for j in range(2):
            first = free[j]
            for n in range(2):
                m = dense(tag, pairs(bank[j])[:, n, :], src, first)
                if late:
                    rotate(*late.pop(0))
                yield
            m = act.mark(act.after(m).activation(rg[:, 2 * j:2 * j + 2, :], pairs(bank[j]), ACT.Silu))
            free[j] = [m]
            R.mg.append(m)
        R.m_in = pe.last

    def retention(l, R, mix):
        mP = []
        for e in range(4):
            b = 2 + e % 2
            pe.after(R.mk[e // 2], R.mq[e // 2], free[b])
            mm(bank[b][:, 0:256], rk[:, e, 0:128], rq[:, e, :])
            mp = pe.mark(mm(bank[b][:, 256:384], rk[:, e, 128:256], rq[:, e, 128:256]))
            m = dve.mark(dve.after(mp).tensor_tensor(rP[:, e, :], bank[b][:, 0:384], dec[:, e, :], ALU.mult))
            free[b] = [m]
            mP.append(m)
        yield
        mo = []
        for j in range(2):
            b = j
            pe.after(mP[2 * j:2 * j + 2], R.mv, free[b])
            for n in range(2):
                e = 2 * j + n
                out, c = pairs(bank[b])[:, n, :], slice(e * 128, (e + 1) * 128)
                mm(out, rv[:, 0, c], rP[:, e, 0:256], start=True, stop=False)
                ins = mm(out[:, 128:256], rv[:, 1, c], rP[:, e, 256:384], start=False, stop=True)
            mp = pe.mark(ins)
            m = act.mark(act.after(mp).activation(ry[:, 2 * j:2 * j + 2, :], pairs(bank[b]), ACT.Copy))
            free[b] = [m]
            mo.append(m)
        yield
        gains = [P('ret_norm', 4 * l + e) for e in range(4)]
        act.after(mp)
        yield from head_norm(ry, mo, 2, (3, 2), gains, rg, R.mg, rsq, (rrows[:, 0, :], rrows[:, 1, :]), mix,
                             spread[:, :], R.m_in)

    def roots(b, n, deps):
        m = act.mark(act.after(deps).activation(rows[0:n, 0, :], bank[b][0:n, 0:256], ACT.Sqrt, bias=epsc[0:n, 0:1]))
        free[b] = [m]
        return dve.mark(dve.after(m).reciprocal(rows[0:n, 1, :], rows[0:n, 0, :]))

    def attention(l, R, mix, mw):
        w = lambda x: x[:, :].unsqueeze(1).to_broadcast([128, 2, 256])
        pe.after(R.lat, free[6])
        for i, c in enumerate((32, 32, 40, 48)):
            ins = mm(bank[6][0:8, 0:256], cols[:, c:c + 8], tmp[:, i // 2, i % 2, :], start=i == 0, stop=i == 3)
        m = roots(6, 8, pe.mark(ins))
        yield
        pe.after(m, free[6], free[7])
        mm(pairs(bank[7])[:, 0, :], spread[:, 0:128], rows[0:8, 1, :])
        mm(pairs(bank[7])[:, 1, :], spread[:, 128:256], rows[0:8, 1, :])
        mp = pe.mark(mm(bank[6][:, 0:256], spread[:, 256:384], rows[0:8, 1, :]))
        ml = []
        for i, (gcol, src) in enumerate(((P('q_lat', 2 * l), 0), (P('q_lat', 2 * l + 1), 0), (P('kv_lat', l), 1),
                                       (P('kn', l), 2))):
            bb = bank[6][:, 0:256] if src == 2 else pairs(bank[7])[:, src, :]
            m = dve.mark(dve.after(mp, R.lat).scalar_tensor_tensor(lat[:, i, :], lat[:, i, :], gcol, bb, ALU.mult, ALU.mult))
            free[6 if src == 2 else 7] = [m]
            ml.append(m)
        yield
        pe.after(ml, free[7])
        mp = pe.mark(mm(bank[7][:, 0:256], permm[:, :], lat[:, 3, :]))
        mb = dve.mark(dve.after(mp).tensor_tensor(tmp[:, 0, 0, :], bank[7][:, 0:256], sinm[:, :], ALU.mult))
        free[7] = [mb]
        ma = dve.mark(dve.after(mp, ml).tensor_tensor(lat[:, 3, :], lat[:, 3, :], cosm[:, :], ALU.mult))
        m = dve.mark(dve.after(ma, mb).tensor_tensor(lat[:, 3, :], lat[:, 3, :], tmp[:, 0, 0, :], ALU.add))
        m_kr = act.mark(act.after(m).activation(
            kf[64:96, :, :], lat[64:96, 3, :].unsqueeze(1).to_broadcast([32, 8, 256]), ACT.Copy))
        pe.after(mw)
        tfree = [mb, None]
        row_first = free[6]
        mk = []
        for j in range(4):
            b = 4 + j % 2
            pe.after(free[b])
            for n in range(2):
                e = 2 * j + n
                ins = mm(pairs(bank[b])[0:64, n, :], w_ukv[:, e * 64:(e + 1) * 64], lat[:, 2, :])
            mp = pe.mark(ins)
            k = j % 2
            m1 = act.mark(act.after(mp).activation(kf[0:64, 2 * j:2 * j + 2, :], pairs(bank[b])[0:64, :, :], ACT.Copy))
            m2 = act.mark(act.after(mp, tfree[k]).activation(tmp[0:64, k, :, :], pairs(bank[b])[0:64, :, :], ACT.Square))
            free[b] = [m1, m2]
            mk.append(m1)
            yield
            pe.after(m2, row_first)
            for n in range(2):
                e = 2 * j + n
                ins = mm(bank[6][0:8, 0:256], cols2[0:64, 39 - e:47 - e], tmp[0:64, k, n, :], start=e == 0, stop=e == 7)
            mp = tfree[k] = pe.mark(ins)
        m = roots(6, 8, mp)
        pe.after(free[4], free[5])
        for tt in range(2):
            ins = mm(bank[4 + tt][:, :], lat[:, 2, tt * 128:(tt + 1) * 128], w_ukv[:, 512:1024])
        mp = pe.mark(ins)
        m_v = []
        for tt in range(2):
            m1 = act.mark(act.after(mp).activation(mv[:, tt, :], bank[4 + tt][:, :], ACT.Copy))
            free[4 + tt] = [m1]
            m_v.append(m1)
        yield
        m_k = []
        for j in range(4):
            b = 4 + j % 2
            pe.after(m, free[b])
            for n in range(2):
                e = 2 * j + n
                ins = mm(pairs(bank[b])[0:64, n, :], spread[:, e * 128:e * 128 + 64], rows[0:8, 1, :])
            mp = pe.mark(ins)
            c = slice(2 * j, 2 * j + 2)
            m1 = dve.mark(dve.after(mp, mk).scalar_tensor_tensor(
                kf[0:64, c, :], kf[0:64, c, :], P('kn', l)[0:64, :], pairs(bank[b])[0:64, :, :], ALU.mult, ALU.mult))
            free[b] = [m1]
            m_k.append(m1)
            yield
        m_rows = m1
        mq = []
        row_first = free[6]
        for j in range(4):
            b = 4 + j % 2
            pe.after(free[b])
            for n in range(2):
                e = 2 * j + n
                for i in range(2):
                    o = i * 512 + (e % 4) * 128
                    ins = mm(pairs(bank[b])[:, n, :], w_uq[:, e // 4, o:o + 128], lat[:, i, :], start=i == 0, stop=i == 1)
            mp = pe.mark(ins)
            k = j % 2
            m1 = act.mark(act.after(mp).activation(qf[:, 2 * j:2 * j + 2, :], pairs(bank[b]), ACT.Copy))
            m2 = act.mark(act.after(mp, tfree[k]).activation(tmp[:, k, :, :], pairs(bank[b]), ACT.Square))
            free[b] = [m1, m2]
            mq.append(m1)
            yield
            pe.after(m2, row_first)
            for n in range(2):
                e = 2 * j + n
                ins = mm(bank[6][0:16, 0:256], cols2[:, 14 - 2 * e:30 - 2 * e], tmp[:, k, n, :], start=e == 0, stop=e == 7)
            mp = tfree[k] = pe.mark(ins)
        R.m_lat = mp
        act.after(m_rows)
        m = roots(6, 16, mp)
        yield
        m_q, turned = [], [None] * 4
        for j in range(5):
            if j < 4:
                b = 4 + j % 2
                pe.after(m, free[b])
                for n in range(2):
                    e = 2 * j + n
                    ins = mm(pairs(bank[b])[:, n, :], spread16[:, e * 128:(e + 1) * 128], rows[0:16, 1, :])
                mp = pe.mark(ins)
                c = slice(2 * j, 2 * j + 2)
                m1 = dve.mark(dve.after(mp, mq).scalar_tensor_tensor(
                    qf[:, c, :], qf[:, c, :], P('qn', l), pairs(bank[b]), ALU.mult, ALU.mult))
                free[b] = [m1]
                turned[j] = m1
            yield
            if j:
                i = j - 1
                b, k = 6 + i % 2, i % 2
                c = slice(2 * i, 2 * i + 2)
                pe.after(turned[i], free[b])
                mp = pe.mark(mm(bank[b][:, :], permm[:, :], qf[:, c, :].rearrange('p a b -> p (a b)')))
                m1 = dve.mark(dve.after(mp, tfree[k]).tensor_tensor(tmp[:, k, :, :], pairs(bank[b]), w(sinm), ALU.mult))
                free[b] = [m1]
                m2 = dve.mark(dve.after(mp).tensor_tensor(qf[:, c, :], qf[:, c, :], w(cosm), ALU.mult))
                m1 = dve.mark(dve.after(m1, m2).tensor_tensor(qf[:, c, :], qf[:, c, :], tmp[:, k, :, :], ALU.add))
                tfree[k] = m1
                m_q.append(m1)
        yield
        m_s = []
        scale = 96.0 ** -0.5
        for e in range(8):
            b = 4 + e % 2
            pe.after(m_q[e // 2], m_k[e // 2], m_kr, free[b])
            mm(bank[b][:, 0:256], qf[0:96, e, 128:256], kf[0:96, e, :])
            mp = pe.mark(mm(bank[b][:, 256:384], qf[0:96, e, 0:128], kf[0:96, e, 0:128]))
            m = dve.mark(dve.after(mp).scalar_tensor_tensor(mS[:, e, :], bank[b][:, 0:384], scale, mask[:, :],
                                                            ALU.mult, ALU.add))
            free[b] = [m]
            m_s.append(m)
            if e % 2:
                yield
        parts = (slice(0, 256), slice(256, 384))
        big = [dve.mark(dve.after(m_s).tensor_reduce(mstat[:, 0, 8 * i:8 * i + 8], mS[:, :, c], AX.X, ALU.max))
               for i, c in enumerate(parts)]
        m = dve.mark(dve.after(big).tensor_scalar(mstat[:, 1, :], mstat[:, 0, :], -1.0, None, ALU.mult))
        for e in range(8):
            for i, c in enumerate(parts):
                mE = act.mark(act.after(m).activation(mS[:, e, c], mS[:, e, c], ACT.Exp, bias=mstat[:, 1, 8 * i + e:8 * i + e + 1],
                                                      accum_out=mstat[:, 2, 8 * i + e:8 * i + e + 1]))
            if e % 4 == 3:
                yield
        mr = dve.mark(dve.after(mE).reciprocal(mstat[:, 3, :], mstat[:, 2, :]))
        mP = [dve.mark(dve.after(mr).tensor_tensor(
            mS[:, :, c], mS[:, :, c], mstat[:, 3, 8 * i:8 * i + 8].unsqueeze(2).to_broadcast([128, 8, c.stop - c.start]),
            ALU.mult)) for i, c in enumerate(parts)]
        yield
        mT = []
        for e in range(8):
            b = 4 + e % 2
            pe.after(mP, free[b])
            nc.tensor.transpose(bank[b][:, 0:128], mS[:, e, 256:384], ident[:, :])
            nc.tensor.transpose(bank[b][:, 128:256], mS[:, e, 0:128], ident[:, :])
            mp = pe.mark(nc.tensor.transpose(bank[b][:, 256:384], mS[:, e, 128:256], ident[:, :]))
            m = act.mark(act.after(mp).activation(PT[:, e, :], bank[b][:, 0:384], ACT.Copy))
            free[b] = [m]
            mT.append(m)
            if e % 2:
                yield
        for j in range(2):
            b = 6 + j
            pe.after(mT[4 * j:4 * j + 4], m_v, free[b])
            for n in range(2):
                for i in range(2):
                    e = 4 * j + 2 * n + i
                    out = pairs(bank[b])[64 * i:64 * i + 64, n, :]
                    mm(out, mv[:, 0, e * 64:(e + 1) * 64], PT[:, e, 0:256], start=n == 0, stop=False)
                    ins = mm(out[:, 128:256], mv[:, 1, e * 64:(e + 1) * 64], PT[:, e, 256:384], start=False, stop=True)
            mp = pe.mark(ins)
            R.out.append((4 + 2 * j, b, mp))
        yield

    def final_norm(s, mx):
        out = squares_into(1)
        mr = one_over_rms(s)
        for e in range(8):
            m = dve.mark(dve.after(mr, mx).scalar_tensor_tensor(X[:, e, :], X[:, e, :], P('final_g', e), nrs[:, :],
                                                                ALU.mult, ALU.mult))
            square(out, X[:, e, :], m)
            if e >= 2:
                add_square(out)
        return out, m

    s, m = final_norm(s, m)

    def sines():
        yield from tables(cols2[:, 48:49], sinr[:, :], cosr[:, :])
        yield from tables(cols2[:, 49:50], sinm[:, :], cosm[:, :])

    pe.after(m_tab)
    state['share'] = 6
    side = sines()
    wfree = None
    for l in range(2):
        mw = [dma(w_uq[:, :, :], t['w_uq'][l], start, wfree), dma(w_ukv[:, :], t['w_ukv'][l], wfree)]
        norm(X, s, P('ffn1_norm', 8 * l, 8 * l + 8), None, h, pe.last, m)
        s = squares_into(2)
        m = ffn('ffn1%d' % l, h, s, side)
        finish(side)
        fence()
        norm(X, s, P('mix_norm', 8 * l, 8 * l + 8), None, h, pe.last, m)
        R = Mixer()
        R.out, R.started = [], False
        mla = attention(l, R, h, mw)

        def after_start():
            while not R.started:
                yield
            yield from mla

        side = after_start()
        run(win2(l, h, R), side)
        mix = Split(h_hi, h_lo)
        run(retention(l, R, mix), side)
        finish(side)
        for base, b, mp in R.out:
            put(mix, base, pairs(bank[b]), [mp], R.m_in)
            free[b] = mix.m[base]
        wfree = pe.last
        s = squares_into(2)
        for res in residual('w_o2%d' % l, mix, None, s, by, m, (0, 1)):
            pass
        m = res
        fence()
        norm(X, s, P('ffn2_norm', 8 * l, 8 * l + 8), None, h, pe.last, m)
        s = squares_into(2) if l == 0 else None
        m = ffn('ffn2%d' % l, h, s)
    m_out = dma(t['out'], X[:, :, :], m)
    sp.after(m_out)
    fence()


def constants():
    f = np.float32
    c = np.zeros((128, 576), f)
    p = np.arange(128)
    c[:, 0:128] = np.eye(128)
    c[:, 128:256] = 1
    c[:, 256:384] = p[None, :]
    c[:, 384:512] = (p[:, None] % 32 == p[None, :])
    c[:, 512 + 7] = 1
    c[:, 528:544] = np.arange(16)[None, :]
    c[:, 512 + 32] = 1 / 256
    c[:, 512 + 41] = 1 / 128
    c[64:96, 512 + 50] = 1 / 32
    masks = np.zeros((128, 8, 128), f)
    for i in range(7):
        b = 1 << i
        masks[:, i, :] = ((p[:, None] // (2 * b) == p[None, :] // (2 * b)) & (p[:, None] // b != p[None, :] // b))
    spread = np.zeros((8, 8, 128), f)
    for i in range(8):
        spread[i, i, :] = 1
    spread16 = np.zeros((16, 8, 128), f)
    for i in range(8):
        spread16[2 * i, i, 0:64] = 1
        spread16[2 * i + 1, i, 64:96] = 1
    s, t = p[:, None].astype(np.float64), np.arange(256)[None, :].astype(np.float64)
    lg = np.log1p(-2.0 ** (-5.0 - np.arange(4)))
    full = np.stack([np.where(t >= s, np.exp(np.maximum(t - s, 0) * g), 0) * 128 ** -0.5 for g in lg], 1)
    decay = np.concatenate([full, full[:, :, 0:128]], 2).astype(f)
    causal = np.where(p[:, None] >= p[None, :], 0, -1e30)
    mask = np.concatenate([np.zeros((128, 128)), causal, causal], 1).astype(f)
    perms = np.zeros((128, 256), f)
    for i in range(64):
        perms[i + 64, i] = -1
        perms[i, i + 64] = 1
    for i in range(16):
        perms[80 + i, 128 + 64 + i] = -1
        perms[64 + i, 128 + 80 + i] = 1
    cols2 = np.zeros((128, 64), f)
    cols2[0:64, 14] = 1 / 64
    cols2[64:96, 15] = 1 / 32
    cols2[0:64, 39] = 1 / 64
    inv = lambda dim: (f(1) / (f(10000.0) ** (np.arange(0, dim, 2, dtype=f) / f(dim)))).astype(f)
    cols2[:, 48] = np.tile(inv(128), 2)
    cols2[64:96, 49] = np.tile(inv(32), 2)
    return dict(consts=c, masks=masks, spread=spread.reshape(8, 1024), spread16=spread16.reshape(16, 1024),
                decay=decay, mask=mask, perms=perms, cols2=cols2)


def pack(inputs):
    a = {k: np.asarray(v) for k, v in inputs.items()}
    out = constants()

    def granules(tl):
        n = tl.shape[0]
        return np.ascontiguousarray(tl.reshape(n // 2, 2, 128, 1024).transpose(0, 2, 1, 3))

    def columns(w):
        n = w.shape[1] // 128
        return w.reshape(8, 128, n, 128).transpose(2, 1, 0, 3).reshape(n, 128, 1024)

    def rows(w):
        return w.reshape(4, 2, 128, 512).transpose(0, 2, 1, 3).reshape(4, 128, 1024)

    def vec(v):
        return v.reshape(-1, 128).T

    out['ctx'] = np.ascontiguousarray(a['ctx'][0].T.reshape(8, 128, 256).transpose(1, 0, 2))
    out['x'] = np.ascontiguousarray(a['x'][0].T.reshape(8, 128, 256).transpose(1, 0, 2))
    pad = np.zeros((2, 32), np.float32)
    pad64 = np.zeros((2, 64), np.float32)
    names = dict(ffn1_norm='ffn1_norm_2', mix_norm='mix_norm_2', ffn2_norm='ffn2_norm_2', ret_norm='ret_head_norm_2',
                 q_lat='q_lat_norm_2', kv_lat='kv_lat_norm_2')
    heads = {'qn': np.concatenate([a['qn_nope_2'], a['qn_rope_2'], pad], 1),
             'kn': np.concatenate([a['kn_nope_2'], a['kn_rope_2'], pad], 1)}
    out['params'] = np.ascontiguousarray(np.concatenate(
        [vec(heads[n] if n in heads else a[names.get(n, n)]) for n, _ in PARAMS], 1))
    for l in range(2):
        out['w_mod%d' % l] = granules(a['w_mod'][l].reshape(4, 2, 128, 12, 512).transpose(3, 0, 2, 1, 4)
                                      .reshape(48, 128, 1024))
        w = a['w_in'][l]
        order = [512, 1024, 1536, 2048, 2560, 3584, 3072]
        out['w_in%d' % l] = granules(np.concatenate([rows(w[:, 0:512])] + [columns(w[:, o:o + 512]) for o in order]))
        out['w_out%d' % l] = granules(columns(a['w_out'][l]))
        out['peer_wq%d' % l] = granules(columns(a['peer_wq'][l]))
        out['peer_u%d' % l] = granules(a['peer_u'][l].reshape(128, 128, 8, 128).transpose(1, 3, 2, 0).reshape(128, 128, 1024))
        out['peer_v%d' % l] = granules(a['peer_v'][l].reshape(128, 128, 1024).transpose(1, 0, 2))
        w = a['w_in_2'][l]
        kr = np.zeros((1024, 128), np.float32)
        kr[:, 64:96] = w[:, 2432:2464]
        out['w_in2%d' % l] = granules(np.concatenate([
            columns(w[:, 2048:2432]), columns(kr), rows(w[:, 1024:1536]), columns(w[:, 512:1024]), columns(w[:, 0:512]),
            columns(w[:, 1536:2048])]))
        out['w_o2%d' % l] = granules(columns(a['w_o_2'][l]))
        for f in ('ffn1', 'ffn2'):
            g, u = columns(a[f + '_w_gate_2'][l]), columns(a[f + '_w_up_2'][l])
            d = a[f + '_w_down_2'][l].reshape(22, 128, 1024)
            seq = []
            for i in range(23):
                if i < 22:
                    seq += [g[i], u[i]]
                if i:
                    seq.append(d[i - 1])
            out['%s%d' % (f, l)] = granules(np.stack(seq))
    out['subkeys'] = np.ascontiguousarray(a['peer_subkeys'].transpose(0, 4, 1, 2, 3).reshape(2, 128, 16, 128))
    uq = np.zeros((2, 2, 128, 8, 128), np.float32)
    uq[..., 0:96] = a['w_uq_2'].reshape(2, 2, 128, 8, 96)
    out['w_uq'] = np.ascontiguousarray(uq.reshape(2, 2, 128, 2, 512).transpose(0, 2, 3, 1, 4).reshape(2, 128, 2, 1024))
    out['w_ukv'] = np.ascontiguousarray(a['w_ukv_2'].reshape(2, 128, 8, 2, 64).transpose(0, 1, 3, 2, 4).reshape(2, 128, 1024))
    out['positions'] = np.ascontiguousarray(a['positions_2'].reshape(1, 256))
    return out


def kernel(**inputs):
    import concourse.bacc as bacc
    from concourse.bass_utils import run_bass_kernel_spmd

    nc = bacc.Bacc("TRN2", target_bir_lowering=False, num_devices=1)
    arrays = pack(inputs)
    t = {k: nc.dram_tensor('in_' + k, v.shape, mybir.dt.from_np(v.dtype), kind="ExternalInput").ap()
         for k, v in arrays.items()}
    t['out'] = nc.dram_tensor('out', (128, 8, 256), F32, kind="ExternalOutput").ap()
    build(nc, t)
    r = run_bass_kernel_spmd(nc, [{'in_' + k: v for k, v in arrays.items()}], core_ids=[0])
    y = r.results[0]['out']
    return np.ascontiguousarray(y.transpose(1, 0, 2).reshape(1024, 256).T.reshape(1, 256, 1024))
```

```python
import numpy as np
import concourse.bass as bass
from concourse import mybir
from concourse.alu_op_type import AluOpType as ALU

F32 = mybir.dt.float32
F32R = mybir.dt.float32r
F16 = mybir.dt.float16
U8 = mybir.dt.uint8
U32 = mybir.dt.uint32
I32 = mybir.dt.int32
ACT = mybir.ActivationFunctionType
AX = mybir.AxisListType

EPS = 1e-6
F_FLOOR = 1e-20
LOWEST = -3.0e38

PARAMS = [('norm1_g', 16), ('norm2_g', 16), ('b_mod', 96), ('final_g', 8), ('conv_w', 24), ('lb_logits', 16),
          ('c', 8), ('c_ctx', 8), ('ffn1_norm', 16), ('mix_norm', 16), ('ffn2_norm', 16), ('ret_norm', 8),
          ('q_lat', 4), ('kv_lat', 2), ('qn', 2), ('kn', 2)]
PCOL, PN = {}, 0
for _n, _w in PARAMS:
    PCOL[_n] = PN
    PN += _w


MOD_IN = [4, 6, 10, 12, 16, 18, 22, 24]
MOD_PEER = [4 * n + 4 for n in range(12)]


class Lane:

    def __init__(self, nc, eng, name):
        self.nc, self.eng, self.name = nc, eng, name
        self.turn, self.n, self.seen = 0, 0, {}
        self.sem = nc.alloc_semaphore(name + '0')
        self.last = None

    def after(self, *marks):
        for m in marks:
            if m is None:
                continue
            if isinstance(m, list):
                self.after(*m)
                continue
            key, sem, value = m
            if self.seen.get(key, 0) < value:
                self.eng.wait_ge(sem, value)
                self.seen[key] = value
        return self.eng

    def mark(self, ins):
        if self.n == 16000:
            self.turn, self.n = self.turn + 1, 0
            self.sem = self.nc.alloc_semaphore('%s%d' % (self.name, self.turn))
        self.n += 1
        ins.then_inc(self.sem, 1)
        self.last = ('%s%d' % (self.name, self.turn), self.sem, self.n)
        return self.last


class Arena:

    def __init__(self, nc, tag, start, end):
        self.nc, self.tag, self.at, self.end = nc, tag, start, end

    def take(self, name, shape, dtype=F32):
        size = int(np.prod(shape[1:])) * mybir.dt.size(dtype)
        at = self.at
        self.at += (size + 31) // 32 * 32
        assert self.at <= self.end, (self.tag, name, self.at, self.end)
        return self.nc.alloc_sbuf_tensor_at('%s_%s' % (self.tag, name), list(shape), dtype, offset=at)


class Tile:
    def __init__(self, tag, granule, sub, raw):
        self.tag, self.granule, self.sub, self.raw = tag, granule, sub, raw
        self.hi = self.lo = None
        self.ready = []


def schedule():
    def run(name, a, b):
        return [(name, g, 2, False) for g in range(a, b)]

    def mods(layer, a, b):
        return [('w_mod%d' % layer, g, 2, True) for g in range(a, b)]

    def mixed(main, side, at):
        out, side = [], list(side)
        for n, g in enumerate(main):
            out.append(g)
            if side and 2 * n + 2 in at:
                out.append(side.pop(0))
        return out

    def peer(layer, side):
        u, v = 'peer_u%d' % layer, 'peer_v%d' % layer
        return (run('peer_wq%d' % layer, 0, 8) + mixed(run(u, 0, 32), side, MOD_PEER) + run(u, 32, 64)
                + run(v, 0, 32) + run(v, 32, 64))

    order = mods(0, 0, 8)
    order += mixed(run('w_in0', 0, 16), mods(0, 8, 16), MOD_IN) + mixed(run('w_in0', 0, 16), mods(0, 16, 24), MOD_IN)
    order += run('w_out0', 0, 4) + run('w_out0', 0, 4)
    order += peer(0, mods(1, 0, 12)) + peer(0, mods(1, 12, 24))
    order += run('w_in1', 0, 6) + run('w_in1', 0, 16) + run('w_out1', 0, 4) + peer(1, [])
    for l in range(2):
        order += run('ffn1%d' % l, 0, 33) + run('w_in2%d' % l, 0, 10) + run('w_o2%d' % l, 0, 4)
        order += run('ffn2%d' % l, 0, 33)
    return order


def build(nc, t):
    pe = Lane(nc, nc.tensor, 'pe')
    act = Lane(nc, nc.scalar, 'act')
    dve = Lane(nc, nc.vector, 'dve')
    pool = Lane(nc, nc.gpsimd, 'pool')
    sp = Lane(nc, nc.sync, 'sp')
    engines = [pe, act, dve, pool]

    KB = 1024
    CONST0 = 16512
    RAW0 = CONST0 + 4960
    HL0 = RAW0 + 24 * KB
    H0 = HL0 + 24 * KB
    G0 = H0 + 16 * KB
    BIG0 = G0 + 11 * KB
    BIG1 = BIG0 + 128 * KB
    R1 = BIG0 + 64 * KB
    NG, NH = 3, 3

    ca = Arena(nc, 'const', CONST0, RAW0)
    ident = ca.take('ident', [128, 128])
    ones = ca.take('ones', [128, 128])
    onehot = ca.take('onehot', [128, 128])
    iota16 = ca.take('iota16', [128, 128], F16)
    par = ca.take('par', [128, PN])
    mod = ca.take('mod', [128, 2, 48, 2])
    gain1 = ca.take('gain1', [128, 2, 2, 8])
    gain2 = ca.take('gain2', [128, 2, 2, 8])
    lbv = ca.take('lbv', [128, 2, 8])
    lbc = ca.take('lbc', [128, 2, 8])
    epsc = ca.take('epsc', [128, 4])
    cols = ca.take('cols', [128, 64])
    gate_s = ca.take('gate_s', [128, 8])

    raw = nc.alloc_sbuf_tensor_at('raw', [128, NG, 2, 1024], F32, offset=RAW0)
    whi = nc.alloc_sbuf_tensor_at('whi', [128, NH, 1024], F32R, offset=HL0)
    wlo = nc.alloc_sbuf_tensor_at('wlo', [128, NH, 1024], F32R, offset=HL0 + 4 * KB * NH)
    ha = Arena(nc, 'h', H0, G0)
    h_hi = ha.take('hi', [128, 8, 256], F32R)
    h_lo = ha.take('lo', [128, 8, 256], F32R)
    X = nc.alloc_sbuf_tensor_at('X', [128, 8, 256], F32, offset=BIG0)
    na = Arena(nc, 'norm', BIG0 + 8 * KB, BIG0 + 16 * KB)
    nsq = na.take('sq', [128, 4, 256])
    nrt = na.take('rt', [128, 256])
    nrs = na.take('rs', [128, 256])
    ny = na.take('y', [128, 2, 256])

    bank = [nc.alloc_psum_tensor('bank%d' % b, [128, 512], F32) for b in range(8)]
    free = [[] for _ in range(8)]

    count = [0]

    def dma(dst, src, *deps):
        s = nc.alloc_semaphore('dma%d' % count[0])
        count[0] += 1
        sp.after(*deps).dma_start(dst, src).then_inc(s, 16)
        return ('dma%d' % (count[0] - 1), s, 16)

    def marks():
        return [e.last for e in engines]

    def fence():
        now = marks()
        for e in engines:
            e.after(now)

    order = schedule()
    tiles = []
    for g, (name, index, k, as_is) in enumerate(order):
        for sub in range(k):
            tiles.append(Tile(name, g, sub, as_is))
    split_tiles = [x for x in tiles if not x.raw]
    slot_sem = [nc.alloc_semaphore('raw%d' % s) for s in range(NG)]
    state = dict(pos=0, fetched=0, split=0, sidx=0, share=0, lot=0)
    landed = {}
    freed = {g: [] for g in range(len(order))}
    used_up = {}
    spent = {}

    def fetch():
        while state['fetched'] < len(order):
            g = state['fetched']
            if g >= NG and used_up.get(g - NG, 0) < order[g - NG][2]:
                return
            name, index, k, as_is = order[g]
            deps = freed[g - NG] if g >= NG else []
            sp.after(*deps).dma_start(raw[:, g % NG, 0:k, :], t[name][index]).then_inc(slot_sem[g % NG], 16)
            landed[g] = ('raw%d' % (g % NG), slot_sem[g % NG], 16 * (g // NG + 1))
            state['fetched'] += 1

    def give_back(g, *marks):
        freed[g].extend(marks)
        used_up[g] = used_up.get(g, 0) + 1
        fetch()

    def split():
        j = state['split']
        x = split_tiles[j]
        fetch()
        src = raw[:, x.granule % NG, x.sub, :]
        s = j % NH
        gone = spent[j - NH] if j >= NH else None
        x.hi, x.lo = whi[:, s, :], wlo[:, s, :]
        m = act.mark(act.after(landed[x.granule], gone).activation(x.hi, src, ACT.Copy))
        state['lot'] += state['share']
        lane = dve
        if state['lot'] >= 16:
            state['lot'] -= 16
            lane = pool
        k = lane.mark(lane.after(landed[x.granule], m, gone).tensor_tensor(x.lo, src, x.hi.bitcast(F32), ALU.subtract))
        x.ready = [m, k]
        state['split'] += 1
        give_back(x.granule, m, k)

    def take(tag, ahead=NH):
        x = tiles[state['pos']]
        assert x.tag == tag, (x.tag, tag, state['pos'])
        state['pos'] += 1
        if x.raw:
            fetch()
            x.hi = raw[:, x.granule % NG, x.sub, :]
            x.ready = [landed[x.granule]]
            return x
        x.at = state['sidx']
        state['sidx'] += 1
        while state['split'] < min(x.at + ahead, len(split_tiles)):
            split()
        return x

    def ahead():
        if state['split'] == state['sidx']:
            split()

    def done(x, m):
        if x.raw:
            give_back(x.granule, m)
        else:
            spent[x.at] = m

    def mm(out, lhsT, rhs, start=True, stop=True, **kw):
        return nc.tensor.matmul(out, lhsT, rhs, start=start, stop=stop, skip_group_check=True, **kw)

    class Split:

        def __init__(self, hi, lo, n=8):
            self.hi, self.lo, self.m, self.m_hi = hi, lo, [None] * 8, [None] * 8
            self.his, self.los = [hi[:, b, :] for b in range(n)], [lo[:, b, :] for b in range(n)]

    def dense(tag, out, src, first, ends=None):
        x = take(tag)
        pe.after(first, x.ready)
        for b in range(8):
            w, v = x.hi[:, b * 128:(b + 1) * 128], x.lo[:, b * 128:(b + 1) * 128]
            pe.after(src.m[b])
            mm(out, w, src.hi[:, b, :], start=b == 0, stop=False)
            mm(out, w, src.lo[:, b, :], start=False, stop=False)
            ins = mm(out, v, src.hi[:, b, :], start=False, stop=b == 7)
            if ends is not None and b % 2:
                ends.append(pe.mark(ins))
        m = ends[-1] if ends else pe.mark(ins)
        done(x, m)
        return m

    def dense_pair(tag, out, src, first):
        pe.after(first)
        two = [take(tag), take(tag, NH - 1)]
        for b in range(8):
            c = slice(b * 128, (b + 1) * 128)
            pe.after(src.m_hi[b])
            for n, x in enumerate(two):
                pe.after(x.ready)
                mm(out[:, n, :], x.hi[:, c], src.hi[:, b, :], start=b == 0 and n == 0, stop=False)
                mm(out[:, n, :], x.lo[:, c], src.hi[:, b, :], start=False, stop=False)
            pe.after(src.m[b])
            for n, x in enumerate(two):
                ins = mm(out[:, n, :], x.hi[:, c], src.lo[:, b, :], start=False, stop=b == 7)
        m = pe.mark(ins)
        for x in two:
            done(x, m)
        return m

    def dense_rows(tag, outs, src, first):
        res = []
        for j in range(4):
            x = take(tag)
            pe.after(first, x.ready)
            for k in range(2):
                b = 2 * j + k
                pe.after(src.m[b])
                w, v = x.hi[:, k * 512:(k + 1) * 512], x.lo[:, k * 512:(k + 1) * 512]
                for tt in range(2):
                    c = slice(tt * 128, (tt + 1) * 128)
                    mm(outs[tt], src.hi[:, b, c], w, start=b == 0, stop=False)
                    mm(outs[tt], src.lo[:, b, c], w, start=False, stop=False)
                    ins = mm(outs[tt], src.hi[:, b, c], v, start=False, stop=b == 7)
            m = pe.mark(ins)
            done(x, m)
            res.append(m)
            yield res

    m_par = dma(par[:, :], t['params'])
    m_ctx = dma(X[:, :, :], t['ctx'])
    cm = [dma(ident[:, :], t['consts'][:, 0:128]), dma(ones[:, :], t['consts'][:, 128:256]),
          dma(onehot[:, :], t['consts'][:, 384:512]), dma(cols[:, :], t['consts'][:, 512:576])]
    iof = ny[:, 0, 0:128]
    im = dma(iof, t['consts'][:, 256:384])
    fetch()
    m_eps = [dve.mark(nc.vector.memset(epsc[:, 0:1], EPS)), dve.mark(nc.vector.memset(epsc[:, 1:2], float(np.pi / 2)))]
    for e in (act, dve):
        e.after(m_par, m_eps)

    def P(name, a, b=None):
        i = PCOL[name] + a
        return par[:, i:i + 1] if b is None else par[:, i:PCOL[name] + b]

    sca = Arena(nc, 'cond', G0 + 2 * KB, G0 + 6 * KB)
    cond = sca.take('cond', [128, 8, 64])
    mev = sca.take('mev', [128, 512])
    mod_m = {}

    def conditions(before):
        m0 = dve.mark(dve.after(before).memset(cond[:, :, :], 0.0))
        m1 = act.mark(act.after(m0).activation(cond[:, :, 30], P('c', 0, 8), ACT.Silu))
        m2 = act.mark(act.after(m0).activation(cond[:, :, 31], P('c_ctx', 0, 8), ACT.Silu))
        pe.after(m0, m1, m2)

    def modulation(layer, groups, b1, b2):
        groups = list(groups)
        n = len(groups)
        first = free[b1]
        for i, g in enumerate(groups):
            for j in range(4):
                x = take('w_mod%d' % layer)
                pe.after(first, x.ready)
                for k in range(2):
                    b = 2 * j + k
                    q = b % 4
                    ins = mm(bank[b1][32 * q:32 * q + 32, :], cond[:, b, 30 - 2 * i:62 - 2 * i],
                             x.hi[:, k * 512:(k + 1) * 512], start=i == 0 and b < 4, stop=i == n - 1 and b >= 4,
                             tile_position=(0, 32 * q))
                m = pe.mark(ins)
                done(x, m)
                if j == 1:
                    yield
            if i < n - 1:
                yield
        m = act.mark(act.after(m).activation(mev[:, :], bank[b1][:, :], ACT.Copy))
        free[b1] = [m]
        yield
        pe.after(m, free[b2])
        for b in range(4):
            ins = mm(bank[b2][:, b * 128:(b + 1) * 128], mev[:, b * 128:(b + 1) * 128], onehot[:, :])
        mp = pe.mark(ins)
        for i, g in enumerate(groups):
            turned = bank[b2][:, :].rearrange('p (b j) -> p b j', b=4)[:, :, 2 * i:2 * i + 2]
            bias = P('b_mod', layer * 48 + g * 4, layer * 48 + g * 4 + 4).unsqueeze(2).to_broadcast([128, 4, 2])
            m = dve.mark(dve.after(mp).tensor_tensor(mod[:, layer, g * 4:g * 4 + 4, :], turned, bias, ALU.add))
            free[b2] = [m]
            mod_m[layer, g] = m
            for dst, norm, base in ((gain1, 'norm1_g', 2), (gain2, 'norm2_g', 8)):
                if base <= g < base + 2:
                    h = g - base
                    for who in range(2):
                        mod_m[layer, g, who] = dve.mark(dve.after(m).scalar_tensor_tensor(
                            dst[:, layer, who, 4 * h:4 * h + 4], mod[:, layer, g * 4:g * 4 + 4, who], 1.0,
                            P(norm, layer * 8 + 4 * h, layer * 8 + 4 * h + 4), ALU.add, ALU.mult))

    def bounds():
        m_iota = dve.mark(dve.after(im).tensor_copy(iota16[:, :], iof))
        for e in engines:
            e.after(cm, m_iota)
        lm = ny[:, 1, 0:8]
        le = ny[:, 1, 16:32].rearrange('p (l e) -> p l e', l=2)
        ls = ny[:, 1, 32:40]
        lg = P('lb_logits', 0, 16).rearrange('p (l e) -> p l e', l=2)
        m = dve.mark(nc.vector.tensor_tensor(lm, lg[:, 0, :], lg[:, 1, :], ALU.max))
        m = dve.mark(dve.after(m).tensor_tensor(le, lg, lm.unsqueeze(1).to_broadcast([128, 2, 8]), ALU.subtract))
        m = act.mark(act.after(m).activation(le, le, ACT.Exp))
        m = dve.mark(dve.after(m).tensor_tensor(ls, le[:, 0, :], le[:, 1, :], ALU.add))
        m = dve.mark(dve.after(m).reciprocal(ls, ls))
        m = dve.mark(dve.after(m).tensor_tensor(le, le, ls.unsqueeze(1).to_broadcast([128, 2, 8]), ALU.mult))
        m1 = dve.mark(dve.after(m).tensor_tensor(lbv[:, 0, :], le[:, 0, :], le[:, 0, :], ALU.subtract))
        m = dve.mark(dve.after(m).tensor_tensor(ls, le[:, 0, :], le[:, 1, :], ALU.add))
        m = dve.mark(dve.after(m).tensor_tensor(lbv[:, 1, :], ls, le[:, 0, :], ALU.subtract))
        m_lb = dve.mark(dve.after(m, m1).tensor_scalar(lbc[:, :, :], lbv[:, :, :], -1.0, 1.0, ALU.mult, ALU.add))
        for e in (act, dve, pool):
            e.after(m_lb)

    def M(layer, part, who):
        return mod[:, layer, part * 8:part * 8 + 8, who]

    class Squares:
        pass

    ys = [ny[:, 0, :], ny[:, 1, :], nsq[:, 2, :], nsq[:, 3, :]]
    yfree = [None] * 4

    def squares_into(b):
        s = Squares()
        s.bank, s.squared, s.added, s.root = b, [], [], None
        return s

    def square(s, x, m):
        k = len(s.squared)
        if k >= 4:
            act.after(s.added[k - 4])
        else:
            act.after(yfree[k] if k >= 2 else None)
        s.squared.append(act.mark(act.after(m).activation(nsq[:, k % 4, :], x, ACT.Square)))

    def add_square(s):
        k = len(s.added)
        if k == 0:
            pe.after(free[s.bank])
        pe.after(s.squared[k])
        s.added.append(pe.mark(mm(bank[s.bank][:, 0:256], ones[:, :], nsq[:, k % 4, :], start=k == 0, stop=k == 7)))

    def one_over_rms(s):
        while len(s.added) < 8:
            add_square(s)
        m = act.mark(act.after(s.added[7]).activation(
            nrt[:, :], bank[s.bank][:, 0:256], ACT.Sqrt, bias=epsc[:, 0:1], scale=1.0 / 1024))
        free[s.bank] = [m]
        s.root = dve.mark(dve.after(m).reciprocal(nrs[:, :], nrt[:, :]))
        return s.root

    def table(f, m):
        act.mark(act.after(m, act.last).activation(epsc[:, 2:3], epsc[:, 0:1], f))

    def norm(x, s, gain, shift, dst, dst_free, x_m=None):
        finish(norm_steps(x, s, gain, shift, dst, dst_free, x_m))
        return dst.m[6] + dst.m[7]

    def norm_steps(x, s, gain, shift, dst, dst_free, x_m=None):
        mr = s.root or one_over_rms(s)
        hi = [None] * 8
        for i in range(10):
            if i < 8:
                b, k = i, i % 4
                y = ys[k]
                m = dve.mark(dve.after(mr, yfree[k], x_m).scalar_tensor_tensor(
                    y, x[:, b, :], gain[:, b:b + 1], nrs[:, :], ALU.mult, ALU.mult))
                if shift is None:
                    m1 = act.mark(act.after(m, dst_free).activation(dst.hi[:, b, :], y, ACT.Copy))
                elif b % 2:
                    m = act.mark(act.after(m).activation(y, y, ACT.Identity, bias=shift[:, b:b + 1]))
                    m1 = act.mark(act.after(m, dst_free).activation(dst.hi[:, b, :], y, ACT.Copy))
                else:
                    m1 = act.mark(act.after(m, dst_free).activation(dst.hi[:, b, :], y, ACT.Identity,
                                                                   bias=shift[:, b:b + 1]))
                hi[b] = dst.m_hi[b] = [m, m1]
            if i >= 2:
                b, k = i - 2, (i - 2) % 4
                lane = pool if b % 2 else dve
                if shift is None or b % 2:
                    m2 = lane.mark(lane.after(hi[b], dst_free).tensor_tensor(
                        dst.lo[:, b, :], ys[k], dst.hi[:, b, :].bitcast(F32), ALU.subtract))
                else:
                    m2 = dve.mark(dve.after(hi[b], dst_free).scalar_tensor_tensor(
                        dst.lo[:, b, :], ys[k], shift[:, b:b + 1], dst.hi[:, b, :].bitcast(F32), ALU.add, ALU.subtract))
                yfree[k] = [hi[b][1], m2]
                dst.m[b] = hi[b] + [m2]
            yield

    def run(main, *side):
        for _ in main:
            for s in side:
                next(s, None)

    def together(gens):
        gens = list(gens)
        while gens:
            gens = [g for g in gens if next(g, gens) is not gens]

    def timed(tiles_, gen):
        for n in range(1, tiles_[-1] + 4):
            if n in tiles_ or n == tiles_[-1] + 3:
                next(gen, None)
            yield

    def finish(gen):
        for _ in gen:
            pass

    class Mixer:
        pass

    def mixers(layer):
        a = Arena(nc, 'mix%d' % layer, BIG0 + 16 * KB, BIG1)
        s = Mixer()
        s.conv_free = None
        s.cg, s.u, s.cv = (a.take(k, [128, 4, 256]) for k in ('cg', 'u', 'cv'))
        s.KC, s.QC = a.take('KC', [128, 1024]), a.take('QC', [128, 1024])
        s.o = a.take('o', [128, 4, 256])
        hi, lo = a.take('hi', [128, 8, 256], F32R), a.take('lo', [128, 8, 256], F32R)
        s.att = a.take('att', [128, 2, 4, 256])
        pair = []
        for n in range(2):
            m = Mixer()
            m.shared = s
            m.V = a.take('V%d' % n, [128, 2, 512])
            m.qP, m.qS, m.kX, m.kY, m.ff, m.fb, m.g = (a.take('%s%d' % (k, n), [128, 4, 256])
                                                      for k in ('qP', 'qS', 'kX', 'kY', 'ff', 'fb', 'g'))
            m.h, m.mix = (Split(hi, lo), Split(hi, lo)) if n else (Split(h_hi, h_lo), Split(h_hi, h_lo))
            m.ready, m.finished, m.m_in, m.out = False, False, None, None
            pair.append(m)
        b = Arena(nc, 'mixc%d' % layer, G0, G0 + 2 * KB)
        s.spread = b.take('spread', [8, 512])
        b = Arena(nc, 'mixs%d' % layer, G0 + 6 * KB, G0 + 11 * KB)
        s.S = b.take('S', [128, 2, 4, 128])
        s.masks = b.take('masks', [128, 256], U32)
        return pair

    def mixer_constants(s, deps):
        s.cm = [dma(s.spread[:, :], t['spread'][:, 0:512], deps), dma(s.masks[:, :], t['masks'], deps)]

    def pairs(bk):
        return bk[:, :].rearrange('p (a b) -> p a b', a=2)

    def win(M_, layer, latent, only_state=False):
        s, h, tag = M_.shared, M_.h, 'w_in%d' % layer
        res = None
        for res in dense_rows(tag, [bank[2][:, :], bank[3][:, :]], h, free[2] + free[3]):
            if len(res) < 4:
                yield
        M_.mV = []
        for tt in range(2):
            m = act.mark(act.after(res).activation(M_.V[:, tt, :], bank[2 + tt][:, :], ACT.Copy))
            free[2 + tt] = [m]
            M_.mV.append(m)
        yield

        turn = [0]

        def two():
            b = turn[0] % 2
            turn[0] += 1
            first = free[b]
            m = None
            for n in range(2):
                m = dense(tag, pairs(bank[b])[:, n, :], h, first)
                yield b, m if n else None

        M_.mk = [[], []]
        M_.mf = [[], []]
        for d, (f, k) in enumerate(((M_.ff, M_.kX), (M_.fb, M_.kY))):
            for j in range(2):
                for b, m in two():
                    yield
                c = slice(2 * j, 2 * j + 2)
                m1 = act.mark(act.after(m).activation(f[:, c, :], pairs(bank[b]), ACT.Sigmoid))
                m2 = act.mark(act.after(m).activation(k[:, c, :], pairs(bank[b]), ACT.Sigmoid, scale=-1.0))
                free[b] = [m1, m2]
                for n in range(2):
                    e = 2 * j + n
                    lb, lc = lbv[:, layer, 4 * d + e:4 * d + e + 1], lbc[:, layer, 4 * d + e:4 * d + e + 1]
                    m = dve.mark(dve.after(m1).tensor_scalar(f[:, e, :], f[:, e, :], lc, lb, ALU.mult, ALU.add))
                    M_.mf[d].append(dve.mark(dve.after(m).tensor_scalar(f[:, e, :], f[:, e, :], F_FLOOR, None, ALU.max)))
                    M_.mk[d].append(dve.mark(dve.after(m2).tensor_scalar(k[:, e, :], k[:, e, :], lc, None, ALU.mult)))
        M_.mk, M_.mf = M_.mk[0] + M_.mk[1], M_.mf[0] + M_.mf[1]
        if only_state:
            M_.ready = True
            return
        M_.mq, M_.mg = [], []
        for j in range(2):
            for b, m in two():
                yield
            m = act.mark(act.after(m).activation(M_.qP[:, 2 * j:2 * j + 2, :], pairs(bank[b]), ACT.Copy))
            free[b] = [m]
            M_.mq.append(m)
        M_.ready = True
        for j in range(2):
            for b, m in two():
                yield
            m = act.mark(act.after(m).activation(M_.g[:, 2 * j:2 * j + 2, :], pairs(bank[b]), ACT.Silu))
            free[b] = [m]
            M_.mg.append(m)
        mc, mu, mv = [], [], [None] * 4
        for j in range(2):
            for b, m in two():
                yield
            m = act.mark(act.after(m, s.conv_free).activation(s.cg[:, 2 * j:2 * j + 2, :], pairs(bank[b]), ACT.Copy))
            free[b] = [m]
            mc.append(m)
        for j in range(2):
            for b, m in two():
                yield
            c = slice(2 * j, 2 * j + 2)
            m = dve.mark(dve.after(m, mc[j]).tensor_tensor(s.u[:, c, :], pairs(bank[b]), s.cg[:, c, :], ALU.mult))
            free[b] = [m]
            mu.append(m)
        for e in range(4):
            w = [P('conv_w', layer * 12 + 4 * i + e) for i in range(3)]
            u, v = s.u[:, e, :], s.cv[:, e, :]
            m = act.mark(act.after(mu[e // 2]).activation(v, u, ACT.Copy, scale=w[1]))
            if latent and e < 2:
                u2, v2 = u.rearrange('p (r c) -> p r c', c=64), v.rearrange('p (r c) -> p r c', c=64)
                steps = [(v2[:, :, 1:64], u2[:, :, 0:63]), (v2[:, :, 0:63], u2[:, :, 1:64])]
            else:
                k = 64 if latent else 1
                steps = [(v[:, k:256], u[:, 0:256 - k]), (v[:, 0:256 - k], u[:, k:256])]
            for (vo, ui), wi in zip(steps, (w[0], w[2])):
                m = dve.mark(dve.after(m, mu[e // 2]).scalar_tensor_tensor(vo, ui, wi, vo, ALU.mult, ALU.add))
            mv[e] = m
        mb = []
        for j in range(2):
            for b, m in two():
                yield
            c = slice(2 * j, 2 * j + 2)
            m = dve.mark(dve.after(m, mv[2 * j:2 * j + 2]).tensor_tensor(s.cv[:, c, :], pairs(bank[b]), s.cv[:, c, :],
                                                                     ALU.mult))
            free[b] = [m]
            mb.append(m)
        M_.m_in = pe.last
        for j in range(2):
            put(M_.mix, 4 + 2 * j, s.cv[:, 2 * j:2 * j + 2, :], mb[j], M_.m_in)
        s.conv_free = M_.mix.m[4] + M_.mix.m[6]

    def put(dst, b, src, m, wait):
        c = slice(b, b + 2)
        m1 = act.mark(act.after(m, wait).activation(dst.hi[:, c, :], src, ACT.Copy))
        m2 = dve.mark(dve.after(m, m1, wait).tensor_tensor(dst.lo[:, c, :], src, dst.hi[:, c, :].bitcast(F32), ALU.subtract))
        dst.m[b] = dst.m[b + 1] = [m1, m2]

    def level_view(a, B):
        v = a.rearrange('p (n w) -> p n w', w=2 * B)
        return v[:, :, 0:B], v[:, :, B:2 * B]

    def flat(a):
        return a[:, :, :].rearrange('p h t -> p (h t)')

    def scan(M_, need_q, before=None):
        s = M_.shared
        for e in engines:
            e.after(before)
        qP, qS, kX, kY, ff, fb = (flat(x) for x in (M_.qP, M_.qS, M_.kX, M_.kY, M_.ff, M_.fb))
        mk, mf = M_.mk, M_.mf
        if need_q:
            kd = dve.mark(dve.after(mk).tensor_tensor(s.KC[:, :], kX, kY, ALU.add))
            m1 = dve.mark(dve.after(mf, M_.mq).tensor_tensor(qS, qP, fb, ALU.mult))
            yield
            pe.after(kd, M_.mq, free[6], free[7])
            for tt in range(2):
                for e in range(4):
                    c = slice(e * 256 + tt * 128, e * 256 + tt * 128 + 128)
                    ins = mm(bank[6 + tt][:, e * 128:(e + 1) * 128], s.KC[:, c], qP[:, c])
            mp = pe.mark(ins)
            m_att = []
            for tt in range(2):
                m = dve.mark(dve.after(mp).tensor_tensor(
                    s.att[:, tt, :, tt * 128:tt * 128 + 128], bank[6 + tt][:, :].rearrange('p (h t) -> p h t', h=4),
                    ident[:, :].unsqueeze(1).to_broadcast([128, 4, 128]), ALU.mult))
                free[6 + tt] = [m]
                m_att.append(m)
            m2 = dve.mark(dve.after(mp, mf).tensor_tensor(qP, qP, ff, ALU.mult))
        B, lev = 1, 0
        kc_free = mp if need_q else None
        mx, my, ms, mp_ = mk, mk, m1 if need_q else None, m2 if need_q else None
        Tf, Tb, mt = ff, fb, mf
        spare = flat(s.o)
        while B <= 64:
            n = 1024 // (2 * B)
            p0, p1 = level_view(qP, B)
            s0, s1 = level_view(qS, B)
            x0, x1 = level_view(kX, B)
            y0, y1 = level_view(kY, B)
            Tf2, Tb2 = (Tf.rearrange('p (n w) -> p n w', w=2), Tb.rearrange('p (n w) -> p n w', w=2))
            f0, f1, b0, b1 = (T[:, :, i:i + 1].to_broadcast([128, n, B]) for T in (Tf2, Tb2) for i in range(2))
            to = (spare[:, 0:n], spare[:, 512:512 + n]) if lev % 2 == 0 else (ff[:, 0:n], fb[:, 0:n])
            mt2 = [pool.mark(pool.after(mt, mx, my, ms, mp_).tensor_tensor(
                o.unsqueeze(2), T[:, :, 0:1], T[:, :, 1:2], ALU.mult)) for o, T in zip(to, (Tf2, Tb2))]
            if need_q:
                c0, c1 = level_view(s.KC[:, :], B)
                d0, d1 = level_view(s.QC[:, :], B)
                cx, cy, cs, cp = (act.mark(act.after(m, kc_free).activation(o, i, ACT.Copy))
                                  for o, i, m in ((c0, x0, mx), (c1, y1, my), (d0, s0, ms), (d1, p1, mp_)))
                copied = [cx, cy, cs, cp]
            else:
                cx = cy = copied = None
            mx = dve.mark(dve.after(mt, mx, cx).tensor_tensor(x0, x0, f1, ALU.mult))
            my = dve.mark(dve.after(mt, my, cy).tensor_tensor(y1, y1, b0, ALU.mult))
            if need_q:
                ms = dve.mark(dve.after(ms, cs).tensor_tensor(s0, s0, b1, ALU.mult))
                mp_ = dve.mark(dve.after(mp_, cp).tensor_tensor(p1, p1, f0, ALU.mult))
            Tf, Tb, mt = to[0], to[1], mt2
            yield
            if need_q:
                pe.after(copied, free[6], free[7])
                for tt in range(2):
                    for e in range(4):
                        c = slice(e * 256 + tt * 128, e * 256 + tt * 128 + 128)
                        ins = mm(bank[6 + tt][:, e * 128:(e + 1) * 128], s.KC[:, c], s.QC[:, c])
                kc_free = pe.mark(ins)
                for tt in range(2):
                    m_att[tt] = dve.mark(dve.after(kc_free, m_att[tt]).copy_predicated(
                        s.att[:, tt, :, tt * 128:tt * 128 + 128],
                        s.masks[:, :].bitcast(U8)[:, lev * 128:(lev + 1) * 128].unsqueeze(1).to_broadcast([128, 4, 128]),
                        bank[6 + tt][:, :].rearrange('p (h t) -> p h t', h=4)))
                    free[6 + tt] = [m_att[tt]]
                yield
            B, lev = 2 * B, lev + 1
        mu = [mx, my, ms, mp_, mt]
        if need_q:
            pe.after(mu, free[6], free[7])
            for e in range(4):
                a, b = slice(e * 256, e * 256 + 128), slice(e * 256 + 128, e * 256 + 256)
                mm(bank[6][:, e * 128:(e + 1) * 128], kX[:, a], qP[:, b])
                ins = mm(bank[7][:, e * 128:(e + 1) * 128], kY[:, b], qS[:, a])
            mp = pe.mark(ins)
            mo = []
            for tt in range(2):
                c = slice(128 - tt * 128, 256 - tt * 128)
                m = act.mark(act.after(mp).activation(s.att[:, tt, :, c],
                                                            bank[6 + tt][:, :].rearrange('p (h t) -> p h t', h=4), ACT.Copy))
                free[6 + tt] = [m]
                mo.append(m)
            M_.m_att = m_att + mo
        v = lambda a: a.rearrange('p (h t) -> p h t', h=4)
        wide = lambda T, i: T.rearrange('p (h w) -> p h w', h=4)[:, :, i:i + 1].to_broadcast([128, 4, 128])
        M_.m_full = [
            dve.mark(dve.after(mu, mp if need_q else None).tensor_tensor(v(kX)[:, :, 0:128], v(kX)[:, :, 0:128], wide(Tf, 1), ALU.mult)),
            dve.mark(dve.after(mu).tensor_tensor(v(kY)[:, :, 128:256], v(kY)[:, :, 128:256], wide(Tb, 0), ALU.mult))]
        if need_q:
            M_.m_full += [
                dve.mark(dve.after(mu).tensor_tensor(v(qS)[:, :, 0:128], v(qS)[:, :, 0:128], wide(Tb, 1), ALU.mult)),
                dve.mark(dve.after(mu).tensor_tensor(v(qP)[:, :, 128:256], v(qP)[:, :, 128:256], wide(Tf, 0), ALU.mult))]
        M_.m_full += mu
        yield

    def states(M_, before=None):
        s = M_.shared
        for e in engines:
            e.after(before)
        ms = []
        kT = [s.KC, s.QC]
        for d, k in enumerate((M_.kX, M_.kY)):
            mt = []
            for tt in range(2):
                pe.after(M_.m_full, free[6 + tt])
                for e in range(4):
                    ins = nc.tensor.transpose(bank[6 + tt][:, e * 128:(e + 1) * 128], k[:, e, tt * 128:(tt + 1) * 128],
                                              ident[:, :])
                mp = pe.mark(ins)
                m = act.mark(act.after(mp).activation(kT[d][:, tt * 512:(tt + 1) * 512], bank[6 + tt][:, :], ACT.Copy))
                free[6 + tt] = [m]
                mt.append(m)
            yield
            pe.after(mt, M_.mV, free[4 + d])
            for e in range(4):
                for tt in range(2):
                    ins = mm(bank[4 + d][:, e * 128:(e + 1) * 128], kT[d][:, tt * 512 + e * 128:tt * 512 + (e + 1) * 128],
                             M_.V[:, tt, e * 128:(e + 1) * 128], start=tt == 0, stop=tt == 1)
            mp = pe.mark(ins)
            m = dve.mark(dve.after(mp).tensor_copy(s.S[:, d, :, :], bank[4 + d][:, :].rearrange('p (h v) -> p h v', h=4)))
            free[4 + d] = [m]
            ms.append(m)
            yield
        s.mS = ms
        for e in engines:
            e.after(ms, mp)

    def head_norm(o, mo, row_bank, wide_banks, gains, gate, mg, sq, rows, mix, spread, mix_free):
        rt, rr = rows
        pe.after(free[row_bank])
        for e in range(4):
            m = act.mark(act.after(mo[e // 2]).activation(sq[:, e, :], o[:, e, :], ACT.Square))
            pe.after(m)
            ins = mm(bank[row_bank][0:8, 0:256], cols[:, 7 - e:15 - e], sq[:, e, :], start=e == 0, stop=e == 3)
        mp = pe.mark(ins)
        m = act.mark(act.after(mp).activation(rt, bank[row_bank][0:8, 0:256], ACT.Sqrt, bias=epsc[0:8, 0:1], scale=1.0 / 128))
        free[row_bank] = [m]
        m = dve.mark(dve.after(m).reciprocal(rr, rt))
        yield
        for j in range(2):
            b = wide_banks[j]
            pe.after(m, free[b])
            for n in range(2):
                e = 2 * j + n
                ins = mm(pairs(bank[b])[:, n, :], spread[:, e * 128:(e + 1) * 128], rr)
            mp = pe.mark(ins)
            c = slice(2 * j, 2 * j + 2)
            if gains is None:
                ma = dve.mark(dve.after(mp, mo[j]).tensor_tensor(o[:, c, :], o[:, c, :], pairs(bank[b]), ALU.mult))
            else:
                for n in range(2):
                    e = 2 * j + n
                    ma = dve.mark(dve.after(mp, mo[j]).scalar_tensor_tensor(
                        o[:, e, :], o[:, e, :], gains[e], pairs(bank[b])[:, n, :], ALU.mult, ALU.mult))
            free[b] = [ma]
            while len(mg) <= j:
                yield
            ma = dve.mark(dve.after(ma, mg).tensor_tensor(o[:, c, :], o[:, c, :], gate[:, c, :], ALU.mult))
            put(mix, 2 * j, o[:, c, :], ma, mix_free())
            yield

    def mix_out(M_, state):
        s = M_.shared
        mo = []
        for j in range(2):
            b = 4 + j
            pe.after(M_.m_att, M_.mV, M_.m_full if state else None, s.mS if state else None, free[b])
            for n in range(2):
                e = 2 * j + n
                c = slice(e * 128, (e + 1) * 128)
                out = pairs(bank[b])[:, n, :]
                mm(out, M_.V[:, 0, c], s.att[:, 0, e, :], start=True, stop=False)
                ins = mm(out, M_.V[:, 1, c], s.att[:, 1, e, :], start=False, stop=not state)
                if state:
                    mm(out, s.S[:, 0, e, :], M_.qP[:, e, :], start=False, stop=False)
                    ins = mm(out, s.S[:, 1, e, :], M_.qS[:, e, :], start=False, stop=True)
            mp = pe.mark(ins)
            m = act.mark(act.after(mp).activation(s.o[:, 2 * j:2 * j + 2, :], pairs(bank[b]), ACT.Copy))
            free[b] = [m]
            mo.append(m)
            yield
        while M_.m_in is None:
            yield
        sq = s.KC[:, :].rearrange('p (h t) -> p h t', h=4)
        rows = s.QC[0:8, 0:256], s.QC[0:8, 256:512]
        yield from head_norm(s.o, mo, 6, (7, 6), None, M_.g, M_.mg, sq, rows, M_.mix, s.spread[:, :], lambda: M_.m_in)
        M_.out = M_.mix.m[0] + M_.mix.m[2]

    def project(tag, src, halves, gate, s, xm):
        first = [free[j] for j in range(4)]

        def update(j, m):
            for n in range(2):
                e = 2 * j + n
                if gate is None:
                    mx = dve.mark(dve.after(m, xm).tensor_tensor(X[:, e, :], pairs(bank[j])[:, n, :], X[:, e, :], ALU.add))
                else:
                    mx = dve.mark(dve.after(m, xm).scalar_tensor_tensor(
                        X[:, e, :], pairs(bank[j])[:, n, :], gate[:, e:e + 1], X[:, e, :], ALU.mult, ALU.add))
                free[j] = [mx]
                if s is not None:
                    square(s, X[:, e, :], mx)
            if s is not None and j:
                add_square(s)
                add_square(s)
            X_now[0] = mx

        for i, half in enumerate(halves):
            for j in range(4):
                yield
                x = take(tag)
                if i and j:
                    update(j - 1, m)
                pe.after(first[j], x.ready)
                for k in range(4):
                    b = 4 * half + k
                    pe.after(src.m[b])
                    for n in range(2):
                        c = slice(k * 256 + n * 128, k * 256 + n * 128 + 128)
                        w, v, out = x.hi[:, c], x.lo[:, c], pairs(bank[j])[:, n, :]
                        mm(out, w, src.his[b], start=i == 0 and k == 0 and n == 0, stop=False)
                        mm(out, w, src.los[b], start=False, stop=False)
                        ins = mm(out, v, src.his[b], start=False, stop=i == 1 and k == 3)
                m = pe.mark(ins)
                done(x, m)
        if s is not None:
            table(ACT.Sqrt, None)
        update(3, m)

    X_now = [None]

    ua = Arena(nc, 'sel', G0, BIG0)
    i1T, i2T, g1T, g2T = (ua.take(k, [128, 256], F16) for k in ('i1T', 'i2T', 'g1T', 'g2T'))
    oneA = ua.take('oneA', [128, 2, 8, 128], F16)
    oneB1 = ua.take('oneB1', [128, 2, 8, 64], F16)
    oneB2 = ua.take('oneB2', [128, 2, 8, 64], F16)
    oneO = ua.take('oneO', [128, 8, 64], F16)
    acts = [nc.alloc_sbuf_tensor_at('act%d' % n, [128, 64, 256], F32, offset=BIG0 + n * 64 * KB) for n in range(2)]
    za = [Arena(nc, 'z0', H0, G0), Arena(nc, 'z1', BIG0 + 16 * KB, BIG0 + 32 * KB)]
    z_hi = [a.take('hi', [128, 4, 2, 256], F32R) for a in za]
    z_lo = [a.take('lo', [128, 4, 2, 256], F32R) for a in za]
    XB = nc.alloc_sbuf_tensor_at('XB', [128, 8, 256], F32, offset=BIG0 + 32 * KB)
    ra = Arena(nc, 'rank', R1, BIG1)
    skT = ra.take('skT', [128, 16, 128])
    qrT = ra.take('qrT', [128, 16, 256])
    SC = ra.take('SC', [128, 2, 16, 128])
    tv = ra.take('tv', [128, 2, 16, 16])
    ti = ra.take('ti', [128, 2, 16, 16], U32)
    tif = ra.take('tif', [128, 2, 16, 16])
    cand = ra.take('cand', [128, 2, 2, 256])
    top = ra.take('top', [128, 2, 8, 16])
    pos = ra.take('pos', [128, 2, 8, 16], U32)
    pab = ra.take('pab', [128, 2, 2, 8, 16], U32)
    paf = ra.take('paf', [128, 2, 2, 8, 16])
    hot = ra.take('hot', [128, 2, 2, 16, 16])
    sel = ra.take('sel', [128, 3, 2, 128])
    tsum = ra.take('tsum', [128, 2, 2, 8])
    iota_f = cols[:, 16:32]

    def ranks(j, msc):
        def best(vals, ids, src, deps, n):
            ms = [dve.mark(dve.after(deps).max(vals(q)[:, 0:8], src(q))) for q in range(n)]
            yield
            m1 = [dve.mark(dve.after(ms[q]).max_index(ids(q)[:, 0:8], vals(q)[:, 0:8], src(q))) for q in range(n)]
            yield
            m2 = [dve.mark(dve.after(m1[q]).match_replace(src(q), vals(q)[:, 0:8], src(q), LOWEST)) for q in range(n)]
            yield
            m3 = [dve.mark(dve.after(m2[q]).max(vals(q)[:, 8:16], src(q))) for q in range(n)]
            yield
            m4 = [dve.mark(dve.after(m3[q]).max_index(ids(q)[:, 8:16], vals(q)[:, 8:16], src(q))) for q in range(n)]
            yield m4

        at = lambda q: (q // 2, 2 * j + q % 2)
        for m in best(lambda q: tv[:, at(q)[0], at(q)[1], :], lambda q: ti[:, at(q)[0], at(q)[1], :],
                      lambda q: SC[:, at(q)[0], at(q)[1], :], msc, 4):
            yield
        mi = dve.mark(dve.after(m).tensor_copy(tif[:, :, 2 * j:2 * j + 2, :], ti[:, :, 2 * j:2 * j + 2, :]))
        cd = cand[:, j % 2, :, :]
        mc = [dve.mark(dve.after(m).tensor_tensor(
            cd[:, tt, :].rearrange('p (a b) -> p a b', a=16),
            tv[:, tt, 2 * j, :].unsqueeze(2).to_broadcast([128, 16, 16]),
            tv[:, tt, 2 * j + 1, :].unsqueeze(1).to_broadcast([128, 16, 16]), ALU.add)) for tt in range(2)]
        yield
        for m in best(lambda q: top[:, q, j, :], lambda q: pos[:, q, j, :], lambda q: cd[:, q, :], mc, 2):
            yield
        m1 = dve.mark(dve.after(m).tensor_scalar(pab[:, 0, :, j, :], pos[:, :, j, :], 4, None, ALU.logical_shift_right))
        m2 = dve.mark(dve.after(m).tensor_scalar(pab[:, 1, :, j, :], pos[:, :, j, :], 15, None, ALU.bitwise_and))
        mf = dve.mark(dve.after(m1, m2).tensor_copy(paf[:, :, :, j, :], pab[:, :, :, j, :]))
        for p in range(2):
            hp = hot[:, p, :, :, :]
            m = dve.mark(dve.after(mf).tensor_tensor(
                hp, paf[:, p, :, j, :].unsqueeze(3).to_broadcast([128, 2, 16, 16]),
                iota_f.unsqueeze(1).unsqueeze(1).to_broadcast([128, 2, 16, 16]), ALU.is_equal))
            yield
            m = dve.mark(dve.after(m, mi).tensor_tensor(
                hp, hp, tif[:, :, 2 * j + p, :].unsqueeze(2).to_broadcast([128, 2, 16, 16]), ALU.mult))
            yield
            m = dve.mark(dve.after(m).tensor_reduce(
                sel[:, p, :, 16 * j:16 * j + 16], hp, AX.X, ALU.add))
            yield
        U.ranked = m

    class Unit:
        pass

    U = Unit()

    def gates():
        ta = top[:, :, :, :]
        m = dve.mark(dve.after(U.ranked).tensor_tensor(
            paf[:, 0, :, :, :], ta, top[:, :, :, 0:1].to_broadcast([128, 2, 8, 16]), ALU.subtract))
        m = act.mark(act.after(m).activation(paf[:, 1, :, :, :], paf[:, 0, :, :, :], ACT.Exp))
        m1 = dve.mark(dve.after(m).tensor_reduce(tsum[:, 0, :, :], paf[:, 1, :, :, :], AX.X, ALU.add))
        m1 = dve.mark(dve.after(m1).reciprocal(tsum[:, 1, :, :], tsum[:, 0, :, :]))
        m1 = dve.mark(dve.after(m1).tensor_scalar(tsum[:, 1, :, :], tsum[:, 1, :, :], 4096.0, None, ALU.mult))
        m = dve.mark(dve.after(m1).tensor_tensor(
            sel[:, 2, :, :].rearrange('p t (h k) -> p t h k', h=8), paf[:, 1, :, :, :],
            tsum[:, 1, :, :].unsqueeze(3).to_broadcast([128, 2, 8, 16]), ALU.mult))
        yield
        pe.after(m, U.ranked, free[2], free[3])
        for n in range(3):
            for tt in range(2):
                c = (n % 2) * 256 + tt * 128
                ins = nc.tensor.transpose(bank[2 + n // 2][:, c:c + 128], sel[:, n, tt, :], ident[:, :])
        m = pe.mark(ins)
        U.off_scratch = [m, dve.last]
        a = act.mark(act.after(m, U.sel_free).activation(i1T[:, :], bank[2][:, 0:256], ACT.Copy))
        b = act.mark(act.after(m, U.sel_free).activation(i2T[:, :], bank[2][:, 256:512], ACT.Copy))
        c = act.mark(act.after(m, U.sel_free).activation(g1T[:, :], bank[3][:, 0:256], ACT.Copy))
        d = dve.mark(dve.after(m, c, U.sel_free).tensor_tensor(g2T[:, :], bank[3][:, 0:256], g1T[:, :], ALU.subtract))
        free[2] = [a, b]
        free[3] = [c, d]
        U.m_sel = [a, b, c, d]

    def queries(layer, h, before):
        ms = dma(skT[:, :, :], t['subkeys'][layer], before)
        for e in (act, dve):
            e.after(before)
        mq, U.todo = [None] * 8, []

        def score(j):
            b = 2 + j % 2
            pe.after(mq[j], ms, free[b])
            out = bank[b][:, :].rearrange('p (s t k) -> p s t k', s=2, t=2)
            for p in range(2):
                for tt in range(2):
                    ins = mm(out[:, p, tt, :], qrT[:, 2 * j + p, tt * 128:(tt + 1) * 128], skT[:, 2 * j + p, :])
            m = pe.mark(ins)
            m = act.mark(act.after(m).activation(
                SC[:, :, 2 * j:2 * j + 2, :].rearrange('p t s k -> p s t k'), out, ACT.Copy))
            free[b] = [m]
            U.todo.append(ranks(j, m))

        for j in range(8):
            first = free[j % 2]
            if j == 0:
                m = dense_pair('peer_wq%d' % layer, pairs(bank[0]), h, first)
                yield
            for n in range(2 if j else 0):
                m = dense('peer_wq%d' % layer, pairs(bank[j % 2])[:, n, :], h, first)
                yield
            mq[j] = act.mark(act.after(m).activation(qrT[:, 2 * j:2 * j + 2, :], pairs(bank[j % 2]), ACT.Copy))
            free[j % 2] = [mq[j]]
            if j:
                score(j - 1)
        score(7)
        U.queried = True

    def ranking():
        n = 0
        while n < 8:
            while len(U.todo) <= n:
                yield
            yield from U.todo[n]
            n += 1
        yield from gates()

    def first_half(layer, h, half, before):
        for i in range(32):
            b = i % 2
            first = free[b]
            for n in range(2):
                ends = [] if i == 31 and n else None
                m = dense('peer_u%d' % layer, pairs(bank[b])[:, n, :], h, first, ends)
                U.h_ends = ends
                yield
            m = act.mark(act.after(m, before() if i == 0 else None).activation(
                acts[half][:, 2 * i:2 * i + 2, :], pairs(bank[b]), ACT.Gelu))
            free[b] = [m]
            U.m_act[half] = m

    def gating(half):
        used = U.hot_free
        zm = [None, None]
        dep = U.m_sel

        made = [None, None]

        def build(n):
            k, c = n % 2, slice(8 * n, 8 * n + 8)
            w = lambda a, x: a.unsqueeze(2).to_broadcast([128, 8, x])
            mA = dve.mark(dve.after(dep, used[k]).tensor_tensor(
                oneA[:, k, :, :], iota16[:, :].unsqueeze(1).to_broadcast([128, 8, 128]), w(i1T[:, c], 128), ALU.is_equal))
            mO = dve.mark(dve.after(dep, made).tensor_tensor(
                oneO[:, :, :], iota16[:, 64 * half:64 * half + 64].unsqueeze(1).to_broadcast([128, 8, 64]),
                w(i2T[:, c], 64), ALU.is_equal))
            m1 = dve.mark(dve.after(mO, used[k]).tensor_tensor(oneB1[:, k, :, :], oneO[:, :, :], w(g1T[:, c], 64), ALU.mult))
            m2 = dve.mark(dve.after(mO, used[k]).tensor_tensor(oneB2[:, k, :, :], oneO[:, :, :], w(g2T[:, c], 64), ALU.mult))
            made[:] = [m1, m2]
            return [mA, m1, m2]

        ready = build(0)
        yield
        for n in range(32):
            k, b = n % 2, 2 + n % 2
            pe.after(ready, free[b])
            for q in range(8):
                out = bank[b][:, 64 * q:64 * q + 64]
                mm(out, oneA[:, k, q, :], oneB1[:, k, q, :], start=True, stop=False)
                ins = mm(out, oneA[:, k, q, :], oneB2[:, k, q, :], start=False, stop=True)
            mp = pe.mark(ins)
            used[k] = mp
            if n < 31:
                ready = build(n + 1)
            yield
            z = acts[half][:, :, 8 * n:8 * n + 8]
            m = dve.mark(dve.after(mp, U.m_act[half]).tensor_tensor(
                z, z, bank[b][:, :].rearrange('p (t k) -> p k t', t=8), ALU.mult))
            free[b] = [m]
            U.m_z[half] = m
            yield

    def second_half(layer, half, accs):
        parts = {}
        zh, zl = z_hi[half], z_lo[half]
        z_free = list(U.z_free[half])

        def split_z(i):
            k = i % 4
            src = acts[half][:, 2 * i:2 * i + 2, :]
            f = z_free[k]
            a = act.mark(act.after(U.m_z[half], f).activation(zh[:, k, :, :], src, ACT.Copy))
            b = dve.mark(dve.after(U.m_z[half], a, f).tensor_tensor(zl[:, k, :, :], src, zh[:, k, :, :].bitcast(F32),
                                                                  ALU.subtract))
            parts[i] = [a, b]
            if i == 15:
                U.m_part = parts[i]

        split_z(0)
        split_z(1)
        U.m_out = []
        yield
        for i in range(32):
            if i + 2 < 32:
                split_z(i + 2)
            k = i % 4
            for n in range(2):
                x = take('peer_v%d' % layer)
                pe.after(x.ready, parts[i], accs)
                first, end = half == 0 and i == 0 and n == 0, half == 1 and i == 31 and n == 1
                for b in range(8):
                    w, v = x.hi[:, b * 128:(b + 1) * 128], x.lo[:, b * 128:(b + 1) * 128]
                    out = pairs(bank[4 + b // 2])[:, b % 2, :]
                    mm(out, w, zh[:, k, n, :], start=first and b % 2 == 0, stop=False)
                    mm(out, w, zl[:, k, n, :], start=False, stop=False)
                    ins = mm(out, v, zh[:, k, n, :], start=False, stop=end)
                    if end and b % 2:
                        m = pe.mark(ins)
                        U.m_out.append(m)
                if not end:
                    m = pe.mark(ins)
                done(x, m)
                yield
            z_free[k] = m
        U.m_split[half] = parts[31]
        U.m_v = m

    def chain(*gens):
        for g in gens:
            yield from g

    def peer(layer, who, h, before, x_src, x_m, side=(), closing=(), at_end=()):
        U.m_act, U.m_z, U.m_split = [None, None], [None, None], [None, None]
        U.z_free = [None, None]
        U.sel_free = before
        U.layer, U.who = layer, who
        side, at_end = iter(side), iter(at_end)
        state['share'] = 16
        q = queries(layer, h, before)
        next(q)
        rank = ranking()
        run(q, rank, rank)
        run(first_half(layer, h, 0, x_free), rank, rank, rank, side)
        finish(rank)
        finish(closing)
        state['share'] = 13
        U.hot_free = [[pe.last, act.last]] * 2
        g0, g1 = gating(0), gating(1)
        run(first_half(layer, h, 1, lambda: U.off_scratch), more(g0))
        finish(g0)
        U.z_free[0] = U.h_ends
        v0 = second_half(layer, 0, free[4] + free[5] + free[6] + free[7])
        next(v0)
        g1 = more(g1)
        v1 = second_half(layer, 1, [])
        for _ in range(62):
            next(v0)
            next(g1, None)
        finish(g1)
        U.z_free[1] = [U.m_part] * 4
        next(v1)
        finish(v0)
        U.h_free = U.m_v
        U.mx = dma(X[:, :, :], x_src, U.m_split[0], x_m)
        state['share'] = 8
        run(v1, at_end)
        finish(at_end)

    def more(gen):
        n = 0
        for _ in gen:
            n += 1
            if n % 9:
                yield

    def peer_end(s):
        table(ACT.Sqrt, None)
        mg = dve.mark(dve.after(X_now[0]).tensor_scalar(gate_s[:, :], M(U.layer, 5, U.who), 2.0 ** -12, None, ALU.mult))
        for e in range(8):
            b = 4 + e // 2
            m = dve.mark(dve.after(U.m_out[e // 2], U.mx, mg).scalar_tensor_tensor(
                X[:, e, :], pairs(bank[b])[:, e % 2, :], gate_s[:, e:e + 1], X[:, e, :], ALU.mult, ALU.add))
            free[b] = [m]
            X_now[0] = m
            if s is not None:
                square(s, X[:, e, :], m)
                if e >= 2:
                    add_square(s)
            yield

    def scratch(name):
        return nc.dram_tensor(name, [128, 8, 256], F32).ap()

    def modulated():
        for e in engines:
            e.after(list(mod_m.values()))

    def squares(x, mx, b):
        s = squares_into(b)
        for e in range(8):
            square(s, x[:, e, :], mx)
            if e >= 2:
                add_square(s)
        return s

    def first_norm(x, s, layer, who, dst, dst_free, mx):
        return norm_steps(x, s, gain1[:, layer, who, :], M(layer, 0, who), dst, dst_free, mx)

    def second_norm(x, s, layer, who, dst, dst_free, mx):
        return norm_steps(x, s, gain2[:, layer, who, :], M(layer, 3, who), dst, dst_free, mx)

    def other_norm(how, src, layer, who, dst, dst_free, deps):
        mx = dma(XB[:, :, :], src, deps())
        for _ in range(4):
            yield
        s = squares(XB, mx, 2 if dst_free else 6)
        yield
        yield from how(XB, s, layer, who, dst, dst_free and dst_free(), mx)
        XB_now[0] = dst.m[6] + dst.m[7]

    def store(dst, *deps):
        m = dma(dst, X[:, :, :], X_now[0], *deps)
        x_stores.append(m)
        return m

    def x_free():
        return x_stores + [X_now[0]]

    XB_now, x_stores = [None], []
    conditions(None)
    mx = m_ctx
    mc_, mr_ = mixers(0)
    sh = mc_.shared
    pe.after(cm)
    m = modulation(0, range(4), 4, 5)
    s = squares(X, mx, 6)
    one_over_rms(s)
    bounds()
    finish(m)
    modulated()
    state['share'] = 16
    ahead()
    finish(first_norm(X, s, 0, 1, mc_.h, None, mx))
    late = modulation(0, range(4, 8), 2, 3)

    def state_chain(m, only_state, before):
        mixer_constants(m.shared, U.consts_after)
        while not m.ready:
            yield
        for e in (pe, dve):
            e.after(m.shared.cm)
        yield from scan(m, not only_state, before and before[0])
        yield from states(m)
        if not only_state:
            yield from mix_out(m, False)
        m.finished = True

    def latent_chain(m, context):
        while not (m.ready and context.finished):
            yield
        yield from scan(m, True, (context.out or []) + [context.shared.mS])
        yield from mix_out(m, True)

    state['share'] = 12
    U.consts_after = None
    side = state_chain(mc_, False, XB_now)
    run(win(mc_, 0, False), other_norm(first_norm, t['x'], 0, 0, mr_.h, None, lambda: None), side, timed(MOD_IN, late))
    finish(late)
    late = modulation(0, range(8, 12), 2, 3)
    late_x = latent_chain(mr_, mc_)
    run(win(mr_, 0, True), side, timed(MOD_IN, late), late_x)
    finish(late)
    finish(side)
    modulated()
    s = squares_into(6)
    run(project('w_out0', mc_.mix, (1, 0), M(0, 2, 1), s, mx), late_x)
    mp = pe.last
    xc1, x1, xc2, x2 = (scratch(k) for k in ('xc1', 'x1', 'xc2', 'x2'))
    m_xc1 = store(xc1)
    h = Split(h_hi, h_lo)
    finish(late_x)
    side = second_norm(X, s, 0, 1, h, mp, X_now[0])
    mx, before = [], marks()
    p = project('w_out0', mr_.mix, (1, 0), M(0, 2, 0), None, mx)
    for _ in range(5):
        next(p)
        for _ in range(4):
            next(side, None)
        if not mx and h.m[7]:
            mx.append(dma(X[:, :, :], t['x'], h.m[6], h.m[7], m_xc1))
    finish(p)
    m_x1 = store(x1)

    side = modulation(1, range(6), 4, 5)
    hx = Split(h_hi, h_lo)
    peer(0, 1, h, before, xc1, m_xc1, timed(MOD_PEER, side), side,
         other_norm(second_norm, x1, 0, 0, hx, lambda: U.h_free, lambda: U.m_split[0] + [m_x1]))
    finish(peer_end(None))
    m_xc2 = store(xc2)
    conditions(U.m_v)
    side = modulation(1, range(6, 12), 4, 5)
    mr_, mc_ = mixers(1)
    peer(0, 0, hx, U.m_split[1] + [U.m_v], x1, m_x1, timed(MOD_PEER, side), side,
         other_norm(first_norm, xc2, 1, 1, mc_.h, lambda: U.m_split[0], lambda: U.m_split[0] + [m_xc2]))

    def latent_norm():
        s = squares_into(4)
        yield from peer_end(s)
        yield from first_norm(X, s, 1, 0, mr_.h, U.h_free, X_now[0])

    state['share'] = 12
    side = latent_norm()
    run(win(mc_, 1, False, True), side)
    finish(side)
    U.consts_after = U.m_out
    side = state_chain(mc_, True, None)
    late_x = latent_chain(mr_, mc_)
    run(win(mr_, 1, True), side, late_x)
    finish(side)
    s = squares_into(6)
    p = project('w_out1', mr_.mix, (1, 0), M(1, 2, 0), s, X_now[0])
    for _ in range(5):
        next(p)
        next(late_x, None)
    finish(late_x)
    before = marks()
    finish(p)
    m_x2 = store(x2)
    finish(second_norm(X, s, 1, 0, h, pe.last, X_now[0]))
    peer(1, 0, h, before, x2, m_x2)
    s = squares_into(4)
    finish(peer_end(s))
    fence()

    ga = Arena(nc, 'tab', G0, BIG0)
    cosr, sinr, cosm, sinm = (ga.take(k, [128, 256]) for k in ('cosr', 'sinr', 'cosm', 'sinm'))
    permr, permm = ga.take('permr', [128, 128]), ga.take('permm', [128, 128])
    mask = ga.take('mask', [128, 384])
    spread = ga.take('spread', [8, 1024])
    a = Arena(nc, 'two', BIG0 + 16 * KB, BIG1)
    dec = a.take('dec', [128, 4, 384])
    spread16 = a.take('spread16', [16, 1024])
    cols2 = a.take('cols2', [128, 64])
    post = a.take('pos', [128, 256], I32)
    w_uq = a.take('uq', [128, 2, 1024])
    w_ukv = a.take('ukv', [128, 1024])
    rv = a.take('rv', [128, 2, 512])
    rraw = a.take('rraw', [128, 2, 2, 256])
    rk, rq, ry, rg = (a.take(k, [128, 4, 256]) for k in ('rk', 'rq', 'ry', 'rg'))
    ret_hi = nc.alloc_sbuf_tensor_at('ret_hi', [128, 4, 256], F32R, offset=a.at - 16 * KB)
    ret_lo = nc.alloc_sbuf_tensor_at('ret_lo', [128, 4, 256], F32R, offset=a.at - 12 * KB)
    rP = a.take('rP', [128, 4, 384])
    rsq = rP[:, :, 0:256]
    rows_l, rows_k, rows_q = (a.take(k, [n, 256]) for k, n in (('rows_l', 8), ('rows_k', 8), ('rows_q', 16)))
    rrows = a.take('rrows', [8, 2, 256])
    lat = a.take('lat', [128, 4, 256])
    tmp = a.take('tmp', [128, 2, 2, 256])
    qf, kf = a.take('qf', [128, 8, 256]), a.take('kf', [128, 8, 256])
    mv = a.take('mv', [128, 2, 512])
    mstat = a.take('mstat', [128, 4, 16])
    at = a.at
    mS = a.take('S', [128, 8, 384])
    PT = a.take('PT', [128, 8, 384])
    fa = Arena(nc, 'ffn', at, BIG1)
    fsg, fa32 = fa.take('sg', [128, 2, 256]), fa.take('a', [128, 2, 256])
    f_hi, f_lo = fa.take('hi', [128, 2, 256], F32R), fa.take('lo', [128, 2, 256], F32R)
    start = marks()
    m_tab = [dma(permr[:, :], t['perms'][:, 0:128], start), dma(permm[:, :], t['perms'][:, 128:256]),
             dma(mask[:, :], t['mask']), dma(spread[:, :], t['spread']), dma(dec[:, :, :], t['decay']),
             dma(spread16[:, :], t['spread16']), dma(cols2[:, :], t['cols2']),
             dma(post[:, :], t['positions'].partition_broadcast(128))]

    def tables(inv, sin, cos):
        r, k = tmp[:, 0, 0, :], tmp[:, 0, 1, :]
        big = 1.5 * 2.0 ** 23
        m = dve.mark(dve.after(m_tab).tensor_copy(k, post[:, :]))
        m = dve.mark(dve.after(m).tensor_scalar(r, k, inv, None, ALU.mult))
        yield
        m = dve.mark(dve.after(m).tensor_scalar(k, r, float(np.float32(0.5 / np.pi)), big, ALU.mult, ALU.add))
        m = dve.mark(dve.after(m).tensor_scalar(k, k, big, None, ALU.subtract))
        yield
        rest = 2 * np.pi
        for bits in (5, 14, 24, 34, 60):
            part = float(np.floor(rest * 2.0 ** bits) / 2.0 ** bits) if bits < 60 else float(rest)
            rest -= part
            m = dve.mark(dve.after(m).scalar_tensor_tensor(r, k, -part, r, ALU.mult, ALU.add))
            yield
        top = float(np.nextafter(np.float32(np.pi), np.float32(0)))
        m = dve.mark(dve.after(m).tensor_scalar(r, r, top, -top, ALU.min, ALU.max))
        m1 = act.mark(act.after(m).activation(sin, r, ACT.Sin))
        m = dve.mark(dve.after(m).scalar_tensor_tensor(k, r, -1.0, r, ALU.mult, ALU.max))
        m2 = act.mark(act.after(m).activation(cos, k, ACT.Sin, bias=epsc[:, 1:2], scale=-1.0))
        for e in (dve, pool):
            e.after(m1, m2)
        yield

    def ffn(tag, src, s, *side):
        f_free, ma, ends = [None, None], {}, []
        accs = free[4] + free[5] + free[6] + free[7]
        for f in range(23):
            if f < 22:
                b = k = f % 2
                first = free[b]
                if f == 0:
                    m2 = dense_pair(tag, pairs(bank[b]), src, first)
                else:
                    dense(tag, pairs(bank[b])[:, 0, :], src, first)
                    m2 = dense(tag, pairs(bank[b])[:, 1, :], src, first)
                m = act.mark(act.after(m2).activation(fsg[:, k, :], pairs(bank[b])[:, 0, :], ACT.Silu))
                free[b] = [m]
                m = dve.mark(dve.after(m, m2).tensor_tensor(fa32[:, k, :], pairs(bank[b])[:, 1, :], fsg[:, k, :], ALU.mult))
                free[b] = [m]
                m1 = act.mark(act.after(m, f_free[k]).activation(f_hi[:, k, :], fa32[:, k, :], ACT.Copy))
                m2 = dve.mark(dve.after(m1, f_free[k]).tensor_tensor(f_lo[:, k, :], fa32[:, k, :],
                                                                     f_hi[:, k, :].bitcast(F32), ALU.subtract))
                ma[f] = [m1, m2]
            if f:
                k = (f - 1) % 2
                x = take(tag)
                pe.after(x.ready, ma[f - 1], accs)
                for b in range(8):
                    w, v = x.hi[:, b * 128:(b + 1) * 128], x.lo[:, b * 128:(b + 1) * 128]
                    out = pairs(bank[4 + b // 2])[:, b % 2, :]
                    mm(out, w, f_hi[:, k, :], start=f == 1 and b % 2 == 0, stop=False)
                    mm(out, w, f_lo[:, k, :], start=False, stop=False)
                    ins = mm(out, v, f_hi[:, k, :], start=False, stop=f == 22)
                    if f == 22 and b % 2:
                        ends.append(pe.mark(ins))
                f_free[k] = ends[-1] if ends else pe.mark(ins)
                done(x, f_free[k])
            for g in side:
                next(g, None)
        table(ACT.Sqrt, ma[21])
        for e in range(8):
            b = 4 + e // 2
            m = dve.mark(dve.after(ends[e // 2]).scalar_tensor_tensor(
                X[:, e, :], pairs(bank[b])[:, e % 2, :], 0.5, X[:, e, :], ALU.mult, ALU.add))
            free[b] = [m]
            if s is not None:
                square(s, X[:, e, :], m)
                if e >= 2:
                    add_square(s)
        return m

    def win2(l, src, R):
        tag = 'w_in2%d' % l
        for j in range(2):
            if j == 0:
                m = dense_pair(tag, pairs(bank[0]), src, free[0])
                yield
            else:
                first = free[1]
                for n in range(2):
                    m = dense(tag, pairs(bank[1])[:, n, :], src, first)
                    yield
            m1 = act.mark(act.after(m).activation(lat[:, 2 * j:2 * j + 2, :], pairs(bank[j]), ACT.Copy))
            m2 = act.mark(act.after(m).activation(tmp[:, j, :, :], pairs(bank[j]), ACT.Square))
            free[j] = [m2]
            R.lat += [m1, m2]
        R.latents = True
        for res in dense_rows(tag, [bank[2][:, :], bank[3][:, :]], src, free[2] + free[3]):
            if len(res) < 4:
                yield
        for tt in range(2):
            m = act.mark(act.after(res).activation(rv[:, tt, :], bank[2 + tt][:, :], ACT.Copy))
            free[2 + tt] = [m]
            R.mv.append(m)
        yield
        raw_free = [None, None]
        late = []

        def rotate(dst, j, n, m, out):
            pe.after(m, free[2 + n])
            mp = pe.mark(mm(bank[2 + n][:, :], permr[:, :], rraw[:, n, :, :].rearrange('p a b -> p (a b)')))
            c = slice(2 * j, 2 * j + 2)
            w = lambda x: x[:, :].unsqueeze(1).to_broadcast([128, 2, 256])
            ma = dve.mark(dve.after(m).tensor_tensor(dst[:, c, :], rraw[:, n, :, :], w(cosr), ALU.mult))
            mb = dve.mark(dve.after(mp, ma).tensor_tensor(rraw[:, n, :, :], pairs(bank[2 + n]), w(sinr), ALU.mult))
            free[2 + n] = [mb]
            raw_free[n] = dve.mark(dve.after(ma, mb).tensor_tensor(dst[:, c, :], dst[:, c, :], rraw[:, n, :, :], ALU.add))
            out.append(raw_free[n])

        for dst, out in ((rk, R.mk), (rq, R.mq)):
            for j in range(2):
                first = free[j]
                for n in range(2):
                    m = dense(tag, pairs(bank[j])[:, n, :], src, first)
                    if n == 0 and late:
                        rotate(*late.pop(0))
                    yield
                m = act.mark(act.after(m, raw_free[j]).activation(rraw[:, j, :, :], pairs(bank[j]), ACT.Copy))
                free[j] = [m]
                late.append((dst, j, j, m, out))
        for j in range(2):
            first = free[j]
            for n in range(2):
                m = dense(tag, pairs(bank[j])[:, n, :], src, first)
                if late:
                    rotate(*late.pop(0))
                yield
            m = act.mark(act.after(m).activation(rg[:, 2 * j:2 * j + 2, :], pairs(bank[j]), ACT.Silu))
            free[j] = [m]
            R.mg.append(m)
        R.m_in = pe.last

    def retention(l, R, mix):
        while len(R.mq) < 2:
            yield
        mP = []
        for e in range(4):
            b = 2 + e % 2
            pe.after(R.mk[e // 2], R.mq[e // 2], free[b])
            mm(bank[b][:, 0:256], rk[:, e, 0:128], rq[:, e, :])
            mp = pe.mark(mm(bank[b][:, 256:384], rk[:, e, 128:256], rq[:, e, 128:256]))
            m = dve.mark(dve.after(mp).tensor_tensor(rP[:, e, :], bank[b][:, 0:384], dec[:, e, :], ALU.mult))
            free[b] = [m]
            mP.append(m)
            if e % 2:
                yield
        mo = []
        for j in range(2):
            b = 2 + j
            pe.after(mP[2 * j:2 * j + 2], R.mv, free[b])
            for n in range(2):
                e = 2 * j + n
                out, c = pairs(bank[b])[:, n, :], slice(e * 128, (e + 1) * 128)
                mm(out, rv[:, 0, c], rP[:, e, 0:256], start=True, stop=False)
                ins = mm(out[:, 128:256], rv[:, 1, c], rP[:, e, 256:384], start=False, stop=True)
            mp = pe.mark(ins)
            m = act.mark(act.after(mp).activation(ry[:, 2 * j:2 * j + 2, :], pairs(bank[b]), ACT.Copy))
            free[b] = [m]
            mo.append(m)
            yield
        gains = [P('ret_norm', 4 * l + e) for e in range(4)]
        act.after(mp)
        yield from head_norm(ry, mo, 2, (3, 2), gains, rg, R.mg, rsq, (rrows[:, 0, :], rrows[:, 1, :]), mix,
                             spread[:, :], lambda: mP)
        R.held = True

    def roots(b, n, rows, deps):
        m = act.mark(act.after(deps).activation(rows[0:n, :], bank[b][0:n, 0:256], ACT.Sqrt, bias=epsc[0:n, 0:1]))
        free[b] = [m]
        return dve.mark(dve.after(m).reciprocal(rows[0:n, :], rows[0:n, :]))

    def latents(l, R):
        while not R.latents:
            yield
        pe.after(R.lat, free[6])
        for i, c in enumerate((32, 32, 40, 48)):
            ins = mm(bank[6][0:8, 0:256], cols[:, c:c + 8], tmp[:, i // 2, i % 2, :], start=i == 0, stop=i == 3)
        R.tmp_free = pe.mark(ins)
        m = roots(6, 8, rows_l, R.tmp_free)
        yield
        pe.after(m, free[6], free[7])
        mm(pairs(bank[7])[:, 0, :], spread[:, 0:128], rows_l[:, :])
        mm(pairs(bank[7])[:, 1, :], spread[:, 128:256], rows_l[:, :])
        mp = pe.mark(mm(bank[6][:, 0:256], spread[:, 256:384], rows_l[:, :]))
        for i, (gcol, src) in enumerate(((P('kv_lat', l), 1), (P('q_lat', 2 * l), 0), (P('q_lat', 2 * l + 1), 0),
                                       (P('kn', l), 2))):
            i = (2, 0, 1, 3)[i]
            bb = bank[6][:, 0:256] if src == 2 else pairs(bank[7])[:, src, :]
            m = dve.mark(dve.after(mp, R.lat).scalar_tensor_tensor(lat[:, i, :], lat[:, i, :], gcol, bb, ALU.mult, ALU.mult))
            free[6 if src == 2 else 7] = [m]
            R.ml.append(m)
        yield
        pe.after(R.ml, free[7])
        mp = pe.mark(mm(bank[7][:, 0:256], permm[:, :], lat[:, 3, :]))
        mb = dve.mark(dve.after(mp, R.tmp_free).tensor_tensor(tmp[:, 0, 0, :], bank[7][:, 0:256], sinm[:, :], ALU.mult))
        free[7] = [mb]
        ma = dve.mark(dve.after(mp, R.ml).tensor_tensor(lat[:, 3, :], lat[:, 3, :], cosm[:, :], ALU.mult))
        m = dve.mark(dve.after(ma, mb).tensor_tensor(lat[:, 3, :], lat[:, 3, :], tmp[:, 0, 0, :], ALU.add))
        R.m_kr = act.mark(act.after(m).activation(
            kf[64:96, :, :], lat[64:96, 3, :].unsqueeze(1).to_broadcast([32, 8, 256]), ACT.Copy))
        R.tmp_free = [R.tmp_free, m]

    def keys(l, R, mw):
        while R.m_kr is None:
            yield
        pe.after(mw, R.ml)
        row_first, used = free[5], R.tmp_free
        mk = []
        for j in range(5):
            if j < 4:
                pe.after(free[4])
                for n in range(2):
                    e = 2 * j + n
                    ins = mm(pairs(bank[4])[0:64, n, :], w_ukv[:, e * 64:(e + 1) * 64], lat[:, 2, :])
                mp = pe.mark(ins)
                m1 = act.mark(act.after(mp).activation(kf[0:64, 2 * j:2 * j + 2, :], pairs(bank[4])[0:64, :, :], ACT.Copy))
                m2 = act.mark(act.after(mp, used).activation(tmp[0:64, 0, :, :], pairs(bank[4])[0:64, :, :], ACT.Square))
                free[4] = [m2]
                mk.append(m1)
                yield
                pe.after(m2, row_first)
                for n in range(2):
                    e = 2 * j + n
                    ins = mm(bank[5][0:8, 0:256], cols2[0:64, 39 - e:47 - e], tmp[0:64, 0, n, :], start=e == 0, stop=e == 7)
                used = pe.mark(ins)
        m = roots(5, 8, rows_k, used)
        for tt in range(2):
            pe.after(free[4])
            mp = pe.mark(mm(bank[4][:, :], lat[:, 2, tt * 128:(tt + 1) * 128], w_ukv[:, 512:1024]))
            m1 = act.mark(act.after(mp).activation(mv[:, tt, :], bank[4][:, :], ACT.Copy))
            free[4] = [m1]
            R.m_v.append(m1)
            yield
        for j in range(4):
            b = 4 + j % 2
            pe.after(m, free[b])
            for n in range(2):
                e = 2 * j + n
                ins = mm(pairs(bank[b])[0:64, n, :], spread[:, e * 128:e * 128 + 64], rows_k[:, :])
            mp = pe.mark(ins)
            c = slice(2 * j, 2 * j + 2)
            m1 = dve.mark(dve.after(mp, mk[j]).scalar_tensor_tensor(
                kf[0:64, c, :], kf[0:64, c, :], P('kn', l)[0:64, :], pairs(bank[b])[0:64, :, :], ALU.mult, ALU.mult))
            free[b] = [m1]
            R.m_k.append(m1)
            yield

    def heads(l, R, mw):
        while R.m_kr is None:
            yield
        w = lambda x: x[:, :].unsqueeze(1).to_broadcast([128, 2, 256])
        pe.after(mw, R.ml)
        mq = []
        row_first, used = free[7], R.tmp_free
        for j in range(4):
            pe.after(free[6])
            for n in range(2):
                e = 2 * j + n
                for i in range(2):
                    o = i * 512 + (e % 4) * 128
                    ins = mm(pairs(bank[6])[:, n, :], w_uq[:, e // 4, o:o + 128], lat[:, i, :], start=i == 0, stop=i == 1)
            mp = pe.mark(ins)
            m1 = act.mark(act.after(mp).activation(qf[:, 2 * j:2 * j + 2, :], pairs(bank[6]), ACT.Copy))
            m2 = act.mark(act.after(mp, used).activation(tmp[:, 1, :, :], pairs(bank[6]), ACT.Square))
            free[6] = [m2]
            mq.append(m1)
            yield
            pe.after(m2, row_first)
            for n in range(2):
                e = 2 * j + n
                ins = mm(bank[7][0:16, 0:256], cols2[:, 14 - 2 * e:30 - 2 * e], tmp[:, 1, n, :], start=e == 0, stop=e == 7)
            used = pe.mark(ins)
        m = roots(7, 16, rows_q, used)
        yield
        turned = [None] * 4
        for j in range(5):
            if j < 4:
                pe.after(m, free[6])
                for n in range(2):
                    e = 2 * j + n
                    ins = mm(pairs(bank[6])[:, n, :], spread16[:, e * 128:(e + 1) * 128], rows_q[:, :])
                mp = pe.mark(ins)
                c = slice(2 * j, 2 * j + 2)
                turned[j] = dve.mark(dve.after(mp, mq[j]).scalar_tensor_tensor(
                    qf[:, c, :], qf[:, c, :], P('qn', l), pairs(bank[6]), ALU.mult, ALU.mult))
                free[6] = [turned[j]]
            if j:
                c = slice(2 * j - 2, 2 * j)
                pe.after(turned[j - 1], free[7])
                mp = pe.mark(mm(bank[7][:, :], permm[:, :], qf[:, c, :].rearrange('p a b -> p (a b)')))
                m1 = dve.mark(dve.after(mp, used).tensor_tensor(tmp[:, 1, :, :], pairs(bank[7]), w(sinm), ALU.mult))
                free[7] = [m1]
                m2 = dve.mark(dve.after(mp).tensor_tensor(qf[:, c, :], qf[:, c, :], w(cosm), ALU.mult))
                used = dve.mark(dve.after(m1, m2).tensor_tensor(qf[:, c, :], qf[:, c, :], tmp[:, 1, :, :], ALU.add))
                R.m_q.append(used)
            yield

    def attention(l, R, g):
        while len(R.m_k) < 2 + 2 * g or len(R.m_q) < 2 + 2 * g or len(R.m_v) < 2:
            yield
        scale = 96.0 ** -0.5
        H = slice(4 * g, 4 * g + 4)
        m_s = []
        b = 4 + g
        for e in range(4 * g, 4 * g + 4):
            pe.after(R.m_q[e // 2], R.m_k[e // 2], R.m_kr, free[b])
            mm(bank[b][:, 0:256], qf[0:96, e, 128:256], kf[0:96, e, :])
            mp = pe.mark(mm(bank[b][:, 256:384], qf[0:96, e, 0:128], kf[0:96, e, 0:128]))
            m = dve.mark(dve.after(mp).scalar_tensor_tensor(mS[:, e, :], bank[b][:, 0:384], scale, mask[:, :],
                                                            ALU.mult, ALU.add))
            free[b] = [m]
            m_s.append(m)
            yield
        parts = (slice(0, 256), slice(256, 384))
        st = lambda r, i: mstat[:, r, 8 * i + 4 * g:8 * i + 4 * g + 4]
        mE = []
        for i, c in enumerate(parts):
            m = dve.mark(dve.after(m_s).tensor_reduce(st(0, i), mS[:, H, c], AX.X, ALU.max))
            m = dve.mark(dve.after(m).tensor_scalar(st(1, i), st(0, i), -1.0, None, ALU.mult))
            for e in range(4 * g, 4 * g + 4):
                k = 8 * i + e
                mE.append(act.mark(act.after(m).activation(mS[:, e, c], mS[:, e, c], ACT.Exp, bias=mstat[:, 1, k:k + 1],
                                                           accum_out=mstat[:, 2, k:k + 1])))
            yield
        mP = []
        for i, c in enumerate(parts):
            m = dve.mark(dve.after(mE).reciprocal(st(3, i), st(2, i)))
            mP.append(dve.mark(dve.after(m).tensor_tensor(
                mS[:, H, c], mS[:, H, c], st(3, i).unsqueeze(2).to_broadcast([128, 4, c.stop - c.start]), ALU.mult)))
        yield
        mT = []
        for e in range(4 * g, 4 * g + 4):
            pe.after(mP, free[b])
            nc.tensor.transpose(bank[b][:, 0:128], mS[:, e, 256:384], ident[:, :])
            nc.tensor.transpose(bank[b][:, 128:256], mS[:, e, 0:128], ident[:, :])
            mp = pe.mark(nc.tensor.transpose(bank[b][:, 256:384], mS[:, e, 128:256], ident[:, :]))
            m = act.mark(act.after(mp).activation(PT[:, e, :], bank[b][:, 0:384], ACT.Copy))
            free[b] = [m]
            mT.append(m)
            yield
        b = 6 + g
        pe.after(mT, R.m_v, free[b])
        for n in range(2):
            for i in range(2):
                e = 4 * g + 2 * n + i
                out = pairs(bank[b])[64 * i:64 * i + 64, n, :]
                mm(out, mv[:, 0, e * 64:(e + 1) * 64], PT[:, e, 0:256], start=n == 0, stop=False)
                ins = mm(out[:, 128:256], mv[:, 1, e * 64:(e + 1) * 64], PT[:, e, 256:384], start=False, stop=True)
        mp = pe.mark(ins)
        while R.m_in is None:
            yield
        put(R.mix, 4 + 2 * g, pairs(bank[b]), [mp], R.m_in)
        free[b] = R.mix.m[4 + 2 * g]

    def final_norm(s, mx):
        out = squares_into(1)
        mr = one_over_rms(s)
        for e in range(8):
            m = dve.mark(dve.after(mr, mx).scalar_tensor_tensor(X[:, e, :], X[:, e, :], P('final_g', e), nrs[:, :],
                                                                ALU.mult, ALU.mult))
            square(out, X[:, e, :], m)
            if e >= 2:
                add_square(out)
        return out, m

    s, m = final_norm(s, X_now[0])

    def sines():
        yield from tables(cols2[:, 48:49], sinr[:, :], cosr[:, :])
        yield from tables(cols2[:, 49:50], sinm[:, :], cosm[:, :])

    pe.after(m_tab)
    state['share'] = 6
    side = sines()
    wfree = None
    for l in range(2):
        mw = [dma(w_uq[:, :, :], t['w_uq'][l], start, wfree), dma(w_ukv[:, :], t['w_ukv'][l], wfree)]
        norm(X, s, P('ffn1_norm', 8 * l, 8 * l + 8), None, h, pe.last, m)
        s = squares_into(2)
        m = ffn('ffn1%d' % l, h, s, side)
        finish(side)
        fence()
        norm(X, s, P('mix_norm', 8 * l, 8 * l + 8), None, h, pe.last, m)
        R = Mixer()
        R.lat, R.mv, R.mk, R.mq, R.mg, R.ml, R.m_k, R.m_q, R.m_v = [], [], [], [], [], [], [], [], []
        R.latents, R.m_kr, R.m_in, R.held = False, None, None, False
        R.mix = Split(h_hi, h_lo)
        for b in range(4):
            R.mix.his[b], R.mix.los[b] = ret_hi[:, b, :], ret_lo[:, b, :]
        rmix = Split(ret_hi, ret_lo, 4)
        rmix.m = R.mix.m
        ret, kv = retention(l, R, rmix), chain(latents(l, R), keys(l, R, mw))
        rest = [kv, heads(l, R, mw), attention(l, R, 0), attention(l, R, 1)]
        run(win2(l, h, R), ret, kv, rest[1], ret, *rest)
        while not R.held:
            for g in [ret] + rest:
                next(g, None)
        s = squares_into(1)
        p = project('w_o2%d' % l, R.mix, (0, 1), None, s, m)
        for _ in range(5):
            next(p)
            for g in rest:
                next(g, None)
        together(rest)
        wfree = pe.last
        finish(p)
        m = X_now[0]
        fence()
        norm(X, s, P('ffn2_norm', 8 * l, 8 * l + 8), None, h, pe.last, m)
        s = squares_into(2) if l == 0 else None
        m = ffn('ffn2%d' % l, h, s)
    m_out = dma(t['out'], X[:, :, :], m)
    sp.after(m_out)
    fence()


def constants():
    f = np.float32
    c = np.zeros((128, 576), f)
    p = np.arange(128)
    c[:, 0:128] = np.eye(128)
    c[:, 128:256] = 1
    c[:, 256:384] = p[None, :]
    c[:, 384:512] = (p[:, None] % 32 == p[None, :])
    c[:, 512 + 7] = 1
    c[:, 528:544] = np.arange(16)[None, :]
    c[:, 512 + 32] = 1 / 256
    c[:, 512 + 41] = 1 / 128
    c[64:96, 512 + 50] = 1 / 32
    masks = np.zeros((128, 8, 128), np.uint8)
    for i in range(7):
        b = 1 << i
        masks[:, i, :] = ((p[:, None] // (2 * b) == p[None, :] // (2 * b)) & (p[:, None] // b != p[None, :] // b))
    spread = np.zeros((8, 8, 128), f)
    for i in range(8):
        spread[i, i, :] = 1
    spread16 = np.zeros((16, 8, 128), f)
    for i in range(8):
        spread16[2 * i, i, 0:64] = 1
        spread16[2 * i + 1, i, 64:96] = 1
    s, t = p[:, None].astype(np.float64), np.arange(256)[None, :].astype(np.float64)
    lg = np.log1p(-2.0 ** (-5.0 - np.arange(4)))
    full = np.stack([np.where(t >= s, np.exp(np.maximum(t - s, 0) * g), 0) * 128 ** -0.5 for g in lg], 1)
    decay = np.concatenate([full, full[:, :, 0:128]], 2).astype(f)
    causal = np.where(p[:, None] >= p[None, :], 0, -1e30)
    mask = np.concatenate([np.zeros((128, 128)), causal, causal], 1).astype(f)
    perms = np.zeros((128, 256), f)
    for i in range(64):
        perms[i + 64, i] = -1
        perms[i, i + 64] = 1
    for i in range(16):
        perms[80 + i, 128 + 64 + i] = -1
        perms[64 + i, 128 + 80 + i] = 1
    cols2 = np.zeros((128, 64), f)
    cols2[0:64, 14] = 1 / 64
    cols2[64:96, 15] = 1 / 32
    cols2[0:64, 39] = 1 / 64
    inv = lambda dim: (f(1) / (f(10000.0) ** (np.arange(0, dim, 2, dtype=f) / f(dim)))).astype(f)
    cols2[:, 48] = np.tile(inv(128), 2)
    cols2[64:96, 49] = np.tile(inv(32), 2)
    return dict(consts=c, masks=masks.reshape(128, 1024).view(np.uint32), spread=spread.reshape(8, 1024), spread16=spread16.reshape(16, 1024),
                decay=decay, mask=mask, perms=perms, cols2=cols2)


def pack(inputs):
    a = {k: np.asarray(v) for k, v in inputs.items()}
    out = constants()

    def granules(tl):
        n = tl.shape[0]
        return np.ascontiguousarray(tl.reshape(n // 2, 2, 128, 1024).transpose(0, 2, 1, 3))

    def columns(w):
        n = w.shape[1] // 128
        return w.reshape(8, 128, n, 128).transpose(2, 1, 0, 3).reshape(n, 128, 1024)

    def rows(w):
        return w.reshape(4, 2, 128, 512).transpose(0, 2, 1, 3).reshape(4, 128, 1024)

    def halves(w):
        return w.reshape(2, 4, 128, 4, 256).transpose(0, 3, 2, 1, 4).reshape(8, 128, 1024)

    def vec(v):
        return v.reshape(-1, 128).T

    out['ctx'] = np.ascontiguousarray(a['ctx'][0].T.reshape(8, 128, 256).transpose(1, 0, 2))
    out['x'] = np.ascontiguousarray(a['x'][0].T.reshape(8, 128, 256).transpose(1, 0, 2))
    pad = np.zeros((2, 32), np.float32)
    pad64 = np.zeros((2, 64), np.float32)
    names = dict(ffn1_norm='ffn1_norm_2', mix_norm='mix_norm_2', ffn2_norm='ffn2_norm_2', ret_norm='ret_head_norm_2',
                 q_lat='q_lat_norm_2', kv_lat='kv_lat_norm_2')
    heads = {'qn': np.concatenate([a['qn_nope_2'], a['qn_rope_2'], pad], 1),
             'kn': np.concatenate([a['kn_nope_2'], a['kn_rope_2'], pad], 1)}
    out['params'] = np.ascontiguousarray(np.concatenate(
        [vec(heads[n] if n in heads else a[names.get(n, n)]) for n, _ in PARAMS], 1))
    for l in range(2):
        out['w_mod%d' % l] = granules(a['w_mod'][l].reshape(4, 2, 128, 12, 512).transpose(3, 0, 2, 1, 4)
                                      .reshape(48, 128, 1024))
        w = a['w_in'][l]
        order = [512, 1024, 1536, 2048, 2560, 3584, 3072]
        out['w_in%d' % l] = granules(np.concatenate([rows(w[:, 0:512])] + [columns(w[:, o:o + 512]) for o in order]))
        out['w_out%d' % l] = granules(halves(a['w_out'][l])[[4, 5, 6, 7, 0, 1, 2, 3]])
        out['peer_wq%d' % l] = granules(columns(a['peer_wq'][l]))
        out['peer_u%d' % l] = granules(a['peer_u'][l].reshape(128, 128, 8, 128).transpose(1, 3, 2, 0).reshape(128, 128, 1024))
        out['peer_v%d' % l] = granules(a['peer_v'][l].reshape(128, 128, 1024).transpose(1, 0, 2))
        w = a['w_in_2'][l]
        kr = np.zeros((1024, 128), np.float32)
        kr[:, 64:96] = w[:, 2432:2464]
        out['w_in2%d' % l] = granules(np.concatenate([
            columns(w[:, 2048:2432]), columns(kr), rows(w[:, 1024:1536]), columns(w[:, 512:1024]), columns(w[:, 0:512]),
            columns(w[:, 1536:2048])]))
        out['w_o2%d' % l] = granules(halves(a['w_o_2'][l]))
        for f in ('ffn1', 'ffn2'):
            g, u = columns(a[f + '_w_gate_2'][l]), columns(a[f + '_w_up_2'][l])
            d = a[f + '_w_down_2'][l].reshape(22, 128, 1024)
            seq = []
            for i in range(23):
                if i < 22:
                    seq += [g[i], u[i]]
                if i:
                    seq.append(d[i - 1])
            out['%s%d' % (f, l)] = granules(np.stack(seq))
    out['subkeys'] = np.ascontiguousarray(a['peer_subkeys'].transpose(0, 4, 1, 2, 3).reshape(2, 128, 16, 128))
    uq = np.zeros((2, 2, 128, 8, 128), np.float32)
    uq[..., 0:96] = a['w_uq_2'].reshape(2, 2, 128, 8, 96)
    out['w_uq'] = np.ascontiguousarray(uq.reshape(2, 2, 128, 2, 512).transpose(0, 2, 3, 1, 4).reshape(2, 128, 2, 1024))
    out['w_ukv'] = np.ascontiguousarray(a['w_ukv_2'].reshape(2, 128, 8, 2, 64).transpose(0, 1, 3, 2, 4).reshape(2, 128, 1024))
    out['positions'] = np.ascontiguousarray(a['positions_2'].reshape(1, 256))
    return out


def kernel(**inputs):
    import concourse.bacc as bacc
    from concourse.bass_utils import run_bass_kernel_spmd

    nc = bacc.Bacc("TRN2", target_bir_lowering=False, num_devices=1)
    arrays = pack(inputs)
    t = {k: nc.dram_tensor('in_' + k, v.shape, mybir.dt.from_np(v.dtype), kind="ExternalInput").ap()
         for k, v in arrays.items()}
    t['out'] = nc.dram_tensor('out', (128, 8, 256), F32, kind="ExternalOutput").ap()
    build(nc, t)
    r = run_bass_kernel_spmd(nc, [{'in_' + k: v for k, v in arrays.items()}], core_ids=[0])
    y = r.results[0]['out']
    return np.ascontiguousarray(y.transpose(1, 0, 2).reshape(1024, 256).T.reshape(1, 256, 1024))
```

```python
import numpy as np
import concourse.bass as bass
from concourse import mybir
from concourse.alu_op_type import AluOpType as ALU

F32 = mybir.dt.float32
F32R = mybir.dt.float32r
F16 = mybir.dt.float16
U8 = mybir.dt.uint8
U32 = mybir.dt.uint32
I32 = mybir.dt.int32
ACT = mybir.ActivationFunctionType
AX = mybir.AxisListType

EPS = 1e-6
F_FLOOR = 1e-20
LOWEST = -3.0e38

PARAMS = [('norm1_g', 16), ('norm2_g', 16), ('b_mod', 96), ('final_g', 8), ('conv_w', 24), ('lb_logits', 16),
          ('c', 8), ('c_ctx', 8), ('ffn1_norm', 16), ('mix_norm', 16), ('ffn2_norm', 16), ('ret_norm', 8),
          ('q_lat', 4), ('kv_lat', 2), ('qn', 2), ('kn', 2)]
PCOL, PN = {}, 0
for _n, _w in PARAMS:
    PCOL[_n] = PN
    PN += _w


MOD_IN = [4, 8, 12, 16, 20, 24]


class Lane:

    def __init__(self, nc, eng, name):
        self.nc, self.eng, self.name = nc, eng, name
        self.turn, self.n, self.seen = 0, 0, {}
        self.sem = nc.alloc_semaphore(name + '0')
        self.last = None

    def after(self, *marks):
        for m in marks:
            if m is None:
                continue
            if isinstance(m, list):
                self.after(*m)
                continue
            key, sem, value = m
            if self.seen.get(key, 0) < value:
                self.eng.wait_ge(sem, value)
                self.seen[key] = value
        return self.eng

    def mark(self, ins):
        if self.n == 16000:
            self.turn, self.n = self.turn + 1, 0
            self.sem = self.nc.alloc_semaphore('%s%d' % (self.name, self.turn))
        self.n += 1
        ins.then_inc(self.sem, 1)
        self.last = ('%s%d' % (self.name, self.turn), self.sem, self.n)
        return self.last


class Arena:

    def __init__(self, nc, tag, start, end):
        self.nc, self.tag, self.at, self.end = nc, tag, start, end

    def take(self, name, shape, dtype=F32):
        size = int(np.prod(shape[1:])) * mybir.dt.size(dtype)
        at = self.at
        self.at += (size + 31) // 32 * 32
        assert self.at <= self.end, (self.tag, name, self.at, self.end)
        return self.nc.alloc_sbuf_tensor_at('%s_%s' % (self.tag, name), list(shape), dtype, offset=at)


class Tile:
    def __init__(self, tag, granule, sub, raw):
        self.tag, self.granule, self.sub, self.raw = tag, granule, sub, raw
        self.hi = self.lo = None
        self.ready = []


def schedule():
    def run(name, a, b):
        return [(name, g, 2, False) for g in range(a, b)]

    def mods(layer, a, b):
        return [('w_mod%d' % layer, g, 2, True) for g in range(a, b)]

    def mixed(main, side, at):
        out, side = [], list(side)
        for n, g in enumerate(main):
            out.append(g)
            if side and 2 * n + 2 in at:
                out.append(side.pop(0))
        return out

    def peer(layer):
        return run('peer_wq%d' % layer, 0, 8) + run('peer_u%d' % layer, 0, 64) + run('peer_v%d' % layer, 0, 64)

    order = mods(0, 0, 8)
    order += mixed(run('w_in0', 0, 16), mods(0, 8, 14), MOD_IN) + mixed(run('w_in0', 0, 16), mods(0, 14, 20), MOD_IN)
    order += run('w_out0', 0, 4) + run('w_out0', 0, 4)
    order += peer(0) + peer(0)
    order += run('w_in1', 0, 6) + run('w_in1', 0, 16) + run('w_out1', 0, 4) + peer(1)
    for l in range(2):
        order += run('ffn1%d' % l, 0, 33) + run('w_in2%d' % l, 0, 10) + run('w_o2%d' % l, 0, 4)
        order += run('ffn2%d' % l, 0, 33)
    return order


def build(nc, t):
    pe = Lane(nc, nc.tensor, 'pe')
    act = Lane(nc, nc.scalar, 'act')
    dve = Lane(nc, nc.vector, 'dve')
    pool = Lane(nc, nc.gpsimd, 'pool')
    sp = Lane(nc, nc.sync, 'sp')
    engines = [pe, act, dve, pool]

    KB = 1024
    CONST0 = 16512
    RAW0 = CONST0 + 4960
    HL0 = RAW0 + 24 * KB
    H0 = HL0 + 24 * KB
    G0 = H0 + 16 * KB
    BIG0 = G0 + 11 * KB
    BIG1 = BIG0 + 128 * KB
    R1 = BIG0 + 64 * KB
    NG, NH = 3, 3

    ca = Arena(nc, 'const', CONST0, RAW0)
    ident = ca.take('ident', [128, 128])
    ones = ca.take('ones', [128, 128])
    onehot = ca.take('onehot', [128, 128])
    iota16 = ca.take('iota16', [128, 128], F16)
    par = ca.take('par', [128, PN])
    mod = ca.take('mod', [128, 2, 48, 2])
    gain1 = ca.take('gain1', [128, 2, 2, 8])
    gain2 = ca.take('gain2', [128, 2, 2, 8])
    lbv = ca.take('lbv', [128, 2, 8])
    lbc = ca.take('lbc', [128, 2, 8])
    epsc = ca.take('epsc', [128, 4])
    cols = ca.take('cols', [128, 64])
    gate_s = ca.take('gate_s', [128, 8])

    raw = nc.alloc_sbuf_tensor_at('raw', [128, NG, 2, 1024], F32, offset=RAW0)
    whi = nc.alloc_sbuf_tensor_at('whi', [128, NH, 1024], F32R, offset=HL0)
    wlo = nc.alloc_sbuf_tensor_at('wlo', [128, NH, 1024], F32R, offset=HL0 + 4 * KB * NH)
    ha = Arena(nc, 'h', H0, G0)
    h_hi = ha.take('hi', [128, 8, 256], F32R)
    h_lo = ha.take('lo', [128, 8, 256], F32R)
    X = nc.alloc_sbuf_tensor_at('X', [128, 8, 256], F32, offset=BIG0)
    na = Arena(nc, 'norm', BIG0 + 8 * KB, BIG0 + 16 * KB)
    nsq = na.take('sq', [128, 4, 256])
    nrr = na.take('rr', [128, 2, 256])
    nrt, nrs = nrr[:, 0, :], nrr[:, 1, :]
    ny = na.take('y', [128, 2, 256])

    bank = [nc.alloc_psum_tensor('bank%d' % b, [128, 512], F32) for b in range(8)]
    free = [[] for _ in range(8)]

    count = [0]

    def dma(dst, src, *deps):
        s = nc.alloc_semaphore('dma%d' % count[0])
        count[0] += 1
        sp.after(*deps).dma_start(dst, src).then_inc(s, 16)
        return ('dma%d' % (count[0] - 1), s, 16)

    def marks():
        return [e.last for e in engines]

    def fence():
        now = marks()
        for e in engines:
            e.after(now)

    order = schedule()
    tiles = []
    for g, (name, index, k, as_is) in enumerate(order):
        for sub in range(k):
            tiles.append(Tile(name, g, sub, as_is))
    split_tiles = [x for x in tiles if not x.raw]
    slot_sem = [nc.alloc_semaphore('raw%d' % s) for s in range(NG)]
    state = dict(pos=0, fetched=0, split=0, sidx=0, turn=0, share=(0,))
    landed = {}
    freed = {g: [] for g in range(len(order))}
    used_up = {}
    spent = {}

    def fetch():
        while state['fetched'] < len(order):
            g = state['fetched']
            if g >= NG and used_up.get(g - NG, 0) < order[g - NG][2]:
                return
            name, index, k, as_is = order[g]
            deps = freed[g - NG] if g >= NG else []
            sp.after(*deps).dma_start(raw[:, g % NG, 0:k, :], t[name][index]).then_inc(slot_sem[g % NG], 16)
            landed[g] = ('raw%d' % (g % NG), slot_sem[g % NG], 16 * (g // NG + 1))
            state['fetched'] += 1

    def give_back(g, *marks):
        freed[g].extend(marks)
        used_up[g] = used_up.get(g, 0) + 1
        fetch()

    def split():
        j = state['split']
        x = split_tiles[j]
        fetch()
        src = raw[:, x.granule % NG, x.sub, :]
        s = j % NH
        gone = spent[j - NH] if j >= NH else None
        x.hi, x.lo = whi[:, s, :], wlo[:, s, :]
        m = act.mark(act.after(landed[x.granule], gone).activation(x.hi, src, ACT.Copy))
        lane = pool if state['share'][state['turn'] % len(state['share'])] else dve
        state['turn'] += 1
        k = lane.mark(lane.after(landed[x.granule], m, gone).tensor_tensor(x.lo, src, x.hi.bitcast(F32), ALU.subtract))
        x.ready = [m, k]
        state['split'] += 1
        give_back(x.granule, m, k)

    def share(*pattern):
        state['share'], state['turn'] = pattern, 0

    def take(tag, ahead=NH):
        x = tiles[state['pos']]
        assert x.tag == tag, (x.tag, tag, state['pos'])
        state['pos'] += 1
        if x.raw:
            fetch()
            x.hi = raw[:, x.granule % NG, x.sub, :]
            x.ready = [landed[x.granule]]
            return x
        x.at = state['sidx']
        state['sidx'] += 1
        while state['split'] < min(x.at + ahead, len(split_tiles)):
            split()
        return x

    def ahead():
        if state['split'] == state['sidx']:
            split()

    def done(x, m):
        if x.raw:
            give_back(x.granule, m)
        else:
            spent[x.at] = m

    def mm(out, lhsT, rhs, start=True, stop=True, **kw):
        return nc.tensor.matmul(out, lhsT, rhs, start=start, stop=stop, skip_group_check=True, **kw)

    class Split:

        def __init__(self, hi, lo, n=8):
            self.hi, self.lo, self.m, self.m_hi = hi, lo, [None] * 8, [None] * 8
            self.his, self.los = [hi[:, b, :] for b in range(n)], [lo[:, b, :] for b in range(n)]

    def dense(tag, out, src, first, ends=None):
        steps = dense_steps(tag, out, src, first, ends)
        next(steps)
        return next(steps)

    def dense_steps(tag, out, src, first, ends=None):
        x = take(tag)
        pe.after(first, x.ready)
        for b in range(8):
            w, v = x.hi[:, b * 128:(b + 1) * 128], x.lo[:, b * 128:(b + 1) * 128]
            pe.after(src.m[b])
            mm(out, w, src.hi[:, b, :], start=b == 0, stop=False)
            mm(out, w, src.lo[:, b, :], start=False, stop=False)
            ins = mm(out, v, src.hi[:, b, :], start=False, stop=b == 7)
            if ends is not None and b % 2:
                ends.append(pe.mark(ins))
            if b == 3:
                yield
        m = ends[-1] if ends else pe.mark(ins)
        done(x, m)
        yield m

    def dense_pair(tag, out, src, first):
        pe.after(first)
        two = [take(tag), take(tag, NH - 1)]
        for b in range(8):
            c = slice(b * 128, (b + 1) * 128)
            pe.after(src.m_hi[b])
            for n, x in enumerate(two):
                pe.after(x.ready)
                mm(out[:, n, :], x.hi[:, c], src.hi[:, b, :], start=b == 0 and n == 0, stop=False)
                mm(out[:, n, :], x.lo[:, c], src.hi[:, b, :], start=False, stop=False)
            pe.after(src.m[b])
            for n, x in enumerate(two):
                ins = mm(out[:, n, :], x.hi[:, c], src.lo[:, b, :], start=False, stop=b == 7)
        m = pe.mark(ins)
        for x in two:
            done(x, m)
        return m

    def dense_rows(tag, outs, src, first):
        res = []
        for j in range(4):
            x = take(tag)
            pe.after(first, x.ready)
            for k in range(2):
                b = 2 * j + k
                pe.after(src.m[b])
                w, v = x.hi[:, k * 512:(k + 1) * 512], x.lo[:, k * 512:(k + 1) * 512]
                for tt in range(2):
                    c = slice(tt * 128, (tt + 1) * 128)
                    mm(outs[tt], src.hi[:, b, c], w, start=b == 0, stop=False)
                    mm(outs[tt], src.lo[:, b, c], w, start=False, stop=False)
                    ins = mm(outs[tt], src.hi[:, b, c], v, start=False, stop=b == 7)
            m = pe.mark(ins)
            done(x, m)
            res.append(m)
            yield res

    m_par = dma(par[:, :], t['params'])
    cm = [dma(ident[:, :], t['consts'][:, 0:128]), dma(ones[:, :], t['consts'][:, 128:256]),
          dma(onehot[:, :], t['consts'][:, 384:512]), dma(cols[:, :], t['consts'][:, 512:576])]
    iof = ny[:, 0, 0:128]
    im = dma(iof, t['consts'][:, 256:384])
    fetch()
    m_ctx = dma(X[:, :, :], t['ctx'])
    m_eps = [dve.mark(nc.vector.memset(epsc[:, 0:1], EPS)), dve.mark(nc.vector.memset(epsc[:, 1:2], float(np.pi / 2)))]
    for e in (act, dve):
        e.after(m_par, m_eps)

    def P(name, a, b=None):
        i = PCOL[name] + a
        return par[:, i:i + 1] if b is None else par[:, i:PCOL[name] + b]

    sca = Arena(nc, 'cond', G0 + 2 * KB, G0 + 6 * KB)
    cond = sca.take('cond', [128, 8, 64])
    mev = sca.take('mev', [128, 512])
    mod_m = {}

    def conditions(before):
        m0 = dve.mark(dve.after(before).memset(cond[:, :, :], 0.0))
        m1 = act.mark(act.after(m0).activation(cond[:, :, 30], P('c', 0, 8), ACT.Silu))
        m2 = act.mark(act.after(m0).activation(cond[:, :, 31], P('c_ctx', 0, 8), ACT.Silu))
        pe.after(m0, m1, m2)

    def modulation(layer, groups, b1, b2):
        groups = list(groups)
        n = len(groups)
        first = free[b1]
        for i, g in enumerate(groups):
            for j in range(4):
                x = take('w_mod%d' % layer)
                pe.after(first, x.ready)
                for k in range(2):
                    b = 2 * j + k
                    q = b % 4
                    ins = mm(bank[b1][32 * q:32 * q + 32, :], cond[:, b, 30 - 2 * i:62 - 2 * i],
                             x.hi[:, k * 512:(k + 1) * 512], start=i == 0 and b < 4, stop=i == n - 1 and b >= 4,
                             tile_position=(0, 32 * q))
                m = pe.mark(ins)
                done(x, m)
                if j == 1:
                    yield
            if i < n - 1:
                yield
        m = act.mark(act.after(m).activation(mev[:, :], bank[b1][:, :], ACT.Copy))
        free[b1] = [m]
        yield
        pe.after(m, free[b2])
        for b in range(4):
            ins = mm(bank[b2][:, b * 128:(b + 1) * 128], mev[:, b * 128:(b + 1) * 128], onehot[:, :])
        mp = pe.mark(ins)
        for i, g in enumerate(groups):
            turned = bank[b2][:, :].rearrange('p (b j) -> p b j', b=4)[:, :, 2 * i:2 * i + 2]
            bias = P('b_mod', layer * 48 + g * 4, layer * 48 + g * 4 + 4).unsqueeze(2).to_broadcast([128, 4, 2])
            m = dve.mark(dve.after(mp).tensor_tensor(mod[:, layer, g * 4:g * 4 + 4, :], turned, bias, ALU.add))
            free[b2] = [m]
            mod_m[layer, g] = m
            for dst, norm, base in ((gain1, 'norm1_g', 2), (gain2, 'norm2_g', 8)):
                if base <= g < base + 2:
                    h = g - base
                    for who in range(2):
                        mod_m[layer, g, who] = dve.mark(dve.after(m).scalar_tensor_tensor(
                            dst[:, layer, who, 4 * h:4 * h + 4], mod[:, layer, g * 4:g * 4 + 4, who], 1.0,
                            P(norm, layer * 8 + 4 * h, layer * 8 + 4 * h + 4), ALU.add, ALU.mult))

    row_sem = [nc.alloc_semaphore('rows%d' % s) for s in range(4)]
    row_count = [0] * 4

    def condition_row(place, name, deps):
        m = dma(place[:, :], t[name].partition_broadcast(128), deps)
        return lambda: act.mark(act.after(m).activation(place[:, :], place[:, :], ACT.Silu))

    def modulation_rows(first, blocks, rows, slots, spare, deps, rest):
        n, k = len(blocks), len(slots)
        gone, here, turn = [deps] * n, {}, [None, None]

        def load(i):
            s = i % k
            row_count[s] += 1
            sp.after(gone[i - k] if i >= k else deps).dma_start(slots[s][:, :], t['w_mod_rows'][first + i]).then_inc(row_sem[s], 16)
            here[i] = ('rows%d' % s, row_sem[s], 16 * row_count[s])

        for i in range(k):
            load(i)
            yield
        rows = [(who, row, make()) for who, row, make in rows]
        for i, (layer, b) in enumerate(blocks):
            for who, row, mr in rows:
                m = dve.mark(dve.after(here[i], mr, turn[0]).scalar_tensor_tensor(
                    spare[0][:, :], slots[i % k][:, :], 1.0, row[:, :], ALU.mult, ALU.mult,
                    accum_out=mod[:, layer, b, who:who + 1]))
                turn, spare = [turn[1], m], spare[::-1]
            gone[i] = m
            if i >= 2 and i - 2 + k < n:
                load(i - 2 + k)
            yield
            if i % rest == rest - 1:
                yield

    def modulation_end(layer, a, b, who):
        m = dve.mark(dve.after(dve.last).tensor_tensor(mod[:, layer, a:b, who], mod[:, layer, a:b, who],
                                                       P('b_mod', layer * 48 + a, layer * 48 + b), ALU.add))
        for dst, norm, at in ((gain1, 'norm1_g', 8), (gain2, 'norm2_g', 32)):
            if a <= at < b:
                m = dve.mark(dve.after(m).scalar_tensor_tensor(dst[:, layer, who, :], mod[:, layer, at:at + 8, who], 1.0,
                                                               P(norm, layer * 8, layer * 8 + 8), ALU.add, ALU.mult))
        mod_m[layer, a, who] = m

    def bounds():
        m_iota = dve.mark(dve.after(im).tensor_copy(iota16[:, :], iof))
        for e in engines:
            e.after(cm, m_iota)
        lm = ny[:, 1, 0:8]
        le = ny[:, 1, 16:32].rearrange('p (l e) -> p l e', l=2)
        ls = ny[:, 1, 32:40]
        lg = P('lb_logits', 0, 16).rearrange('p (l e) -> p l e', l=2)
        m = dve.mark(nc.vector.tensor_tensor(lm, lg[:, 0, :], lg[:, 1, :], ALU.max))
        m = dve.mark(dve.after(m).tensor_tensor(le, lg, lm.unsqueeze(1).to_broadcast([128, 2, 8]), ALU.subtract))
        m = act.mark(act.after(m).activation(le, le, ACT.Exp))
        m = dve.mark(dve.after(m).tensor_tensor(ls, le[:, 0, :], le[:, 1, :], ALU.add))
        m = dve.mark(dve.after(m).reciprocal(ls, ls))
        m = dve.mark(dve.after(m).tensor_tensor(le, le, ls.unsqueeze(1).to_broadcast([128, 2, 8]), ALU.mult))
        m1 = dve.mark(dve.after(m).tensor_tensor(lbv[:, 0, :], le[:, 0, :], le[:, 0, :], ALU.subtract))
        m = dve.mark(dve.after(m).tensor_tensor(ls, le[:, 0, :], le[:, 1, :], ALU.add))
        m = dve.mark(dve.after(m).tensor_tensor(lbv[:, 1, :], ls, le[:, 0, :], ALU.subtract))
        m_lb = dve.mark(dve.after(m, m1).tensor_scalar(lbc[:, :, :], lbv[:, :, :], -1.0, 1.0, ALU.mult, ALU.add))
        for e in (act, dve, pool):
            e.after(m_lb)

    def M(layer, part, who):
        return mod[:, layer, part * 8:part * 8 + 8, who]

    class Squares:
        pass

    ys = [ny[:, 0, :], ny[:, 1, :], nsq[:, 2, :], nsq[:, 3, :]]
    yfree = [None] * 4

    def squares_into(b, summed=(1, 2)):
        s = Squares()
        s.bank, s.summed, s.pairs, s.parts, s.added, s.root = b, summed, 0, [], 0, None
        return s

    def square(s, x, m):
        k = s.pairs
        s.pairs += 1
        place = (nsq[:, 0:2, :], nsq[:, 2:4, :], ny[:, :, :], nrr[:, :, :])[k]
        m = act.mark(act.after(m, yfree if k == 1 else None).activation(place, x, ACT.Square))
        if k in s.summed:
            m = pool.mark(pool.after(m, s.parts[0][1]).tensor_tensor(s.parts[0][0], s.parts[0][0], place, ALU.add))
            s.parts[0] = (s.parts[0][0], m)
        else:
            s.parts.append((place, m))

    def add_squares(s):
        for place, m in s.parts[s.added:]:
            pe.after(free[s.bank] if s.added == 0 else None, m)
            s.added += 1
            for k in range(2):
                ins = mm(bank[s.bank][:, 0:256], ones[:, :], place[:, k, :], start=s.added == 1 and k == 0,
                         stop=s.pairs == 4 and s.added == len(s.parts) and k == 1)
            s.last = pe.mark(ins)

    def one_over_rms(s):
        add_squares(s)
        m = act.mark(act.after(s.last).activation(
            nrt, bank[s.bank][:, 0:256], ACT.Sqrt, bias=epsc[:, 0:1], scale=1.0 / 1024))
        free[s.bank] = [m]
        s.root = dve.mark(dve.after(m).reciprocal(nrs, nrt))
        return s.root

    def table(f, m):
        act.mark(act.after(m, act.last).activation(epsc[:, 2:3], epsc[:, 0:1], f))

    def norm_steps(x, s, gain, shift, dst, dst_free, x_m=None):
        mr = s.root or one_over_rms(s)
        hi = [None] * 8
        for i in range(10):
            if i < 8:
                b, k = i, i % 4
                y = ys[k]
                m = dve.mark(dve.after(mr, yfree[k], x_m).scalar_tensor_tensor(
                    y, x[:, b, :], gain[:, b:b + 1], nrs, ALU.mult, ALU.mult))
                if b % 2:
                    m = act.mark(act.after(m).activation(y, y, ACT.Identity, bias=shift[:, b:b + 1]))
                    m1 = act.mark(act.after(m, dst_free).activation(dst.hi[:, b, :], y, ACT.Copy))
                else:
                    m1 = act.mark(act.after(m, dst_free).activation(dst.hi[:, b, :], y, ACT.Identity,
                                                                   bias=shift[:, b:b + 1]))
                hi[b] = dst.m_hi[b] = [m, m1]
            if i >= 2:
                b, k = i - 2, (i - 2) % 4
                if b % 2:
                    m2 = dve.mark(dve.after(hi[b], dst_free).tensor_tensor(
                        dst.lo[:, b, :], ys[k], dst.hi[:, b, :].bitcast(F32), ALU.subtract))
                else:
                    m2 = dve.mark(dve.after(hi[b], dst_free).scalar_tensor_tensor(
                        dst.lo[:, b, :], ys[k], shift[:, b:b + 1], dst.hi[:, b, :].bitcast(F32), ALU.add, ALU.subtract))
                yfree[k] = [hi[b][1], m2]
                dst.m[b] = hi[b] + [m2]
            yield

    def scaled(gain, dst, dst_free):
        def low(e):
            dst.m[e] = dst.m_hi[e] + [dve.mark(dve.after(dst.m_hi[e], dst_free).scalar_tensor_tensor(
                dst.lo[:, e, :], X[:, e, :], gain[:, e:e + 1], dst.hi[:, e, :].bitcast(F32), ALU.mult, ALU.subtract))]

        def block(e, m):
            if e % 4 == 1:
                k = e // 4
                m1 = act.mark(act.after(m, yfree[k]).activation(ys[k], X[:, e, :], ACT.Copy, scale=gain[:, e:e + 1]))
                m2 = act.mark(act.after(m1, dst_free).activation(dst.hi[:, e, :], ys[k], ACT.Copy))
                dst.m_hi[e] = [m2]
                m3 = pool.mark(pool.after(m2, dst_free).tensor_tensor(
                    dst.lo[:, e, :], ys[k], dst.hi[:, e, :].bitcast(F32), ALU.subtract))
                dst.m[e] = [m2, m3]
                yfree[k] = [m3]
            else:
                dst.m_hi[e] = [m, act.mark(act.after(m, dst_free).activation(
                    dst.hi[:, e, :], X[:, e, :], ACT.Copy, scale=gain[:, e:e + 1]))]
            if e and e % 4 != 2:
                low(e - 1)
            if e == 7:
                low(7)

        return block

    def mean_square(b, more, m, rows=None):
        found = mean_square_found
        found.clear()
        place = [nsq[:, 0:2, :], nsq[:, 2:4, :], more[:, 0:2, :], more[:, 2:4, :]]
        sq = [act.mark(act.after(m).activation(place[k], X[:, 2 * k:2 * k + 2, :], ACT.Square)) for k in range(4)]
        table(ACT.Sqrt, None)
        m1 = pool.mark(pool.after(sq[0], sq[1]).tensor_tensor(place[0], place[0], place[1], ALU.add))
        m2 = pool.mark(pool.after(sq[2], sq[3]).tensor_tensor(place[2], place[2], place[3], ALU.add))
        m1 = pool.mark(pool.after(m1, m2).tensor_tensor(place[0], place[0], place[2], ALU.add))
        yield
        pe.after(m1, free[b])
        for k in range(2):
            ins = mm(bank[b][:, 0:256], ones[:, :], nsq[:, k, :], start=k == 0, stop=k == 1)
        mp = pe.mark(ins)
        m = act.mark(act.after(mp).activation(nrt, bank[b][:, 0:256], ACT.Sqrt, bias=epsc[:, 0:1], scale=1.0 / 1024))
        free[b] = [m]
        if rows is not None:
            free[b] = [act.mark(act.after(mp).activation(rows, bank[b][0:8, 0:256], ACT.Identity, bias=epsc[0:8, 0:1],
                                                         scale=1.0 / 1024))]
        found.extend([dve.mark(dve.after(m).reciprocal(nrs, nrt)), free[b][0]])
        yield

    mean_square_found = []

    def run(main, *side):
        for _ in main:
            for s in side:
                next(s, None)

    def together(gens):
        gens = list(gens)
        while gens:
            gens = [g for g in gens if next(g, gens) is not gens]

    def timed(tiles_, gen):
        for n in range(1, tiles_[-1] + 4):
            if n in tiles_ or n == tiles_[-1] + 3:
                next(gen, None)
            yield

    def idle(n):
        for _ in range(n):
            yield

    def both(*gens):
        gens = list(gens)
        while gens:
            gens = [g for g in gens if next(g, gens) is not gens]
            yield

    def finish(gen):
        for _ in gen:
            pass

    class Mixer:
        pass

    def mixers(layer):
        a = Arena(nc, 'mix%d' % layer, BIG0 + 16 * KB, BIG1)
        s = Mixer()
        s.conv_free = None
        s.cg, s.u, s.cv = (a.take(k, [128, 4, 256]) for k in ('cg', 'u', 'cv'))
        s.KC, s.QC = a.take('KC', [128, 1024]), a.take('QC', [128, 1024])
        s.parts = nc.alloc_sbuf_tensor_at('mix%d_parts' % layer, [128, 2, 256], F32R, offset=a.at - 3 * KB)
        s.o = a.take('o', [128, 4, 256])
        hi, lo = a.take('hi', [128, 8, 256], F32R), a.take('lo', [128, 8, 256], F32R)
        s.att = a.take('att', [128, 2, 4, 256])
        pair = []
        for n in range(2):
            m = Mixer()
            m.shared = s
            m.V = a.take('V%d' % n, [128, 2, 512])
            m.qP, m.qS, m.kX, m.kY, m.ff, m.fb, m.g = (a.take('%s%d' % (k, n), [128, 4, 256])
                                                      for k in ('qP', 'qS', 'kX', 'kY', 'ff', 'fb', 'g'))
            m.h, m.mix = (Split(hi, lo), Split(hi, lo)) if n else (Split(h_hi, h_lo), Split(h_hi, h_lo))
            m.ready, m.finished, m.m_in, m.out = False, False, None, None
            pair.append(m)
        b = Arena(nc, 'mixc%d' % layer, G0, G0 + 2 * KB)
        s.four_in = b.take('four_in', [128, 4, 128])
        s.four = nc.alloc_sbuf_tensor_at('mix%d_four' % layer, [128, 4, 128], F32R, offset=b.at - 2 * KB)
        b = Arena(nc, 'mixs%d' % layer, G0 + 6 * KB, G0 + 11 * KB)
        s.S = b.take('S', [128, 2, 4, 128])
        s.masks = b.take('masks', [128, 256], U32)
        return pair

    def mixer_constants(s, deps):
        s.cm = [dma(s.four_in[:, :, :], t['four'], deps), dma(s.masks[:, :], t['masks'], deps)]

    def pairs(bk):
        return bk[:, :].rearrange('p (a b) -> p a b', a=2)

    def win(M_, layer, latent, only_state=False):
        s, h, tag = M_.shared, M_.h, 'w_in%d' % layer
        res = None
        for res in dense_rows(tag, [bank[2][:, :], bank[3][:, :]], h, free[2] + free[3]):
            if len(res) < 4:
                yield
        M_.mV = []
        for tt in range(2):
            m = act.mark(act.after(res).activation(M_.V[:, tt, :], bank[2 + tt][:, :], ACT.Copy))
            free[2 + tt] = [m]
            M_.mV.append(m)
        yield

        turn = [0]

        def two():
            b = turn[0] % 2
            turn[0] += 1
            first = free[b]
            m = None
            for n in range(2):
                m = dense(tag, pairs(bank[b])[:, n, :], h, first)
                yield b, m if n else None

        M_.mk = [[], []]
        M_.mf = [[], []]
        for d, (f, k) in enumerate(((M_.ff, M_.kX), (M_.fb, M_.kY))):
            for j in range(2):
                for b, m in two():
                    yield
                c = slice(2 * j, 2 * j + 2)
                m1 = act.mark(act.after(m).activation(f[:, c, :], pairs(bank[b]), ACT.Sigmoid))
                m2 = act.mark(act.after(m).activation(k[:, c, :], pairs(bank[b]), ACT.Sigmoid, scale=-1.0))
                free[b] = [m1, m2]
                for n in range(2):
                    e = 2 * j + n
                    lb, lc = lbv[:, layer, 4 * d + e:4 * d + e + 1], lbc[:, layer, 4 * d + e:4 * d + e + 1]
                    m = dve.mark(dve.after(m1).tensor_scalar(f[:, e, :], f[:, e, :], lc, lb, ALU.mult, ALU.add))
                    M_.mf[d].append(dve.mark(dve.after(m).tensor_scalar(f[:, e, :], f[:, e, :], F_FLOOR, None, ALU.max)))
                    M_.mk[d].append(dve.mark(dve.after(m2).tensor_scalar(k[:, e, :], k[:, e, :], lc, None, ALU.mult)))
        M_.mk, M_.mf = M_.mk[0] + M_.mk[1], M_.mf[0] + M_.mf[1]
        if only_state:
            M_.ready = True
            return
        M_.mq, M_.mg = [], []
        for j in range(2):
            for b, m in two():
                yield
            m = act.mark(act.after(m).activation(M_.qP[:, 2 * j:2 * j + 2, :], pairs(bank[b]), ACT.Copy))
            free[b] = [m]
            M_.mq.append(m)
        M_.ready = True
        for j in range(2):
            for b, m in two():
                yield
            m = act.mark(act.after(m).activation(M_.g[:, 2 * j:2 * j + 2, :], pairs(bank[b]), ACT.Silu))
            free[b] = [m]
            M_.mg.append(m)
        mc, mu, mv = [], [], [None] * 4
        for j in range(2):
            for b, m in two():
                yield
            m = act.mark(act.after(m, s.conv_free).activation(s.cg[:, 2 * j:2 * j + 2, :], pairs(bank[b]), ACT.Copy))
            free[b] = [m]
            mc.append(m)
        for j in range(2):
            for b, m in two():
                yield
            c = slice(2 * j, 2 * j + 2)
            m = dve.mark(dve.after(m, mc[j]).tensor_tensor(s.u[:, c, :], pairs(bank[b]), s.cg[:, c, :], ALU.mult))
            free[b] = [m]
            mu.append(m)
        for e in range(4):
            w = [P('conv_w', layer * 12 + 4 * i + e) for i in range(3)]
            u, v = s.u[:, e, :], s.cv[:, e, :]
            m = act.mark(act.after(mu[e // 2]).activation(v, u, ACT.Copy, scale=w[1]))
            if latent and e < 2:
                u2, v2 = u.rearrange('p (r c) -> p r c', c=64), v.rearrange('p (r c) -> p r c', c=64)
                steps = [(v2[:, :, 1:64], u2[:, :, 0:63]), (v2[:, :, 0:63], u2[:, :, 1:64])]
            else:
                k = 64 if latent else 1
                steps = [(v[:, k:256], u[:, 0:256 - k]), (v[:, 0:256 - k], u[:, k:256])]
            for (vo, ui), wi in zip(steps, (w[0], w[2])):
                m = dve.mark(dve.after(m, mu[e // 2]).scalar_tensor_tensor(vo, ui, wi, vo, ALU.mult, ALU.add))
            mv[e] = m
        mb = []
        for j in range(2):
            for b, m in two():
                yield
            c = slice(2 * j, 2 * j + 2)
            m = dve.mark(dve.after(m, mv[2 * j:2 * j + 2]).tensor_tensor(s.cv[:, c, :], pairs(bank[b]), s.cv[:, c, :],
                                                                     ALU.mult))
            free[b] = [m]
            mb.append(m)
        M_.m_in = pe.last
        for j in range(2):
            put(M_.mix, 4 + 2 * j, s.cv[:, 2 * j:2 * j + 2, :], mb[j], M_.m_in)
        s.conv_free = M_.mix.m[4] + M_.mix.m[6]

    def put(dst, b, src, m, wait):
        c = slice(b, b + 2)
        m1 = act.mark(act.after(m, wait).activation(dst.hi[:, c, :], src, ACT.Copy))
        m2 = dve.mark(dve.after(m, m1, wait).tensor_tensor(dst.lo[:, c, :], src, dst.hi[:, c, :].bitcast(F32), ALU.subtract))
        dst.m[b] = dst.m[b + 1] = [m1, m2]

    def level_view(a, B):
        v = a.rearrange('p (n w) -> p n w', w=2 * B)
        return v[:, :, 0:B], v[:, :, B:2 * B]

    def flat(a):
        return a[:, :, :].rearrange('p h t -> p (h t)')

    def scan(M_, need_q, before=None):
        s = M_.shared
        for e in engines:
            e.after(before)
        qP, qS, kX, kY, ff, fb = (flat(x) for x in (M_.qP, M_.qS, M_.kX, M_.kY, M_.ff, M_.fb))
        mk, mf = M_.mk, M_.mf
        if need_q:
            kd = dve.mark(dve.after(mk).tensor_tensor(s.KC[:, :], kX, kY, ALU.add))
            m1 = dve.mark(dve.after(mf, M_.mq).tensor_tensor(qS, qP, fb, ALU.mult))
            yield
            pe.after(kd, M_.mq, free[6], free[7])
            for tt in range(2):
                for e in range(4):
                    c = slice(e * 256 + tt * 128, e * 256 + tt * 128 + 128)
                    ins = mm(bank[6 + tt][:, e * 128:(e + 1) * 128], s.KC[:, c], qP[:, c])
            mp = pe.mark(ins)
            m_att = []
            for tt in range(2):
                m = dve.mark(dve.after(mp).tensor_tensor(
                    s.att[:, tt, :, tt * 128:tt * 128 + 128], bank[6 + tt][:, :].rearrange('p (h t) -> p h t', h=4),
                    ident[:, :].unsqueeze(1).to_broadcast([128, 4, 128]), ALU.mult))
                free[6 + tt] = [m]
                m_att.append(m)
            m2 = dve.mark(dve.after(mp, mf).tensor_tensor(qP, qP, ff, ALU.mult))
        B, lev = 1, 0
        kc_free = mp if need_q else None
        mx, my, ms, mp_ = mk, mk, m1 if need_q else None, m2 if need_q else None
        Tf, Tb, mt = ff, fb, mf
        spare = flat(s.o)
        while B <= 64:
            n = 1024 // (2 * B)
            p0, p1 = level_view(qP, B)
            s0, s1 = level_view(qS, B)
            x0, x1 = level_view(kX, B)
            y0, y1 = level_view(kY, B)
            Tf2, Tb2 = (Tf.rearrange('p (n w) -> p n w', w=2), Tb.rearrange('p (n w) -> p n w', w=2))
            f0, f1, b0, b1 = (T[:, :, i:i + 1].to_broadcast([128, n, B]) for T in (Tf2, Tb2) for i in range(2))
            to = (spare[:, 0:n], spare[:, 512:512 + n]) if lev % 2 == 0 else (ff[:, 0:n], fb[:, 0:n])
            mt2 = [pool.mark(pool.after(mt, mx, my, ms, mp_).tensor_tensor(
                o.unsqueeze(2), T[:, :, 0:1], T[:, :, 1:2], ALU.mult)) for o, T in zip(to, (Tf2, Tb2))]
            if need_q:
                c0, c1 = level_view(s.KC[:, :], B)
                d0, d1 = level_view(s.QC[:, :], B)
                cx, cy, cs, cp = (act.mark(act.after(m, kc_free).activation(o, i, ACT.Copy))
                                  for o, i, m in ((c0, x0, mx), (c1, y1, my), (d0, s0, ms), (d1, p1, mp_)))
                copied = [cx, cy, cs, cp]
            else:
                cx = cy = copied = None
            mx = dve.mark(dve.after(mt, mx, cx).tensor_tensor(x0, x0, f1, ALU.mult))
            my = dve.mark(dve.after(mt, my, cy).tensor_tensor(y1, y1, b0, ALU.mult))
            if need_q:
                ms = dve.mark(dve.after(ms, cs).tensor_tensor(s0, s0, b1, ALU.mult))
                mp_ = dve.mark(dve.after(mp_, cp).tensor_tensor(p1, p1, f0, ALU.mult))
            Tf, Tb, mt = to[0], to[1], mt2
            yield
            if need_q:
                pe.after(copied, free[6], free[7])
                for tt in range(2):
                    for e in range(4):
                        c = slice(e * 256 + tt * 128, e * 256 + tt * 128 + 128)
                        ins = mm(bank[6 + tt][:, e * 128:(e + 1) * 128], s.KC[:, c], s.QC[:, c])
                kc_free = pe.mark(ins)
                for tt in range(2):
                    m_att[tt] = dve.mark(dve.after(kc_free, m_att[tt]).copy_predicated(
                        s.att[:, tt, :, tt * 128:tt * 128 + 128],
                        s.masks[:, :].bitcast(U8)[:, lev * 128:(lev + 1) * 128].unsqueeze(1).to_broadcast([128, 4, 128]),
                        bank[6 + tt][:, :].rearrange('p (h t) -> p h t', h=4)))
                    free[6 + tt] = [m_att[tt]]
                yield
            B, lev = 2 * B, lev + 1
        mu = [mx, my, ms, mp_, mt]
        if need_q:
            pe.after(mu, free[6], free[7])
            for e in range(4):
                a, b = slice(e * 256, e * 256 + 128), slice(e * 256 + 128, e * 256 + 256)
                mm(bank[6][:, e * 128:(e + 1) * 128], kX[:, a], qP[:, b])
                ins = mm(bank[7][:, e * 128:(e + 1) * 128], kY[:, b], qS[:, a])
            mp = pe.mark(ins)
            mo = []
            for tt in range(2):
                c = slice(128 - tt * 128, 256 - tt * 128)
                m = act.mark(act.after(mp).activation(s.att[:, tt, :, c],
                                                            bank[6 + tt][:, :].rearrange('p (h t) -> p h t', h=4), ACT.Copy))
                free[6 + tt] = [m]
                mo.append(m)
            M_.m_att = m_att + mo
        v = lambda a: a.rearrange('p (h t) -> p h t', h=4)
        wide = lambda T, i: T.rearrange('p (h w) -> p h w', h=4)[:, :, i:i + 1].to_broadcast([128, 4, 128])
        M_.m_full = [
            dve.mark(dve.after(mu, mp if need_q else None).tensor_tensor(v(kX)[:, :, 0:128], v(kX)[:, :, 0:128], wide(Tf, 1), ALU.mult)),
            dve.mark(dve.after(mu).tensor_tensor(v(kY)[:, :, 128:256], v(kY)[:, :, 128:256], wide(Tb, 0), ALU.mult))]
        if need_q:
            M_.m_full += [
                dve.mark(dve.after(mu).tensor_tensor(v(qS)[:, :, 0:128], v(qS)[:, :, 0:128], wide(Tb, 1), ALU.mult)),
                dve.mark(dve.after(mu).tensor_tensor(v(qP)[:, :, 128:256], v(qP)[:, :, 128:256], wide(Tf, 0), ALU.mult))]
        M_.m_full += mu
        yield

    def states(M_, before=None):
        s = M_.shared
        for e in engines:
            e.after(before)
        ms = []
        kT = [s.KC, s.QC]
        for d, k in enumerate((M_.kX, M_.kY)):
            mt = []
            for tt in range(2):
                pe.after(M_.m_full, free[6 + tt])
                for e in range(4):
                    ins = nc.tensor.transpose(bank[6 + tt][:, e * 128:(e + 1) * 128], k[:, e, tt * 128:(tt + 1) * 128],
                                              ident[:, :])
                mp = pe.mark(ins)
                m = act.mark(act.after(mp).activation(kT[d][:, tt * 512:(tt + 1) * 512], bank[6 + tt][:, :], ACT.Copy))
                free[6 + tt] = [m]
                mt.append(m)
            yield
            pe.after(mt, M_.mV, free[4 + d])
            for e in range(4):
                for tt in range(2):
                    ins = mm(bank[4 + d][:, e * 128:(e + 1) * 128], kT[d][:, tt * 512 + e * 128:tt * 512 + (e + 1) * 128],
                             M_.V[:, tt, e * 128:(e + 1) * 128], start=tt == 0, stop=tt == 1)
            mp = pe.mark(ins)
            m = dve.mark(dve.after(mp).tensor_copy(s.S[:, d, :, :], bank[4 + d][:, :].rearrange('p (h v) -> p h v', h=4)))
            free[4 + d] = [m]
            ms.append(m)
            yield
        s.mS = ms
        for e in engines:
            e.after(ms, mp)

    def two_parts(x, hi, lo, m):
        m = dve.mark(dve.after(m).reciprocal(x, x))
        m = dve.mark(dve.after(m).tensor_copy(hi, x))
        return dve.mark(dve.after(m).tensor_tensor(lo, x, hi.bitcast(F32), ALU.subtract))

    def head_norm(o, mo, row_bank, wide_banks, gains, gate, mg, sq, rows, mix, four, mix_free):
        rt, hi, lo = rows
        pe.after(free[row_bank])
        for e in range(4):
            m = act.mark(act.after(mo[e // 2]).activation(sq[:, e, :], o[:, e, :], ACT.Square))
            pe.after(m)
            ins = mm(bank[row_bank][32 * e:32 * e + 32, 0:256], ones[:, 0:32], sq[:, e, :], tile_position=(0, 32 * e))
        mp = pe.mark(ins)
        m = act.mark(act.after(mp).activation(rt, bank[row_bank][:, 0:256], ACT.Sqrt, bias=epsc[:, 0:1], scale=1.0 / 128))
        free[row_bank] = [m]
        m = two_parts(rt, hi, lo, m)
        yield
        for j in range(2):
            b = wide_banks[j]
            pe.after(m, free[b])
            for n in range(2):
                e = 2 * j + n
                mm(pairs(bank[b])[:, n, :], four[:, e, :], hi, stop=False)
                ins = mm(pairs(bank[b])[:, n, :], four[:, e, :], lo, start=False)
            mp = pe.mark(ins)
            c = slice(2 * j, 2 * j + 2)
            if gains is None:
                ma = dve.mark(dve.after(mp, mo[j]).tensor_tensor(o[:, c, :], o[:, c, :], pairs(bank[b]), ALU.mult))
            else:
                for n in range(2):
                    e = 2 * j + n
                    ma = dve.mark(dve.after(mp, mo[j]).scalar_tensor_tensor(
                        o[:, e, :], o[:, e, :], gains[e], pairs(bank[b])[:, n, :], ALU.mult, ALU.mult))
            free[b] = [ma]
            while len(mg) <= j:
                yield
            ma = dve.mark(dve.after(ma, mg).tensor_tensor(o[:, c, :], o[:, c, :], gate[:, c, :], ALU.mult))
            put(mix, 2 * j, o[:, c, :], ma, mix_free())
            yield

    def mix_out(M_, state):
        s = M_.shared
        mo = []
        for j in range(2):
            b = 4 + j
            pe.after(M_.m_att, M_.mV, M_.m_full if state else None, s.mS if state else None, free[b])
            for n in range(2):
                e = 2 * j + n
                c = slice(e * 128, (e + 1) * 128)
                out = pairs(bank[b])[:, n, :]
                mm(out, M_.V[:, 0, c], s.att[:, 0, e, :], start=True, stop=False)
                ins = mm(out, M_.V[:, 1, c], s.att[:, 1, e, :], start=False, stop=not state)
                if state:
                    mm(out, s.S[:, 0, e, :], M_.qP[:, e, :], start=False, stop=False)
                    ins = mm(out, s.S[:, 1, e, :], M_.qS[:, e, :], start=False, stop=True)
            mp = pe.mark(ins)
            m = act.mark(act.after(mp).activation(s.o[:, 2 * j:2 * j + 2, :], pairs(bank[b]), ACT.Copy))
            free[b] = [m]
            mo.append(m)
            yield
        while M_.m_in is None:
            yield
        sq = s.KC[:, :].rearrange('p (h t) -> p h t', h=4)
        rows = s.QC[:, 0:256], s.parts[:, 0, :], s.parts[:, 1, :]
        yield from head_norm(s.o, mo, 6, (7, 6), None, M_.g, M_.mg, sq, rows, M_.mix, s.four, lambda: M_.m_in)
        M_.out = M_.mix.m[0] + M_.mix.m[2]

    def project(tag, src, halves, gate, s, xm, then=None):
        first = [free[j] for j in range(4)]

        def update(j, m):
            ready = []
            for n in range(2):
                e = 2 * j + n
                if gate is None:
                    mx = dve.mark(dve.after(m, xm).tensor_tensor(X[:, e, :], pairs(bank[j])[:, n, :], X[:, e, :], ALU.add))
                else:
                    mx = dve.mark(dve.after(m, xm).scalar_tensor_tensor(
                        X[:, e, :], pairs(bank[j])[:, n, :], gate[:, e:e + 1], X[:, e, :], ALU.mult, ALU.add))
                free[j] = [mx]
                ready.append((e, mx))
            X_now[0] = mx
            return ready

        def follow(ready):
            for e, mx in ready:
                if then is not None:
                    then(e, mx)
            if s is not None:
                square(s, X[:, ready[0][0]:ready[0][0] + 2, :], ready[1][1])

        for i, half in enumerate(halves):
            for j in range(4):
                yield
                ready = update(j - 1, m) if i and j else []
                x = take(tag)
                if ready:
                    follow(ready)
                pe.after(first[j], x.ready)
                for k in range(4):
                    b = 4 * half + k
                    pe.after(src.m[b])
                    for n in range(2):
                        c = slice(k * 256 + n * 128, k * 256 + n * 128 + 128)
                        w, v, out = x.hi[:, c], x.lo[:, c], pairs(bank[j])[:, n, :]
                        mm(out, w, src.his[b], start=i == 0 and k == 0 and n == 0, stop=False)
                        mm(out, w, src.los[b], start=False, stop=False)
                        ins = mm(out, v, src.his[b], start=False, stop=i == 1 and k == 3)
                m = pe.mark(ins)
                done(x, m)
        if s is not None:
            table(ACT.Sqrt, None)
        follow(update(3, m))

    X_now = [None]

    ua = Arena(nc, 'sel', G0, BIG0)
    i1T, i2T, g1T, g2T = (ua.take(k, [128, 256], F16) for k in ('i1T', 'i2T', 'g1T', 'g2T'))
    oneA = ua.take('oneA', [128, 2, 8, 128], F16)
    oneB1 = ua.take('oneB1', [128, 2, 8, 64], F16)
    oneB2 = ua.take('oneB2', [128, 2, 8, 64], F16)
    oneO = ua.take('oneO', [128, 8, 64], F16)
    acts = [nc.alloc_sbuf_tensor_at('act%d' % n, [128, 64, 256], F32, offset=BIG0 + n * 64 * KB) for n in range(2)]
    za = [Arena(nc, 'z0', H0, G0), Arena(nc, 'z1', BIG0 + 16 * KB, BIG0 + 32 * KB)]
    z_hi = [a.take('hi', [128, 4, 2, 256], F32R) for a in za]
    z_lo = [a.take('lo', [128, 4, 2, 256], F32R) for a in za]
    XB = nc.alloc_sbuf_tensor_at('XB', [128, 8, 256], F32, offset=BIG0 + 32 * KB)
    ra = Arena(nc, 'rank', R1, BIG1)
    skT = ra.take('skT', [128, 16, 128])
    qrT = ra.take('qrT', [128, 16, 256])
    SC = ra.take('SC', [128, 2, 16, 128])
    tv = ra.take('tv', [128, 2, 16, 16])
    ti = ra.take('ti', [128, 2, 16, 16], U32)
    tif = ra.take('tif', [128, 2, 16, 16])
    cand = ra.take('cand', [128, 2, 2, 256])
    top = ra.take('top', [128, 2, 8, 16])
    pos = ra.take('pos', [128, 2, 8, 16], U32)
    pab = ra.take('pab', [128, 2, 2, 8, 16], U32)
    paf = ra.take('paf', [128, 2, 2, 8, 16])
    hot = ra.take('hot', [128, 2, 2, 16, 16])
    sel = ra.take('sel', [128, 3, 2, 128])
    tsum = ra.take('tsum', [128, 2, 2, 8])
    iota_f = cols[:, 16:32]

    def ranks(j, msc):
        def best(vals, ids, src, deps, n):
            ms = [dve.mark(dve.after(deps).max(vals(q)[:, 0:8], src(q))) for q in range(n)]
            yield
            m1 = [dve.mark(dve.after(ms[q]).max_index(ids(q)[:, 0:8], vals(q)[:, 0:8], src(q))) for q in range(n)]
            yield
            m2 = [dve.mark(dve.after(m1[q]).match_replace(src(q), vals(q)[:, 0:8], src(q), LOWEST)) for q in range(n)]
            yield
            m3 = [dve.mark(dve.after(m2[q]).max(vals(q)[:, 8:16], src(q))) for q in range(n)]
            yield
            m4 = [dve.mark(dve.after(m3[q]).max_index(ids(q)[:, 8:16], vals(q)[:, 8:16], src(q))) for q in range(n)]
            yield m4

        at = lambda q: (q // 2, 2 * j + q % 2)
        for m in best(lambda q: tv[:, at(q)[0], at(q)[1], :], lambda q: ti[:, at(q)[0], at(q)[1], :],
                      lambda q: SC[:, at(q)[0], at(q)[1], :], msc, 4):
            yield
        mi = dve.mark(dve.after(m).tensor_copy(tif[:, :, 2 * j:2 * j + 2, :], ti[:, :, 2 * j:2 * j + 2, :]))
        cd = cand[:, j % 2, :, :]
        mc = [dve.mark(dve.after(m).tensor_tensor(
            cd[:, tt, :].rearrange('p (a b) -> p a b', a=16),
            tv[:, tt, 2 * j, :].unsqueeze(2).to_broadcast([128, 16, 16]),
            tv[:, tt, 2 * j + 1, :].unsqueeze(1).to_broadcast([128, 16, 16]), ALU.add)) for tt in range(2)]
        yield
        for m in best(lambda q: top[:, q, j, :], lambda q: pos[:, q, j, :], lambda q: cd[:, q, :], mc, 2):
            yield
        m1 = dve.mark(dve.after(m).tensor_scalar(pab[:, 0, :, j, :], pos[:, :, j, :], 4, None, ALU.logical_shift_right))
        m2 = dve.mark(dve.after(m).tensor_scalar(pab[:, 1, :, j, :], pos[:, :, j, :], 15, None, ALU.bitwise_and))
        mf = dve.mark(dve.after(m1, m2).tensor_copy(paf[:, :, :, j, :], pab[:, :, :, j, :]))
        for p in range(2):
            hp = hot[:, p, :, :, :]
            m = dve.mark(dve.after(mf).tensor_tensor(
                hp, paf[:, p, :, j, :].unsqueeze(3).to_broadcast([128, 2, 16, 16]),
                iota_f.unsqueeze(1).unsqueeze(1).to_broadcast([128, 2, 16, 16]), ALU.is_equal))
            yield
            m = dve.mark(dve.after(m, mi).tensor_tensor(
                hp, hp, tif[:, :, 2 * j + p, :].unsqueeze(2).to_broadcast([128, 2, 16, 16]), ALU.mult))
            yield
            m = dve.mark(dve.after(m).tensor_reduce(
                sel[:, p, :, 16 * j:16 * j + 16], hp, AX.X, ALU.add))
            yield
        U.ranked = m

    class Unit:
        pass

    U = Unit()

    def gates():
        ta = top[:, :, :, :]
        m = dve.mark(dve.after(U.ranked).tensor_tensor(
            paf[:, 0, :, :, :], ta, top[:, :, :, 0:1].to_broadcast([128, 2, 8, 16]), ALU.subtract))
        m = act.mark(act.after(m).activation(paf[:, 1, :, :, :], paf[:, 0, :, :, :], ACT.Exp))
        yield from idle(3)
        m1 = dve.mark(dve.after(m).tensor_reduce(tsum[:, 0, :, :], paf[:, 1, :, :, :], AX.X, ALU.add))
        m1 = dve.mark(dve.after(m1).reciprocal(tsum[:, 1, :, :], tsum[:, 0, :, :]))
        m1 = dve.mark(dve.after(m1).tensor_scalar(tsum[:, 1, :, :], tsum[:, 1, :, :], 4096.0, None, ALU.mult))
        m = dve.mark(dve.after(m1).tensor_tensor(
            sel[:, 2, :, :].rearrange('p t (h k) -> p t h k', h=8), paf[:, 1, :, :, :],
            tsum[:, 1, :, :].unsqueeze(3).to_broadcast([128, 2, 8, 16]), ALU.mult))
        yield from idle(4)
        pe.after(m, U.ranked, free[2], free[3])
        for n in range(3):
            for tt in range(2):
                c = (n % 2) * 256 + tt * 128
                ins = nc.tensor.transpose(bank[2 + n // 2][:, c:c + 128], sel[:, n, tt, :], ident[:, :])
        m = pe.mark(ins)
        U.off_scratch = [m, dve.last]
        yield from idle(4)
        a = act.mark(act.after(m, U.sel_free).activation(i1T[:, :], bank[2][:, 0:256], ACT.Copy))
        b = act.mark(act.after(m, U.sel_free).activation(i2T[:, :], bank[2][:, 256:512], ACT.Copy))
        c = act.mark(act.after(m, U.sel_free).activation(g1T[:, :], bank[3][:, 0:256], ACT.Copy))
        d = dve.mark(dve.after(m, c, U.sel_free).tensor_tensor(g2T[:, :], bank[3][:, 0:256], g1T[:, :], ALU.subtract))
        free[2] = [a, b]
        free[3] = [c, d]
        U.m_sel = [a, b, c, d]

    def queries(layer, h, before):
        ms = dma(skT[:, :, :], t['subkeys'][layer], before)
        for e in (act, dve):
            e.after(before)
        mq, U.todo = [None] * 8, []

        def score(j):
            b = 2 + j % 2
            pe.after(mq[j], ms, free[b])
            out = bank[b][:, :].rearrange('p (s t k) -> p s t k', s=2, t=2)
            for p in range(2):
                for tt in range(2):
                    ins = mm(out[:, p, tt, :], qrT[:, 2 * j + p, tt * 128:(tt + 1) * 128], skT[:, 2 * j + p, :])
            m = pe.mark(ins)
            m = act.mark(act.after(m).activation(
                SC[:, :, 2 * j:2 * j + 2, :].rearrange('p t s k -> p s t k'), out, ACT.Copy))
            free[b] = [m]
            U.todo.append(ranks(j, m))

        for j in range(8):
            first = free[j % 2]
            if j == 0:
                m = dense_pair('peer_wq%d' % layer, pairs(bank[0]), h, first)
                yield
            for n in range(2 if j else 0):
                m = dense('peer_wq%d' % layer, pairs(bank[j % 2])[:, n, :], h, first)
                yield
            mq[j] = act.mark(act.after(m).activation(qrT[:, 2 * j:2 * j + 2, :], pairs(bank[j % 2]), ACT.Copy))
            free[j % 2] = [mq[j]]
            if j:
                score(j - 1)
        score(7)
        U.queried = True

    def ranking():
        n = 0
        while n < 8:
            while len(U.todo) <= n:
                yield
            yield from U.todo[n]
            n += 1
        yield from gates()

    def first_half(layer, h, half, before):
        for i in range(32):
            b = i % 2
            first = free[b]
            for n in range(2):
                ends = [] if i == 31 and n else None
                m = dense('peer_u%d' % layer, pairs(bank[b])[:, n, :], h, first, ends)
                U.h_ends = ends
                yield

            def end(i=i, b=b, m=m):
                m = act.mark(act.after(m, before() if i == 0 else None).activation(
                    acts[half][:, 2 * i:2 * i + 2, :], pairs(bank[b]), ACT.Gelu))
                free[b] = [m]
                U.m_act[half] = m

            U.last_act = end
            if i < 31 or half == 0:
                end()

    def gating(half):
        used = U.hot_free
        zm = [None, None]
        dep = U.m_sel

        made = [None, None]

        def build(n):
            k, c = n % 2, slice(8 * n, 8 * n + 8)
            w = lambda a, x: a.unsqueeze(2).to_broadcast([128, 8, x])
            mA = dve.mark(dve.after(dep, used[k]).tensor_tensor(
                oneA[:, k, :, :], iota16[:, :].unsqueeze(1).to_broadcast([128, 8, 128]), w(i1T[:, c], 128), ALU.is_equal))
            mO = dve.mark(dve.after(dep, made).tensor_tensor(
                oneO[:, :, :], iota16[:, 64 * half:64 * half + 64].unsqueeze(1).to_broadcast([128, 8, 64]),
                w(i2T[:, c], 64), ALU.is_equal))
            m1 = dve.mark(dve.after(mO, used[k]).tensor_tensor(oneB1[:, k, :, :], oneO[:, :, :], w(g1T[:, c], 64), ALU.mult))
            m2 = dve.mark(dve.after(mO, used[k]).tensor_tensor(oneB2[:, k, :, :], oneO[:, :, :], w(g2T[:, c], 64), ALU.mult))
            made[:] = [m1, m2]
            return [mA, m1, m2]

        ready = build(0)
        yield
        for n in range(32):
            k, b = n % 2, 2 + n % 2
            pe.after(ready, free[b])
            for q in range(8):
                out = bank[b][:, 64 * q:64 * q + 64]
                mm(out, oneA[:, k, q, :], oneB1[:, k, q, :], start=True, stop=False)
                ins = mm(out, oneA[:, k, q, :], oneB2[:, k, q, :], start=False, stop=True)
            mp = pe.mark(ins)
            used[k] = mp
            if n < 31:
                ready = build(n + 1)
            yield
            z = acts[half][:, :, 8 * n:8 * n + 8]
            m = dve.mark(dve.after(mp, U.m_act[half]).tensor_tensor(
                z, z, bank[b][:, :].rearrange('p (t k) -> p k t', t=8), ALU.mult))
            free[b] = [m]
            U.m_z[half] = m
            yield

    def second_half(layer, half, accs):
        parts = {}
        zh, zl = z_hi[half], z_lo[half]
        z_free = list(U.z_free[half])

        def split_z(i):
            k = i % 4
            src = acts[half][:, 2 * i:2 * i + 2, :]
            f = z_free[k]
            a = act.mark(act.after(U.m_z[half], f).activation(zh[:, k, :, :], src, ACT.Copy))
            b = dve.mark(dve.after(U.m_z[half], a, f).tensor_tensor(zl[:, k, :, :], src, zh[:, k, :, :].bitcast(F32),
                                                                  ALU.subtract))
            parts[i] = [a, b]
            if i == 15:
                U.m_part = parts[i]

        split_z(0)
        split_z(1)
        U.m_out = []
        yield
        for i in range(32):
            if i + 2 < 32:
                split_z(i + 2)
            k = i % 4
            for n in range(2):
                x = take('peer_v%d' % layer)
                pe.after(x.ready, parts[i], accs)
                first, end = half == 0 and i == 0 and n == 0, half == 1 and i == 31 and n == 1
                for b in range(8):
                    w, v = x.hi[:, b * 128:(b + 1) * 128], x.lo[:, b * 128:(b + 1) * 128]
                    out = pairs(bank[4 + b // 2])[:, b % 2, :]
                    mm(out, w, zh[:, k, n, :], start=first and b % 2 == 0, stop=False)
                    mm(out, w, zl[:, k, n, :], start=False, stop=False)
                    ins = mm(out, v, zh[:, k, n, :], start=False, stop=end)
                    if end and b % 2:
                        m = pe.mark(ins)
                        U.m_out.append(m)
                if not end:
                    m = pe.mark(ins)
                done(x, m)
                yield
            z_free[k] = m
        U.m_split[half] = parts[31]
        U.m_v = m

    def chain(*gens):
        for g in gens:
            yield from g

    def peer(layer, who, h, before, x_src, x_m, side=(), closing=(), at_end=()):
        U.m_act, U.m_z, U.m_split = [None, None], [None, None], [None, None]
        U.z_free = [None, None]
        U.sel_free = before
        U.layer, U.who = layer, who
        side, at_end = iter(side), iter(at_end)
        share(1)
        q = queries(layer, h, before)
        next(q)
        rank = ranking()
        run(q, rank, rank)
        run(first_half(layer, h, 0, x_free), rank, rank, rank, side)
        finish(rank)
        finish(closing)
        share(1, 1, 1, 1, 0)
        U.hot_free = [[pe.last, act.last]] * 2
        g0, g1 = gating(0), gating(1)
        run(first_half(layer, h, 1, lambda: U.off_scratch), more(g0))
        finish(g0)
        U.z_free[0] = U.h_ends
        v0 = second_half(layer, 0, free[4] + free[5] + free[6] + free[7])
        next(v0)
        U.last_act()
        g1 = more(g1)
        v1 = second_half(layer, 1, [])
        for _ in range(62):
            next(v0)
            next(g1, None)
        finish(g1)
        U.z_free[1] = [U.m_part] * 4
        next(v1)
        finish(v0)
        U.h_free = U.m_v
        U.mx = dma(X[:, :, :], x_src, U.m_split[0], x_m)
        share(1, 1, 0)
        run(v1, at_end)
        finish(at_end)

    def more(gen):
        n = 0
        for _ in gen:
            n += 1
            if n % 9:
                yield

    def peer_end(s):
        table(ACT.Sqrt, None)
        mg = dve.mark(dve.after(X_now[0]).tensor_scalar(gate_s[:, :], M(U.layer, 5, U.who), 2.0 ** -12, None, ALU.mult))
        for e in range(8):
            b = 4 + e // 2
            m = dve.mark(dve.after(U.m_out[e // 2], U.mx, mg).scalar_tensor_tensor(
                X[:, e, :], pairs(bank[b])[:, e % 2, :], gate_s[:, e:e + 1], X[:, e, :], ALU.mult, ALU.add))
            free[b] = [m]
            X_now[0] = m
            if s is not None and e % 2:
                square(s, X[:, e - 1:e + 1, :], m)
                if not s.summed:
                    add_squares(s)
            yield

    def scratch(name):
        return nc.dram_tensor(name, [128, 8, 256], F32).ap()

    def modulated():
        for e in engines:
            e.after(list(mod_m.values()))

    def first_norm(x, s, layer, who, dst, dst_free, mx):
        return norm_steps(x, s, gain1[:, layer, who, :], M(layer, 0, who), dst, dst_free, mx)

    def second_norm(x, s, layer, who, dst, dst_free, mx):
        return norm_steps(x, s, gain2[:, layer, who, :], M(layer, 3, who), dst, dst_free, mx)

    def other_norm(how, src, layer, who, dst, dst_free, deps):
        mx = dma(XB[:, :, :], src, deps())
        for _ in range(4):
            yield
        s = squares_into(2 if dst_free else 6, (1, 2, 3))
        for k in range(4):
            square(s, XB[:, 2 * k:2 * k + 2, :], mx)
            yield
        yield from idle(2)
        yield from how(XB, s, layer, who, dst, dst_free and dst_free(), mx)
        XB_now[0] = dst.m[6] + dst.m[7]

    def store(dst, *deps):
        m = dma(dst, X[:, :, :], X_now[0], *deps)
        x_stores.append(m)
        return m

    def x_free():
        return x_stores + [X_now[0]]

    XB_now, x_stores = [None], []
    conditions(None)
    mx = m_ctx
    mc_, mr_ = mixers(0)
    sh = mc_.shared
    bounds()
    m = modulation(0, range(4), 4, 5)
    for n in range(8):
        next(m)
        if n == 3:
            s = squares_into(6, (1, 2, 3))
            for k in range(4):
                square(s, X[:, 2 * k:2 * k + 2, :], mx)
            one_over_rms(s)
    share(0)
    ahead()
    finish(m)
    modulated()
    share(1)
    finish(first_norm(X, s, 0, 1, mc_.h, None, mx))
    late = modulation(0, range(4, 7), 2, 3)

    def state_chain(m, only_state, before):
        mixer_constants(m.shared, U.consts_after)
        while not m.ready:
            yield
        s = m.shared
        s.cm.append(act.mark(act.after(s.cm).activation(s.four[:, :, :], s.four_in[:, :, :], ACT.Copy)))
        for e in (pe, dve):
            e.after(m.shared.cm)
        yield from scan(m, not only_state, before and before[0])
        yield from states(m)
        if not only_state:
            yield from mix_out(m, False)
        m.finished = True

    def latent_chain(m, context):
        while not (m.ready and context.finished):
            yield
        yield from scan(m, True, (context.out or []) + [context.shared.mS])
        yield from mix_out(m, True)

    share(0, 1)
    U.consts_after = None
    side = state_chain(mc_, False, XB_now)
    run(win(mc_, 0, False), other_norm(first_norm, t['x'], 0, 0, mr_.h, None, lambda: None), side, timed(MOD_IN, late))
    finish(late)
    late = modulation(0, range(7, 10), 2, 3)
    late_x = latent_chain(mr_, mc_)
    run(win(mr_, 0, True), side, timed(MOD_IN, late), late_x)
    finish(late)
    finish(side)
    modulated()
    s = squares_into(6)
    run(project('w_out0', mc_.mix, (1, 0), M(0, 2, 1), s, mx), late_x)
    mp = pe.last
    xc1, x1, xc2, x2 = (scratch(k) for k in ('xc1', 'x1', 'xc2', 'x2'))
    m_xc1 = store(xc1)
    h = Split(h_hi, h_lo)
    finish(late_x)
    side = second_norm(X, s, 0, 1, h, mp, X_now[0])
    mx, before = [], marks()
    p = project('w_out0', mr_.mix, (1, 0), M(0, 2, 0), None, mx)
    for _ in range(5):
        next(p)
        for _ in range(4):
            next(side, None)
        if not mx and h.m[7]:
            mx.append(dma(X[:, :, :], t['x'], h.m[6], h.m[7], m_xc1))
    finish(p)
    m_x1 = store(x1)

    hx = Split(h_hi, h_lo)
    row_x, row_c = (nc.alloc_sbuf_tensor_at('row%d' % n, [128, 1024], F32, offset=G0 + 4 * KB * n) for n in range(2))

    def places(name, at, n):
        return [nc.alloc_sbuf_tensor_at(name + str(i), [128, 1024], F32, offset=at + 4 * KB * i) for i in range(n)]

    def first_rows():
        yield from idle(10)
        rows = [(0, row_x, condition_row(row_x, 'c_row', U.m_z[1])), (1, row_c, condition_row(row_c, 'c_ctx_row', U.m_z[1]))]
        blocks = [(0, b) for b in range(40, 48)] + [(1, b) for b in range(16)]
        yield from modulation_rows(0, blocks, rows, places('rowsA', BIG0 + 48 * KB, 4), places('spareA', BIG0 + 40 * KB, 2),
                                   U.m_split[0], 2)
        for who in range(2):
            modulation_end(0, 40, 48, who)
            modulation_end(1, 0, 16, who)
        yield

    def last_rows():
        yield from idle(10)
        rows = [(0, row_x, condition_row(row_x, 'c_row', U.m_z[1]))]
        yield from modulation_rows(24, [(1, b) for b in range(16, 48)], rows, places('rowsB', H0, 4),
                                   places('spareB', BIG0 + 56 * KB, 2), [U.h_free] + U.m_split[0], 2)
        modulation_end(1, 16, 48, 0)
        yield

    peer(0, 1, h, before, xc1, m_xc1, (), (),
         both(other_norm(second_norm, x1, 0, 0, hx, lambda: U.h_free, lambda: U.m_split[0] + [m_x1]), first_rows()))
    m_rows = dve.last
    finish(peer_end(None))
    m_xc2 = store(xc2)
    mr_, mc_ = mixers(1)
    peer(0, 0, hx, U.m_split[1] + [U.m_v, m_rows], x1, m_x1, (), (),
         both(other_norm(first_norm, xc2, 1, 1, mc_.h, lambda: U.m_split[0], lambda: U.m_split[0] + [m_xc2]), last_rows()))

    def latent_norm():
        s = squares_into(4, (1, 2, 3))
        yield from peer_end(s)
        yield from idle(2)
        yield from first_norm(X, s, 1, 0, mr_.h, U.h_free, X_now[0])

    share(0, 1)
    side = latent_norm()
    run(win(mc_, 1, False, True), side)
    finish(side)
    U.consts_after = U.m_out
    side = state_chain(mc_, True, None)
    late_x = latent_chain(mr_, mc_)
    run(win(mr_, 1, True), side, late_x)
    finish(side)
    s = squares_into(6)
    p = project('w_out1', mr_.mix, (1, 0), M(1, 2, 0), s, X_now[0])
    for _ in range(5):
        next(p)
        next(late_x, None)
    finish(late_x)
    before = marks()
    finish(p)
    m_x2 = store(x2)
    finish(second_norm(X, s, 1, 0, h, pe.last, X_now[0]))
    peer(1, 0, h, before, x2, m_x2)
    s = squares_into(4, ())
    finish(peer_end(s))

    ga = Arena(nc, 'tab', G0, BIG0)
    cosr, sinr, cosm, sinm, tabq = (ga.take(k, [128, 256]) for k in ('cosr', 'sinr', 'cosm', 'sinm', 'tabq'))
    permr, permm = ga.take('permr', [128, 128]), ga.take('permm', [128, 128])
    mask = ga.take('mask', [128, 384])
    cols2 = ga.take('cols2', [128, 192])
    scol, rscol = ga.take('scol', [128, 16]), ga.take('rscol', [128, 2])
    mstat = ga.take('mstat', [128, 4, 16])
    rowsA, rowsB = (ga.take(k, [8, 256]) for k in ('rowsA', 'rowsB'))
    a = Arena(nc, 'two', BIG0 + 16 * KB, BIG1)
    dec = a.take('dec', [128, 4, 384])
    spread = a.take('spread', [8, 128])
    four_in, eight_in = a.take('four_in', [128, 4, 128]), a.take('eight_in', [128, 8, 128])
    four = nc.alloc_sbuf_tensor_at('two_four', [128, 4, 128], F32R, offset=a.at - 6 * KB)
    eight = nc.alloc_sbuf_tensor_at('two_eight', [128, 8, 128], F32R, offset=a.at - 4 * KB)
    w_uq = a.take('uq', [128, 2, 1024])
    w_ukv = a.take('ukv', [128, 1024])
    rv = a.take('rv', [128, 2, 512])
    rraw = a.take('rraw', [128, 2, 2, 256])
    ret_parts = nc.alloc_sbuf_tensor_at('ret_parts', [128, 2, 256], F32R, offset=a.at - 3 * KB)
    lat = a.take('lat', [128, 4, 256])
    tmp = a.take('tmp', [128, 2, 2, 256])
    mla_hi = nc.alloc_sbuf_tensor_at('mla_hi', [128, 4, 256], F32R, offset=a.at - 8 * KB)
    mla_lo = nc.alloc_sbuf_tensor_at('mla_lo', [128, 4, 256], F32R, offset=a.at - 4 * KB)
    rk, rq, ry, rg = (a.take(k, [128, 4, 256]) for k in ('rk', 'rq', 'ry', 'rg'))
    ret_hi = nc.alloc_sbuf_tensor_at('ret_hi', [128, 4, 256], F32R, offset=a.at - 16 * KB)
    ret_lo = nc.alloc_sbuf_tensor_at('ret_lo', [128, 4, 256], F32R, offset=a.at - 12 * KB)
    rP = a.take('rP', [128, 4, 384])
    rsq = rP[:, :, 0:256]
    rows_l = a.take('rows_l', [8, 256])
    rows_k, rows_q = (a.take(k, [128, 2, 256]) for k in ('rows_k', 'rows_q'))
    parts_k, parts_q = (nc.alloc_sbuf_tensor_at(k, [128, 2, 256], F32R, offset=a.at - o)
                        for k, o in (('parts_k', 4 * KB), ('parts_q', 2 * KB)))
    qf, kf = a.take('qf', [128, 8, 256]), a.take('kf', [128, 8, 256])
    mv = a.take('mv', [128, 2, 512])
    at = a.at
    mS = a.take('S', [128, 8, 384])
    PT = a.take('PT', [128, 8, 384])
    fa = Arena(nc, 'ffn', at, BIG1)
    fg, fs = fa.take('g', [128, 2, 2, 256]), fa.take('s', [128, 2, 256])
    f_hi, f_lo = fa.take('hi', [128, 2, 256], F32R), fa.take('lo', [128, 2, 256], F32R)
    nsq2 = fa.take('sq', [128, 4, 256])
    post = fa.take('pos', [128, 256], I32)
    cosn, sinn, tabg, rowsX = nsq[:, 0, :], nsq[:, 1, :], nsq[:, 2, :], nsq[0:8, 3, :]
    start = marks()
    m_tab = [dma(post[:, :], t['positions'].partition_broadcast(128), start), dma(cols2[:, :], t['cols2'])]
    m_fix = [dma(permr[:, :], t['perms'][:, 0:128]), dma(permm[:, :], t['perms'][:, 128:256]),
             dma(mask[:, :], t['mask']), dma(spread[:, :], t['spread']), dma(dec[:, :, :], t['decay']),
             dma(four_in[:, :, :], t['four']), dma(eight_in[:, :, :], t['eight'])]
    wide = lambda x: x.unsqueeze(1).to_broadcast([128, 2, 256])

    def tables(inv, sin, cos):
        r, k = lat[:, 0, :], lat[:, 1, :]
        big = 1.5 * 2.0 ** 23
        m = dve.mark(dve.after(m_tab).tensor_copy(k, post[:, :]))
        m = dve.mark(dve.after(m).tensor_scalar(r, k, inv, None, ALU.mult))
        yield
        m = dve.mark(dve.after(m).tensor_scalar(k, r, float(np.float32(0.5 / np.pi)), big, ALU.mult, ALU.add))
        m = dve.mark(dve.after(m).tensor_scalar(k, k, big, None, ALU.subtract))
        yield
        rest = 2 * np.pi
        for bits in (5, 14, 24, 34, 60):
            part = float(np.floor(rest * 2.0 ** bits) / 2.0 ** bits) if bits < 60 else float(rest)
            rest -= part
            m = dve.mark(dve.after(m).scalar_tensor_tensor(r, k, -part, r, ALU.mult, ALU.add))
            yield
        top = float(np.nextafter(np.float32(np.pi), np.float32(0)))
        m = dve.mark(dve.after(m).tensor_scalar(r, r, top, -top, ALU.min, ALU.max))
        m1 = act.mark(act.after(m).activation(sin, r, ACT.Sin))
        m = dve.mark(dve.after(m).scalar_tensor_tensor(k, r, -1.0, r, ALU.mult, ALU.max))
        m2 = act.mark(act.after(m).activation(cos, k, ACT.Sin, bias=epsc[:, 1:2], scale=-1.0))
        dve.after(m1, m2)
        yield

    def sines():
        yield from tables(cols2[:, 48:49], sinr[:, :], cosr[:, :])
        yield from tables(cols2[:, 49:50], sinm[:, :], cosm[:, :])
        m = dve.mark(nc.vector.tensor_copy(tabq[0:96, :], cosm[0:96, :]))
        m1 = dve.mark(nc.vector.tensor_scalar(tabq[96:128, :], sinm[96:128, :], cols2[96:128, 50:51], None, ALU.mult))
        dve.after(m, m1)
        for x, x_in in ((four, four_in), (eight, eight_in)):
            m_fix.append(act.mark(act.after(m_fix).activation(x[:, :, :], x_in[:, :, :], ACT.Copy)))
        yield

    def ffn(tag, src, m_x, then, *side):
        f_free, ma, ends = [None, None], {}, []
        fg_free = [None, None]
        accs = free[4] + free[5] + free[6] + free[7]
        total = mean_square(3, nsq2, m_x)
        made, gate = {}, {}

        def gated(f):
            k = f % 2
            m = dve.mark(dve.after(made[f], mean_square_found, fg_free[k]).tensor_tensor(
                fg[:, k, :, :], pairs(bank[f % 4]), wide(nrs), ALU.mult))
            free[f % 4] = [m]
            m1 = act.mark(act.after(m).activation(fs[:, k, :], fg[:, k, 0, :], ACT.Silu))
            gate[f] = pool.mark(pool.after(m, m1).tensor_tensor(fs[:, k, :], fs[:, k, :], fg[:, k, 1, :], ALU.mult))

        def parts(f):
            k = f % 2
            m1 = act.mark(act.after(gate[f], f_free[k]).activation(f_hi[:, k, :], fs[:, k, :], ACT.Copy))
            m2 = dve.mark(dve.after(gate[f], m1, f_free[k]).tensor_tensor(
                f_lo[:, k, :], fs[:, k, :], f_hi[:, k, :].bitcast(F32), ALU.subtract))
            ma[f] = fg_free[k] = [m1, m2]

        for f in range(24):
            if f < 22:
                b = f % 4
                first = free[b]
                if f == 0:
                    made[f] = dense_pair(tag, pairs(bank[b]), src, first)
                else:
                    dense(tag, pairs(bank[b])[:, 0, :], src, first)
                    next(total, None)
                    made[f] = dense(tag, pairs(bank[b])[:, 1, :], src, first)
            if f == 0:
                next(total)
            if f in (0, 23):
                pass
            elif f == 22:
                parts(21)
            else:
                gated(f - 1)
                parts(f - 1)
                if f == 21:
                    gated(21)
            if f >= 2:
                k = f % 2
                x = take(tag)
                pe.after(x.ready, ma[f - 2], accs)
                for b in range(8):
                    w, v = x.hi[:, b * 128:(b + 1) * 128], x.lo[:, b * 128:(b + 1) * 128]
                    out = pairs(bank[4 + b // 2])[:, b % 2, :]
                    mm(out, w, f_hi[:, k, :], start=f == 2 and b % 2 == 0, stop=False)
                    mm(out, w, f_lo[:, k, :], start=False, stop=False)
                    ins = mm(out, v, f_hi[:, k, :], start=False, stop=f == 23)
                    if f == 23 and b % 2:
                        ends.append(pe.mark(ins))
                f_free[k] = ends[-1] if ends else pe.mark(ins)
                done(x, f_free[k])
            for g in side:
                next(g, None)
        for e in range(8):
            b = 4 + e // 2
            m = dve.mark(dve.after(ends[e // 2]).scalar_tensor_tensor(
                X[:, e, :], pairs(bank[b])[:, e % 2, :], 0.5, X[:, e, :], ALU.mult, ALU.add))
            free[b] = [m]
            if then is not None:
                then(e, m)
        return m

    def win2(l, src, R, m_x):
        tag = 'w_in2%d' % l
        total = mean_square(3, nsq2, m_x, rowsX)
        share(0)
        m = dense_pair(tag, pairs(bank[0]), src, free[0])
        split()
        next(total)
        yield
        m1 = act.mark(act.after(m).activation(lat[:, 0, :], pairs(bank[0])[:, 0, :], ACT.Copy, scale=P('kv_lat', l)))
        m2 = act.mark(act.after(m).activation(lat[:, 1, :], pairs(bank[0])[:, 1, :], ACT.Copy))
        m3 = act.mark(act.after(m).activation(tmp[:, 0, :, :], pairs(bank[0]), ACT.Square))
        free[0] = [m3]
        R.kv = [m1, m2, m3]
        first = free[1]
        for n in range(2):
            for m in dense_steps(tag, pairs(bank[1])[:, n, :], src, first):
                if n and m:
                    next(total)
                yield
        R.rms, R.m_rows = mean_square_found
        share(0, 0, 1)
        ms = [act.mark(act.after(m).activation(lat[:, 2 + n, :], pairs(bank[1])[:, n, :], ACT.Copy,
                                               scale=P('q_lat', 2 * l + n))) for n in range(2)]
        m3 = act.mark(act.after(m).activation(tmp[:, 1, :, :], pairs(bank[1]), ACT.Square))
        free[1] = [m3]
        R.q = ms + [m3]
        mt = [dve.mark(dve.after(R.rms).tensor_tensor(o, i, nrs, ALU.mult))
              for o, i in ((cosn, cosr[:, :]), (sinn, sinr[:, :]))]
        dve.after(mt)
        raw_free = [None, None]
        late = []

        def rotate(dst, j, n, m, out):
            pe.after(m, free[2 + n])
            mp = pe.mark(mm(bank[2 + n][:, :], permr[:, :], rraw[:, n, :, :].rearrange('p a b -> p (a b)')))
            c = slice(2 * j, 2 * j + 2)
            ma = dve.mark(dve.after(m).tensor_tensor(dst[:, c, :], rraw[:, n, :, :], wide(cosn), ALU.mult))
            mb = dve.mark(dve.after(mp, ma).tensor_tensor(rraw[:, n, :, :], pairs(bank[2 + n]), wide(sinn), ALU.mult))
            free[2 + n] = [mb]
            raw_free[n] = dve.mark(dve.after(ma, mb).tensor_tensor(dst[:, c, :], dst[:, c, :], rraw[:, n, :, :], ALU.add))
            out.append(raw_free[n])

        for dst, out in ((rk, R.mk), (rq, R.mq)):
            for j in range(2):
                first = free[j]
                for n in range(2):
                    for m in dense_steps(tag, pairs(bank[j])[:, n, :], src, first):
                        if n == 0 and m and late:
                            rotate(*late.pop(0))
                        yield
                m = act.mark(act.after(m, raw_free[j]).activation(rraw[:, j, :, :], pairs(bank[j]), ACT.Copy))
                free[j] = [m]
                late.append((dst, j, j, m, out))
        pe.after(R.rms, free[0])
        for tt in range(2):
            ins = mm(bank[0][:, 2 * tt:2 * tt + 1], nrs[0:8, tt * 128:(tt + 1) * 128], ident[0:8, 0:1])
        mp = pe.mark(ins)
        mr = act.mark(act.after(mp).activation(rscol[:, :], bank[0][:, 0:4:2], ACT.Copy))
        free[0] = [mr]
        rows = dense_rows(tag, [bank[0][:, :], bank[1][:, :]], src, free[0] + free[1])
        for res in rows:
            if late:
                rotate(*late.pop(0))
            if len(res) < 4:
                yield
        for tt in range(2):
            m = act.mark(act.after(res, mr).activation(rv[:, tt, :], bank[tt][:, :], ACT.Copy, scale=rscol[:, tt:tt + 1]))
            free[tt] = [m]
            R.mv.append(m)
        yield
        for j in range(2):
            first = free[j]
            for n in range(2):
                for m in dense_steps(tag, pairs(bank[j])[:, n, :], src, first):
                    yield
            c = slice(2 * j, 2 * j + 2)
            m = dve.mark(dve.after(m).tensor_tensor(rg[:, c, :], pairs(bank[j]), wide(nrs), ALU.mult))
            free[j] = [m]
            R.mg.append(act.mark(act.after(m).activation(rg[:, c, :], rg[:, c, :], ACT.Silu)))
        R.m_in = pe.last

    def retention(l, R, mix):
        while len(R.mq) < 2:
            yield
        mP = []
        for e in range(4):
            b = 2 + e % 2
            pe.after(R.mk[e // 2], R.mq[e // 2], free[b])
            mm(bank[b][:, 0:256], rk[:, e, 0:128], rq[:, e, :])
            mp = pe.mark(mm(bank[b][:, 256:384], rk[:, e, 128:256], rq[:, e, 128:256]))
            m = dve.mark(dve.after(mp).tensor_tensor(rP[:, e, :], bank[b][:, 0:384], dec[:, e, :], ALU.mult))
            free[b] = [m]
            mP.append(m)
            if e % 2:
                yield
        while len(R.mv) < 2:
            yield
        mo = []
        for j in range(2):
            b = 2 + j
            pe.after(mP[2 * j:2 * j + 2], R.mv, free[b])
            for n in range(2):
                e = 2 * j + n
                out, c = pairs(bank[b])[:, n, :], slice(e * 128, (e + 1) * 128)
                mm(out, rv[:, 0, c], rP[:, e, 0:256], start=True, stop=False)
                ins = mm(out[:, 128:256], rv[:, 1, c], rP[:, e, 256:384], start=False, stop=True)
            mp = pe.mark(ins)
            m = act.mark(act.after(mp).activation(ry[:, 2 * j:2 * j + 2, :], pairs(bank[b]), ACT.Copy))
            free[b] = [m]
            mo.append(m)
            yield
        gains = [P('ret_norm', 4 * l + e) for e in range(4)]
        act.after(mp)
        yield from head_norm(ry, mo, 2, (3, 2), gains, rg, R.mg, rsq, (rraw[:, 0, 0, :], ret_parts[:, 0, :], ret_parts[:, 1, :]),
                             mix, four, lambda: mP)
        R.held = True

    def strips(b, j, k, squares):
        for n in range(2):
            e, o = 2 * j + n, 16 - 16 * (j // 2)
            s = slice(32 * (e % 4), 32 * (e % 4) + 32)
            ins = mm(bank[b][s, 0:256], cols2[0:k, o:o + 32], squares[:, n, :], start=j < 2, stop=False, tile_position=(0, s.start))
        return pe.mark(ins)

    def picked(out, pick, parts):
        mm(out, pick, parts[:, 1, :], stop=False)
        return mm(out, pick, parts[:, 0, :], start=False)

    def roots(b, rows, parts, row):
        mp = pe.mark(mm(bank[b][:, 0:256], eps128, row, start=False))
        m = act.mark(act.after(mp).activation(rows[:, 0, :], bank[b][:, 0:256], ACT.Sqrt))
        free[b] = [m]
        return two_parts(rows[:, 0, :], parts[:, 1, :], parts[:, 0, :], m)

    eps8, eps128 = cols2[0:8, 52:60], cols2[0:8, 52:180]

    def latents(l, R):
        while R.rms is None:
            yield
        pe.after(R.kv, R.m_rows, free[6])
        mm(bank[6][0:8, 0:256], cols[:, 41:49], tmp[:, 0, 0, :], stop=False)
        mm(bank[6][0:8, 0:256], cols[:, 49:57], tmp[:, 0, 1, :], start=False, stop=False)
        R.tmp_free = pe.mark(mm(bank[6][0:8, 0:256], eps8, rowsX, start=False))
        R.m_rowA = act.mark(act.after(R.tmp_free).activation(rowsA[:, :], bank[6][0:8, 0:256], ACT.Copy))
        m = act.mark(act.after(R.tmp_free).activation(rows_l[:, :], bank[6][0:8, 0:256], ACT.Sqrt))
        free[6] = [m]
        m = dve.mark(dve.after(m).reciprocal(rows_l[:, :], rows_l[:, :]))
        yield
        pe.after(m, free[7])
        mm(bank[7][:, 0:256], spread[:, :], rows_l[:, :])
        for tt in range(2):
            ins = mm(bank[7][:, 256 + 8 * tt:264 + 8 * tt], rows_l[:, tt * 128:(tt + 1) * 128], ident[0:8, 0:8])
        mp = pe.mark(ins)
        R.m_scol = act.mark(act.after(mp).activation(scol[:, :], bank[7][:, 256:272], ACT.Copy))
        m = dve.mark(dve.after(R.m_scol, R.kv).scalar_tensor_tensor(
            lat[:, 1, :], lat[:, 1, :], P('kn', l), bank[7][:, 0:256], ALU.mult, ALU.mult))
        free[7] = [m]
        yield
        pe.after(m, free[7])
        mp = pe.mark(mm(bank[7][:, 0:256], permm[:, :], lat[:, 1, :]))
        mb = dve.mark(dve.after(mp).tensor_tensor(nrt, bank[7][:, 0:256], sinm[:, :], ALU.mult))
        free[7] = [mb]
        ma = dve.mark(dve.after(mp, m).tensor_tensor(lat[:, 1, :], lat[:, 1, :], cosm[:, :], ALU.mult))
        m = dve.mark(dve.after(ma, mb).tensor_tensor(lat[:, 1, :], lat[:, 1, :], nrt, ALU.add))
        yield
        R.m_kr = act.mark(act.after(m).activation(
            kf[64:128, :, :], lat[64:128, 1, :].unsqueeze(1).to_broadcast([64, 8, 256]), ACT.Copy))

    def keys(l, R, mw):
        while R.m_rowA is None:
            yield
        pe.after(mw)
        row_first, used = free[5], R.tmp_free
        mk = []
        for j in range(4):
            pe.after(R.kv, free[4])
            for n in range(2):
                e = 2 * j + n
                ins = mm(pairs(bank[4])[0:64, n, :], w_ukv[:, e * 64:(e + 1) * 64], lat[:, 0, :])
            mp = pe.mark(ins)
            m2 = act.mark(act.after(mp, used).activation(tmp[0:64, 0, :, :], pairs(bank[4])[0:64, :, :], ACT.Square))
            m1 = dve.mark(dve.after(m2).tensor_scalar(kf[0:64, 2 * j:2 * j + 2, :], pairs(bank[4])[0:64, :, :],
                                                      P('kn', l)[0:64, :], None, ALU.mult))
            free[4] = [m1]
            mk.append(m1)
            yield
            pe.after(m2, row_first)
            used = strips(5, j, 64, tmp[0:64, 0, :, :])
        pe.after(R.m_rowA)
        m = roots(5, rows_k, parts_k, rowsA[:, :])
        yield
        for tt in range(2):
            pe.after(R.kv, free[4])
            mp = pe.mark(mm(bank[4][:, :], lat[:, 0, tt * 128:(tt + 1) * 128], w_ukv[:, 512:1024]))
            m1 = act.mark(act.after(mp, R.m_scol).activation(mv[:, tt, :], bank[4][:, :], ACT.Copy,
                                                             scale=scol[:, 8 * tt:8 * tt + 1]))
            free[4] = [m1]
            R.m_v.append(m1)
            yield
        for j in range(4):
            b = 4 + j % 2
            pe.after(m, free[b])
            for n in range(2):
                e = 2 * j + n
                ins = picked(pairs(bank[b])[0:64, n, :], eight[:, e, 0:64], parts_k)
            mp = pe.mark(ins)
            c = slice(2 * j, 2 * j + 2)
            m1 = dve.mark(dve.after(mp, mk[j]).tensor_tensor(kf[0:64, c, :], kf[0:64, c, :], pairs(bank[b])[0:64, :, :],
                                                             ALU.mult))
            free[b] = [m1]
            R.m_k.append(m1)
            yield

    def heads(l, R, mw):
        while R.q is None or R.m_kr is None:
            yield
        m_tq = dve.mark(dve.after(R.rms).tensor_scalar(tabg, tabq[:, :], P('qn', l), None, ALU.mult))
        pe.after(mw, R.q, R.m_rows, free[7])
        for n in range(2):
            mm(bank[7][0:8, 0:256], cols[:, 32:40], tmp[:, 1, n, :], start=n == 0, stop=False)
        used = pe.mark(mm(bank[7][0:8, 0:256], eps8, rowsX, start=False))
        m_row = act.mark(act.after(used).activation(rowsB[:, :], bank[7][0:8, 0:256], ACT.Copy))
        row_first = [m_row]
        mq = []
        for j in range(4):
            pe.after(free[6])
            for n in range(2):
                e = 2 * j + n
                for i in range(2):
                    o = i * 512 + (e % 4) * 128
                    ins = mm(pairs(bank[6])[:, n, :], w_uq[:, e // 4, o:o + 128], lat[:, 2 + i, :], start=i == 0, stop=i == 1)
            mp = pe.mark(ins)
            m2 = act.mark(act.after(mp, used).activation(tmp[:, 1, :, :], pairs(bank[6]), ACT.Square))
            m1 = dve.mark(dve.after(m2, m_tq).tensor_tensor(qf[:, 2 * j:2 * j + 2, :], pairs(bank[6]), wide(tabg), ALU.mult))
            free[6] = [m1]
            mq.append(m1)
            yield
            pe.after(m2, row_first)
            used = strips(7, j, 128, tmp[:, 1, :, :])
        pe.after(m_row)
        m = roots(7, rows_q, parts_q, rowsB[:, :])
        yield
        for j in range(4):
            b = 6 + j % 2
            pe.after(m, free[b])
            for n in range(2):
                e = 2 * j + n
                ins = picked(pairs(bank[b])[:, n, :], eight[:, e, :], parts_q)
            mp = pe.mark(ins)
            c = slice(2 * j, 2 * j + 2)
            m1 = dve.mark(dve.after(mp, mq[j]).tensor_tensor(qf[:, c, :], qf[:, c, :], pairs(bank[b]), ALU.mult))
            free[b] = [m1]
            R.m_q.append(m1)
            yield


    def attention(l, R, g, mix):
        while len(R.m_k) < 2 + 2 * g or len(R.m_q) < 2 + 2 * g or len(R.m_v) < 2:
            yield
        scale = 96.0 ** -0.5
        H = slice(4 * g, 4 * g + 4)
        m_s = []
        for e in range(4 * g, 4 * g + 4):
            b = 4 + g + 2 * (e % 2)
            pe.after(R.m_q[e // 2], R.m_k[e // 2], R.m_kr, free[b])
            mm(bank[b][:, 0:256], qf[:, e, 128:256], kf[:, e, :])
            mp = pe.mark(mm(bank[b][:, 256:384], qf[:, e, 0:128], kf[:, e, 0:128]))
            m = dve.mark(dve.after(mp).scalar_tensor_tensor(mS[:, e, :], bank[b][:, 0:384], scale, mask[:, :],
                                                            ALU.mult, ALU.add))
            free[b] = [m]
            m_s.append(m)
            if e % 2:
                yield
        parts = (slice(0, 256), slice(256, 384))
        st = lambda r, i: mstat[:, r, 8 * i + 4 * g:8 * i + 4 * g + 4]
        ms = []
        for i, c in enumerate(parts):
            m = dve.mark(dve.after(m_s).tensor_reduce(st(0, i), mS[:, H, c], AX.X, ALU.max))
            ms.append(dve.mark(dve.after(m).tensor_scalar(st(1, i), st(0, i), -1.0, None, ALU.mult)))
        yield from idle(4)
        mE = []
        for i, c in enumerate(parts):
            for e in range(4 * g, 4 * g + 4):
                k = 8 * i + e
                mE.append(act.mark(act.after(ms[i]).activation(mS[:, e, c], mS[:, e, c], ACT.Exp, bias=mstat[:, 1, k:k + 1],
                                                               accum_out=mstat[:, 2, k:k + 1])))
            yield
        mP = []
        for i, c in enumerate(parts):
            m = dve.mark(dve.after(mE).reciprocal(st(3, i), st(2, i)))
            mP.append(dve.mark(dve.after(m).tensor_tensor(
                mS[:, H, c], mS[:, H, c], st(3, i).unsqueeze(2).to_broadcast([128, 4, c.stop - c.start]), ALU.mult)))
        yield from idle(2)
        mT = []
        for e in range(4 * g, 4 * g + 4):
            b = 4 + g + 2 * (e % 2)
            pe.after(mP, free[b])
            nc.tensor.transpose(bank[b][:, 0:128], mS[:, e, 256:384], ident[:, :])
            nc.tensor.transpose(bank[b][:, 128:256], mS[:, e, 0:128], ident[:, :])
            mp = pe.mark(nc.tensor.transpose(bank[b][:, 256:384], mS[:, e, 128:256], ident[:, :]))
            m = act.mark(act.after(mp).activation(PT[:, e, :], bank[b][:, 0:384], ACT.Copy))
            free[b] = [m]
            mT.append(m)
            if e % 2:
                yield
        b = 6 + g
        pe.after(mT, R.m_v, free[b])
        for n in range(2):
            for i in range(2):
                e = 4 * g + 2 * n + i
                out = pairs(bank[b])[64 * i:64 * i + 64, n, :]
                mm(out, mv[:, 0, e * 64:(e + 1) * 64], PT[:, e, 0:256], start=n == 0, stop=False)
                ins = mm(out[:, 128:256], mv[:, 1, e * 64:(e + 1) * 64], PT[:, e, 256:384], start=False, stop=True)
        mp = pe.mark(ins)
        yield
        put(mix, 2 * g, pairs(bank[b]), [mp], None)
        free[b] = mix.m[2 * g]
        R.mix.m[4 + 2 * g] = R.mix.m[5 + 2 * g] = mix.m[2 * g]

    def final_norm(s, mx, then):
        mr = one_over_rms(s)
        for e in range(8):
            m = dve.mark(dve.after(mr, mx).scalar_tensor_tensor(X[:, e, :], X[:, e, :], P('final_g', e), nrs,
                                                                ALU.mult, ALU.mult))
            then(e, m)
        return m

    def norm_gain(name, l):
        return P(name, 8 * l, 8 * l + 8)

    h_free = U.h_free
    share(0, 0, 1)
    side = sines()
    wfree = None
    m = final_norm(s, X_now[0], scaled(norm_gain('ffn1_norm', 0), h, h_free))
    for l in range(2):
        mw = [dma(w_uq[:, :, :], t['w_uq'][l], start, wfree), dma(w_ukv[:, :], t['w_ukv'][l], wfree)]
        m = ffn('ffn1%d' % l, h, m, scaled(norm_gain('mix_norm', l), h, None), side)
        finish(side)
        for e in (pe, dve):
            e.after(m_tab, m_fix)
        R = Mixer()
        R.mv, R.mk, R.mq, R.mg, R.m_k, R.m_q, R.m_v = [], [], [], [], [], [], []
        R.kv = R.q = R.rms = R.m_rowA = R.m_kr = R.m_in = R.m_scol = R.tmp_free = None
        R.held = False
        R.mix = Split(h_hi, h_lo)
        for b in range(4):
            R.mix.his[b], R.mix.los[b] = ret_hi[:, b, :], ret_lo[:, b, :]
            R.mix.his[4 + b], R.mix.los[4 + b] = mla_hi[:, b, :], mla_lo[:, b, :]
        rmix, mmix = Split(ret_hi, ret_lo, 4), Split(mla_hi, mla_lo, 4)
        rmix.m = R.mix.m
        ret = retention(l, R, rmix)
        rest = [latents(l, R), keys(l, R, mw), heads(l, R, mw), attention(l, R, 0, mmix), attention(l, R, 1, mmix)]
        run(win2(l, h, R, m), ret, *rest)
        together(rest)
        p = project('w_o2%d' % l, R.mix, (1, 0), None, None, m, scaled(norm_gain('ffn2_norm', l), h, R.m_in))
        wfree = pe.last
        for _ in range(5):
            next(p)
            next(ret, None)
        finish(ret)
        finish(p)
        m = ffn('ffn2%d' % l, h, X_now[0], scaled(norm_gain('ffn1_norm', 1), h, None) if l == 0 else None)
    m_out = dma(t['out'], X[:, :, :], m)
    sp.after(m_out)
    fence()


def constants():
    f = np.float32
    c = np.zeros((128, 576), f)
    p = np.arange(128)
    c[:, 0:128] = np.eye(128)
    c[:, 128:256] = 1
    c[:, 256:384] = p[None, :]
    c[:, 384:512] = (p[:, None] % 32 == p[None, :])
    c[:, 512 + 7] = 1
    c[:, 528:544] = np.arange(16)[None, :]
    c[:, 512 + 32] = 1 / 256
    c[:, 512 + 41] = 1 / 128
    c[64:96, 512 + 50] = 1 / 32
    masks = np.zeros((128, 8, 128), np.uint8)
    for i in range(7):
        b = 1 << i
        masks[:, i, :] = ((p[:, None] // (2 * b) == p[None, :] // (2 * b)) & (p[:, None] // b != p[None, :] // b))
    spread = np.zeros((8, 128), f)
    spread[1, :] = 1
    four, eight = np.zeros((128, 4, 128), f), np.zeros((128, 8, 128), f)
    for e in range(4):
        four[32 * e, e, :] = 1
    for e in range(8):
        o = 32 * (e % 4) + 16 * (e // 4)
        eight[o, e, 0:64] = 1
        eight[o + 8, e, 64:128] = 1
    s, t = p[:, None].astype(np.float64), np.arange(256)[None, :].astype(np.float64)
    lg = np.log1p(-2.0 ** (-5.0 - np.arange(4)))
    full = np.stack([np.where(t >= s, np.exp(np.maximum(t - s, 0) * g), 0) * 128 ** -0.5 for g in lg], 1)
    decay = np.concatenate([full, full[:, :, 0:128]], 2).astype(f)
    causal = np.where(p[:, None] >= p[None, :], 0, -1e30)
    mask = np.concatenate([np.zeros((128, 128)), causal, causal], 1).astype(f)
    perms = np.zeros((128, 256), f)
    for i in range(64):
        perms[i + 64, i] = -1
        perms[i, i + 64] = 1
    for i in range(16):
        for o in (64, 96):
            perms[o + 16 + i, 128 + o + i] = -1
            perms[o + i, 128 + o + 16 + i] = 1
    cols2 = np.zeros((128, 192), f)
    cols2[0:64, 16:24] = 1 / 64
    cols2[64:96, 24:32] = 1 / 32
    inv = lambda dim: (f(1) / (f(10000.0) ** (np.arange(0, dim, 2, dtype=f) / f(dim)))).astype(f)
    cols2[:, 48] = np.tile(inv(128), 2)
    cols2[64:128, 49] = np.tile(inv(32), 4)
    cols2[96:112, 50], cols2[112:128, 50] = -1, 1
    cols2[0, 52:180] = EPS
    return dict(consts=c, masks=masks.reshape(128, 1024).view(np.uint32), spread=spread, four=four, eight=eight,
                decay=decay, mask=mask, perms=perms, cols2=cols2)


def pack(inputs):
    a = {k: np.asarray(v) for k, v in inputs.items()}
    out = constants()

    def granules(tl):
        n = tl.shape[0]
        return np.ascontiguousarray(tl.reshape(n // 2, 2, 128, 1024).transpose(0, 2, 1, 3))

    def columns(w):
        n = w.shape[1] // 128
        return w.reshape(8, 128, n, 128).transpose(2, 1, 0, 3).reshape(n, 128, 1024)

    def rows(w):
        return w.reshape(4, 2, 128, 512).transpose(0, 2, 1, 3).reshape(4, 128, 1024)

    def halves(w):
        return w.reshape(2, 4, 128, 4, 256).transpose(0, 3, 2, 1, 4).reshape(8, 128, 1024)

    def vec(v):
        return v.reshape(-1, 128).T

    out['ctx'] = np.ascontiguousarray(a['ctx'][0].T.reshape(8, 128, 256).transpose(1, 0, 2))
    out['x'] = np.ascontiguousarray(a['x'][0].T.reshape(8, 128, 256).transpose(1, 0, 2))
    names = dict(ffn1_norm='ffn1_norm_2', mix_norm='mix_norm_2', ffn2_norm='ffn2_norm_2', ret_norm='ret_head_norm_2',
                 q_lat='q_lat_norm_2', kv_lat='kv_lat_norm_2')
    heads = {'qn': np.concatenate([a['qn_nope_2'], a['qn_rope_2'], np.roll(a['qn_rope_2'], 16, 1)], 1),
             'kn': np.concatenate([a['kn_nope_2'], a['kn_rope_2'], a['kn_rope_2']], 1)}
    out['params'] = np.ascontiguousarray(np.concatenate(
        [vec(heads[n] if n in heads else a[names.get(n, n)]) for n, _ in PARAMS], 1))
    w = a['w_mod'][0][:, 0:5120].reshape(4, 2, 128, 10, 512)
    out['w_mod0'] = granules(w.transpose(3, 0, 2, 1, 4).reshape(40, 128, 1024))
    w = np.concatenate([a['w_mod'][0][:, 5120:6144], a['w_mod'][1]], 1)
    out['w_mod_rows'] = np.ascontiguousarray(w.T.reshape(56, 128, 1024))
    out['c_row'], out['c_ctx_row'] = a['c'].reshape(1, 1024), a['c_ctx'].reshape(1, 1024)
    for l in range(2):
        w = a['w_in'][l]
        order = [512, 1024, 1536, 2048, 2560, 3584, 3072]
        out['w_in%d' % l] = granules(np.concatenate([rows(w[:, 0:512])] + [columns(w[:, o:o + 512]) for o in order]))
        out['w_out%d' % l] = granules(halves(a['w_out'][l])[[4, 5, 6, 7, 0, 1, 2, 3]])
        out['peer_wq%d' % l] = granules(columns(a['peer_wq'][l]))
        out['peer_u%d' % l] = granules(a['peer_u'][l].reshape(128, 128, 8, 128).transpose(1, 3, 2, 0).reshape(128, 128, 1024))
        out['peer_v%d' % l] = granules(a['peer_v'][l].reshape(128, 128, 1024).transpose(1, 0, 2))
        w = a['w_in_2'][l]
        kr = np.zeros((1024, 128), np.float32)
        kr[:, 64:96] = kr[:, 96:128] = w[:, 2432:2464]
        out['w_in2%d' % l] = granules(np.concatenate([
            columns(w[:, 2304:2432]), columns(kr), columns(w[:, 2048:2304]), columns(w[:, 512:1024]), columns(w[:, 0:512]),
            rows(w[:, 1024:1536]), columns(w[:, 1536:2048])]))
        out['w_o2%d' % l] = granules(halves(a['w_o_2'][l])[[4, 5, 6, 7, 0, 1, 2, 3]])
        for f in ('ffn1', 'ffn2'):
            g, u = columns(a[f + '_w_gate_2'][l]), columns(a[f + '_w_up_2'][l])
            d = a[f + '_w_down_2'][l].reshape(22, 128, 1024)
            seq = []
            for i in range(24):
                if i < 22:
                    seq += [g[i], u[i]]
                if i >= 2:
                    seq.append(d[i - 2])
            out['%s%d' % (f, l)] = granules(np.stack(seq))
    out['subkeys'] = np.ascontiguousarray(a['peer_subkeys'].transpose(0, 4, 1, 2, 3).reshape(2, 128, 16, 128))
    uq = np.zeros((2, 2, 128, 8, 128), np.float32)
    uq[..., 0:96] = a['w_uq_2'].reshape(2, 2, 128, 8, 96)
    uq[..., 96:128] = np.roll(uq[..., 64:96], 16, -1)
    out['w_uq'] = np.ascontiguousarray(uq.reshape(2, 2, 128, 2, 512).transpose(0, 2, 3, 1, 4).reshape(2, 128, 2, 1024))
    out['w_ukv'] = np.ascontiguousarray(a['w_ukv_2'].reshape(2, 128, 8, 2, 64).transpose(0, 1, 3, 2, 4).reshape(2, 128, 1024))
    out['positions'] = np.ascontiguousarray(a['positions_2'].reshape(1, 256))
    return out


def kernel(**inputs):
    import concourse.bacc as bacc
    from concourse.bass_utils import run_bass_kernel_spmd

    nc = bacc.Bacc("TRN2", target_bir_lowering=False, num_devices=1)
    arrays = pack(inputs)
    t = {k: nc.dram_tensor('in_' + k, v.shape, mybir.dt.from_np(v.dtype), kind="ExternalInput").ap()
         for k, v in arrays.items()}
    t['out'] = nc.dram_tensor('out', (128, 8, 256), F32, kind="ExternalOutput").ap()
    build(nc, t)
    r = run_bass_kernel_spmd(nc, [{'in_' + k: v for k, v in arrays.items()}], core_ids=[0])
    y = r.results[0]['out']
    return np.ascontiguousarray(y.transpose(1, 0, 2).reshape(1024, 256).T.reshape(1, 256, 1024))
```
